# Optimizing a Trainium2 kernel written in Bass

```python
import math
import jax, jax.numpy as jnp
from jax import lax
import numpy as np

D_MODEL = 2048
BATCH = 1
SEQ = 256
DEPTH = 2

N_MIXERS = 2
NORM_EPS = 1e-6

GLA_HEADS = 4
GLA_QK = D_MODEL // 2
GLA_V = D_MODEL
GLA_DK = GLA_QK // GLA_HEADS
GLA_DV = GLA_V // GLA_HEADS
GLA_GATE_RANK = 16
GLA_GATE_TAU = 16.0
GLA_CHUNK = 64
GLA_IN = 2 * GLA_QK + 2 * GLA_V + GLA_GATE_RANK

MLA_HEADS = 16
MLA_Q_RANK = 512
MLA_KV_RANK = 512
MLA_NOPE = 128
MLA_ROPE = 64
MLA_V = 128
MLA_WIDTH = MLA_HEADS * MLA_V
MLA_IN = MLA_Q_RANK + MLA_KV_RANK + MLA_ROPE + MLA_WIDTH
ROPE_THETA = 10000.0
Q_BLOCK = 128


def rms_norm(x, g, eps=NORM_EPS):
    xf = x.astype(jnp.float32)
    y = xf * lax.rsqrt(jnp.mean(xf * xf, axis=-1, keepdims=True) + eps)
    return (y * g.astype(jnp.float32)).astype(x.dtype)

def _to_chunks(t, n_chunks):
    B, S, H, D = t.shape
    return t.reshape(B, n_chunks, S // n_chunks, H, D).transpose(0, 3, 1, 2, 4)

def gla_mixer(h, w_in, w_gk2, b_gk, g_onorm, w_out):
    B, S, _ = h.shape
    nC = S // GLA_CHUNK
    proj = h @ w_in
    q, k, v, gate, gk_low = jnp.split(
        proj, [GLA_QK, 2 * GLA_QK, 2 * GLA_QK + GLA_V, 2 * GLA_QK + 2 * GLA_V], axis=-1)
    gk = gk_low @ w_gk2 + b_gk
    log_a = jax.nn.log_sigmoid(gk.astype(jnp.float32)) / GLA_GATE_TAU

    q = _to_chunks(q.reshape(B, S, GLA_HEADS, GLA_DK), nC) * (GLA_DK ** -0.5)
    k = _to_chunks(k.reshape(B, S, GLA_HEADS, GLA_DK), nC)
    v = _to_chunks(v.reshape(B, S, GLA_HEADS, GLA_DV), nC)
    log_a = _to_chunks(log_a.reshape(B, S, GLA_HEADS, GLA_DK), nC)

    b = jnp.cumsum(log_a, axis=3)
    b_last = b[..., -1:, :]
    q_e = q * jnp.exp(b)
    k_e = k * jnp.exp(-b)
    k_last = k * jnp.exp(b_last - b)

    A = jnp.einsum('bhncd,bhnsd->bhncs', q_e, k_e)
    causal = jnp.tril(jnp.ones((GLA_CHUNK, GLA_CHUNK), dtype=bool))
    A = jnp.where(causal, A, 0.0)
    o_intra = jnp.einsum('bhncs,bhnsv->bhncv', A, v.astype(A.dtype))

    def step(state, xs):
        q_c, kl_c, v_c, dl_c = xs
        o_c = jnp.einsum('bhcd,bhdv->bhcv', q_c, state)
        state = state * dl_c[..., :, None] + jnp.einsum('bhcd,bhcv->bhdv', kl_c, v_c)
        return state, o_c

    state0 = jnp.zeros((B, GLA_HEADS, GLA_DK, GLA_DV), dtype=jnp.float32)
    xs = (jnp.moveaxis(q_e, 2, 0).astype(jnp.float32),
          jnp.moveaxis(k_last, 2, 0).astype(jnp.float32),
          jnp.moveaxis(v, 2, 0).astype(jnp.float32),
          jnp.moveaxis(jnp.exp(b_last[..., 0, :]), 2, 0).astype(jnp.float32))
    _, o_inter = lax.scan(step, state0, xs)
    o = o_intra + jnp.moveaxis(o_inter, 0, 2)

    o = o.transpose(0, 2, 3, 1, 4).reshape(B, S, GLA_HEADS, GLA_DV).astype(h.dtype)
    o = rms_norm(o, g_onorm).reshape(B, S, GLA_V)
    return (o * jax.nn.silu(gate)) @ w_out

def _rope(t, cos, sin):
    half = t.shape[-1] // 2
    t1, t2 = t[..., :half], t[..., half:]
    return jnp.concatenate([t1 * cos - t2 * sin, t2 * cos + t1 * sin], axis=-1)

def mla_mixer(h, positions, w_in, g_qa, w_qb, g_kva, w_kvb, w_out):
    B, S, _ = h.shape
    proj = h @ w_in
    c_q, c_kv, k_rope, gate = jnp.split(
        proj, [MLA_Q_RANK, MLA_Q_RANK + MLA_KV_RANK, MLA_Q_RANK + MLA_KV_RANK + MLA_ROPE], axis=-1)
    q = (rms_norm(c_q, g_qa) @ w_qb).reshape(B, S, MLA_HEADS, MLA_NOPE + MLA_ROPE)
    kv = (rms_norm(c_kv, g_kva) @ w_kvb).reshape(B, S, MLA_HEADS, MLA_NOPE + MLA_V)
    q_nope, q_rope = q[..., :MLA_NOPE], q[..., MLA_NOPE:]
    k_nope, v = kv[..., :MLA_NOPE], kv[..., MLA_NOPE:]

    inv_freq = ROPE_THETA ** (-jnp.arange(0, MLA_ROPE, 2, dtype=jnp.float32) / MLA_ROPE)
    ang = positions.astype(jnp.float32)[..., None] * inv_freq
    cos, sin = jnp.cos(ang), jnp.sin(ang)
    q_rope = _rope(q_rope, cos[:, :, None, :], sin[:, :, None, :]).astype(h.dtype)
    k_rope = _rope(k_rope, cos, sin).astype(h.dtype)
    q = jnp.concatenate([q_nope, q_rope], axis=-1)
    k = jnp.concatenate(
        [k_nope, jnp.broadcast_to(k_rope[:, :, None, :], (B, S, MLA_HEADS, MLA_ROPE))], axis=-1)
    scale = (MLA_NOPE + MLA_ROPE) ** -0.5

    n_blocks = S // Q_BLOCK
    q_blocks = q.reshape(B, n_blocks, Q_BLOCK, MLA_HEADS, -1).transpose(1, 0, 2, 3, 4)
    starts = jnp.arange(n_blocks, dtype=jnp.int32) * Q_BLOCK
    k_idx = jnp.arange(S, dtype=jnp.int32)

    def attend(args):
        qb, start = args
        s = jnp.einsum('bqhd,bkhd->bhqk', qb, k).astype(jnp.float32) * scale
        q_idx = start + jnp.arange(Q_BLOCK, dtype=jnp.int32)
        s = jnp.where(k_idx[None, :] <= q_idx[:, None], s, jnp.finfo(jnp.float32).min)
        p = jax.nn.softmax(s, axis=-1).astype(v.dtype)
        return jnp.einsum('bhqk,bkhv->bqhv', p, v)

    o = lax.map(attend, (q_blocks, starts))
    o = o.transpose(1, 0, 2, 3, 4).reshape(B, S, MLA_WIDTH)
    return (o * jax.nn.silu(gate)) @ w_out

def first_inputs(seed: int = 0) -> dict:
    key = jax.random.key(seed)
    ks = jax.random.split(key, 16)

    def w(k, shape):
        return jax.random.normal(k, shape, jnp.float32) * (shape[0] ** -0.5)

    def gain(k, n):
        return 1.0 + 0.05 * jax.random.normal(k, (n,), jnp.float32)

    x = jax.random.normal(ks[0], (BATCH, SEQ, D_MODEL), jnp.float32)
    positions = jnp.broadcast_to(jnp.arange(SEQ, dtype=jnp.int32)[None, :], (BATCH, SEQ))
    return {
        "x": x,
        "positions": positions,
        "l0_pre_norm": gain(ks[1], D_MODEL),
        "l0_gla_w_in": w(ks[2], (D_MODEL, GLA_IN)),
        "l0_gla_w_gk2": w(ks[3], (GLA_GATE_RANK, GLA_QK)),
        "l0_gla_b_gk": 0.1 * jax.random.normal(ks[4], (GLA_QK,), jnp.float32),
        "l0_gla_g_onorm": gain(ks[5], GLA_DV),
        "l0_gla_w_out": w(ks[6], (GLA_V, D_MODEL)),
        "l0_post_norm": gain(ks[7], D_MODEL),
        "l1_pre_norm": gain(ks[8], D_MODEL),
        "l1_mla_w_in": w(ks[9], (D_MODEL, MLA_IN)),
        "l1_mla_g_qa": gain(ks[10], MLA_Q_RANK),
        "l1_mla_w_qb": w(ks[11], (MLA_Q_RANK, MLA_HEADS * (MLA_NOPE + MLA_ROPE))),
        "l1_mla_g_kva": gain(ks[12], MLA_KV_RANK),
        "l1_mla_w_kvb": w(ks[13], (MLA_KV_RANK, MLA_HEADS * (MLA_NOPE + MLA_V))),
        "l1_mla_w_out": w(ks[14], (MLA_WIDTH, D_MODEL)),
        "l1_post_norm": gain(ks[15], D_MODEL),
    }

def first_block(x, positions,
              l0_pre_norm, l0_gla_w_in, l0_gla_w_gk2, l0_gla_b_gk, l0_gla_g_onorm, l0_gla_w_out,
              l0_post_norm,
              l1_pre_norm, l1_mla_w_in, l1_mla_g_qa, l1_mla_w_qb, l1_mla_g_kva, l1_mla_w_kvb,
              l1_mla_w_out, l1_post_norm):
    layers = [
        (l0_pre_norm, (l0_gla_w_in, l0_gla_w_gk2, l0_gla_b_gk, l0_gla_g_onorm, l0_gla_w_out),
         l0_post_norm),
        (l1_pre_norm, (l1_mla_w_in, l1_mla_g_qa, l1_mla_w_qb, l1_mla_g_kva, l1_mla_w_kvb,
                       l1_mla_w_out), l1_post_norm),
    ]
    for i in range(DEPTH):
        g_pre, params, g_post = layers[i]
        h = rms_norm(x, g_pre)
        if i % N_MIXERS == 0:
            y = gla_mixer(h, *params)
        else:
            y = mla_mixer(h, positions, *params)
        x = x + rms_norm(y, g_post)
    return x


DEPTH_2 = 1

NSA_HEADS = 8
NSA_KV_HEADS = 2
NSA_GROUP = NSA_HEADS // NSA_KV_HEADS
HEAD_DIM = 128
NSA_DIM = NSA_HEADS * HEAD_DIM
NSA_KV_DIM = NSA_KV_HEADS * HEAD_DIM
CMP_BLOCK = 32
CMP_STRIDE = 16
SEL_BLOCK = 64
SEL_TOPK = 16
WINDOW = 512
WIN_Q_BLOCK = 128
SEL_Q_BLOCK = 64
FORCE_SCORE = 1e9
DN_HEADS = 8
DN_HEAD_DIM = 128
DN_DIM = DN_HEADS * DN_HEAD_DIM
DN_CHUNK = 64
CONV_K = 4
D_FF = -(-(8 * D_MODEL) // (3 * 256)) * 256
NEG_INF = -1e30
IN_SPLITS = (NSA_DIM, 6 * NSA_KV_DIM, 3 * NSA_HEADS, 3 * DN_DIM, DN_DIM, DN_HEADS, DN_HEADS, 2 * D_MODEL)
N_IN = sum(IN_SPLITS)


def rms_norm_2(x, w):
    xf = x.astype(jnp.float32)
    y = xf * lax.rsqrt(jnp.mean(xf * xf, axis=-1, keepdims=True) + NORM_EPS)
    return (y * w.astype(jnp.float32)).astype(x.dtype)

def l2norm(x):
    return x * lax.rsqrt(jnp.sum(x * x, axis=-1, keepdims=True) + NORM_EPS)

def rope_tables(seq):
    inv = 1.0 / (ROPE_THETA ** (jnp.arange(0, HEAD_DIM, 2, dtype=jnp.float32) / HEAD_DIM))
    ang = jnp.arange(seq, dtype=jnp.float32)[:, None] * inv[None, :]
    return jnp.cos(ang), jnp.sin(ang)

def apply_rope(x, cos, sin):
    x1, x2 = jnp.split(x.astype(jnp.float32), 2, axis=-1)
    c = cos[None, :, None, :]
    s = sin[None, :, None, :]
    return jnp.concatenate([x1 * c - x2 * s, x2 * c + x1 * s], axis=-1).astype(x.dtype)

def masked_softmax(s, mask):
    return jax.nn.softmax(jnp.where(mask, s.astype(jnp.float32), NEG_INF), axis=-1)

def split_points():
    return [int(v) for v in np.cumsum(IN_SPLITS)[:-1]]

def cmp_to_sel_overlap(n_cmp, n_sel):
    cs = np.arange(n_cmp)[:, None] * CMP_STRIDE
    ss = np.arange(n_sel)[None, :] * SEL_BLOCK
    ov = np.clip(np.minimum(cs + CMP_BLOCK, ss + SEL_BLOCK) - np.maximum(cs, ss), 0, None)
    return jnp.asarray(ov / CMP_BLOCK, dtype=jnp.float32)

def compress_blocks(t, pe, w1, w2):
    b, s, hk, d = t.shape
    n_cmp = (s - CMP_BLOCK) // CMP_STRIDE + 1
    idx = np.arange(n_cmp)[:, None] * CMP_STRIDE + np.arange(CMP_BLOCK)[None, :]
    blk = jnp.swapaxes(t[:, idx], 2, 3) + pe
    blk = blk.reshape(b, n_cmp, hk, CMP_BLOCK * d)
    return jax.nn.gelu(blk @ w1) @ w2

def nsa_mixer(q, kv, gate_logits, cmp_pe_k, cmp_w1_k, cmp_w2_k, cmp_pe_v, cmp_w1_v, cmp_w2_v, cos, sin):
    b, s, _, d = q.shape
    hk, g = NSA_KV_HEADS, NSA_GROUP
    scale = HEAD_DIM ** -0.5
    kv = kv.reshape(b, s, 6, hk, d)
    k_c = apply_rope(kv[:, :, 0], cos, sin)
    v_c = kv[:, :, 1]
    k_s = apply_rope(kv[:, :, 2], cos, sin)
    v_s = kv[:, :, 3]
    k_w = apply_rope(kv[:, :, 4], cos, sin)
    v_w = kv[:, :, 5]
    qg = q.reshape(b, s, hk, g, d)
    t_pos = jnp.arange(s)

    kc = compress_blocks(k_c, cmp_pe_k, cmp_w1_k, cmp_w2_k)
    vc = compress_blocks(v_c, cmp_pe_v, cmp_w1_v, cmp_w2_v)
    n_cmp = kc.shape[1]
    s_cmp = jnp.einsum('bshgd,bchd->bhgsc', qg, kc) * scale
    cmp_end = jnp.arange(n_cmp) * CMP_STRIDE + CMP_BLOCK - 1
    cmp_valid = cmp_end[None, :] <= t_pos[:, None]
    p_cmp = masked_softmax(s_cmp, cmp_valid) * jnp.any(cmp_valid, axis=-1)[:, None].astype(jnp.float32)
    o_cmp = jnp.einsum('bhgsc,bchd->bshgd', p_cmp, vc.astype(jnp.float32))

    n_sel = s // SEL_BLOCK
    imp = jnp.einsum('bhgsc,cj->bhsj', p_cmp, cmp_to_sel_overlap(n_cmp, n_sel))
    blk_t = (t_pos // SEL_BLOCK)[:, None]
    j = jnp.arange(n_sel)[None, :]
    forced = (j == 0) | (j == blk_t) | (j == blk_t - 1)
    imp = jnp.where(forced, FORCE_SCORE, jnp.where(j > blk_t, -FORCE_SCORE, imp))
    n_top = min(SEL_TOPK, n_sel)
    _, sel_idx = lax.top_k(imp, n_top)
    kb = k_s.reshape(b, n_sel, SEL_BLOCK, hk, d).transpose(0, 3, 1, 2, 4)
    vb = v_s.reshape(b, n_sel, SEL_BLOCK, hk, d).transpose(0, 3, 1, 2, 4)
    nqb = s // SEL_Q_BLOCK
    q_blocks = qg.reshape(b, nqb, SEL_Q_BLOCK, hk, g, d).transpose(1, 0, 2, 3, 4, 5)
    idx_blocks = sel_idx.reshape(b, hk, nqb, SEL_Q_BLOCK, n_top).transpose(2, 0, 1, 3, 4)
    pos_blocks = t_pos.reshape(nqb, SEL_Q_BLOCK)
    gather = jax.vmap(jax.vmap(lambda blocks, ix: blocks[ix]))

    def sel_block(args):
        qb, ib, tb = args
        kg = gather(kb, ib)
        vg = gather(vb, ib)
        sc = jnp.einsum('bqhgd,bhqnkd->bhgqnk', qb, kg) * scale
        kpos = ib[..., None] * SEL_BLOCK + jnp.arange(SEL_BLOCK)
        valid = (kpos <= tb[None, None, :, None, None]).reshape(b, hk, 1, SEL_Q_BLOCK, n_top * SEL_BLOCK)
        p = masked_softmax(sc.reshape(b, hk, g, SEL_Q_BLOCK, n_top * SEL_BLOCK), valid)
        p = p.reshape(b, hk, g, SEL_Q_BLOCK, n_top, SEL_BLOCK)
        return jnp.einsum('bhgqnk,bhqnkd->bqhgd', p, vg.astype(jnp.float32))

    o_sel = lax.map(sel_block, (q_blocks, idx_blocks, pos_blocks))
    o_sel = o_sel.transpose(1, 0, 2, 3, 4, 5).reshape(b, s, hk, g, d)

    nb = s // WIN_Q_BLOCK
    n_prev = WINDOW // WIN_Q_BLOCK
    pad = ((0, 0), (WINDOW, 0), (0, 0), (0, 0))
    kp = jnp.pad(k_w, pad).reshape(b, nb + n_prev, WIN_Q_BLOCK, hk, d)
    vp = jnp.pad(v_w, pad).reshape(b, nb + n_prev, WIN_Q_BLOCK, hk, d)
    k_band = jnp.concatenate([kp[:, i:i + nb] for i in range(n_prev + 1)], axis=2)
    v_band = jnp.concatenate([vp[:, i:i + nb] for i in range(n_prev + 1)], axis=2)
    qw = qg.reshape(b, nb, WIN_Q_BLOCK, hk, g, d)
    s_win = jnp.einsum('bnqhgd,bnkhd->bhgnqk', qw, k_band) * scale
    qpos = t_pos.reshape(nb, WIN_Q_BLOCK)
    kpos = (jnp.arange(nb) * WIN_Q_BLOCK - WINDOW)[:, None] + jnp.arange((n_prev + 1) * WIN_Q_BLOCK)[None, :]
    diff = qpos[:, :, None] - kpos[:, None, :]
    win_valid = (diff >= 0) & (diff < WINDOW) & (kpos[:, None, :] >= 0)
    p_win = masked_softmax(s_win, win_valid)
    o_win = jnp.einsum('bhgnqk,bnkhd->bnqhgd', p_win, v_band.astype(jnp.float32)).reshape(b, s, hk, g, d)

    gates = jax.nn.sigmoid(gate_logits.astype(jnp.float32)).reshape(b, s, hk, g, 3)
    o = gates[..., 0:1] * o_cmp + gates[..., 1:2] * o_sel + gates[..., 2:3] * o_win
    return o.reshape(b, s, NSA_DIM)

def gated_deltanet(qkv, z, a, beta_logit, conv_w, a_log, dt_bias, norm_w):
    b, s, c3 = qkv.shape
    h, dk, c = DN_HEADS, DN_HEAD_DIM, DN_CHUNK
    n = s // c
    qkv = lax.conv_general_dilated(qkv, conv_w.astype(qkv.dtype), window_strides=(1,), padding=[(CONV_K - 1, 0)],
                                   dimension_numbers=('NWC', 'WIO', 'NWC'), feature_group_count=c3)
    qkv = jax.nn.silu(qkv.astype(jnp.float32))
    q, k, v = [t.reshape(b, s, h, dk) for t in jnp.split(qkv, 3, axis=-1)]
    q = l2norm(q) * dk ** -0.5
    k = l2norm(k)
    beta = jax.nn.sigmoid(beta_logit.astype(jnp.float32))
    gdec = -jnp.exp(a_log.astype(jnp.float32)) * jax.nn.softplus(a.astype(jnp.float32) + dt_bias.astype(jnp.float32))

    def chunks(t):
        return t.reshape(b, n, c, h, -1).transpose(0, 3, 1, 2, 4)

    q, k, v = chunks(q), chunks(k), chunks(v)
    beta = chunks(beta[..., None])[..., 0]
    gc = jnp.cumsum(chunks(gdec[..., None])[..., 0], axis=-1)
    lower_incl = np.tril(np.ones((c, c), dtype=bool))
    strict = np.tril(np.ones((c, c), dtype=bool), -1)
    decay = jnp.exp(jnp.where(lower_incl, gc[..., :, None] - gc[..., None, :], -jnp.inf))
    kb = k * beta[..., None]
    lmat = jnp.where(strict, jnp.einsum('bhnid,bhnjd->bhnij', kb, k) * decay, 0.0)
    eye = jnp.eye(c, dtype=jnp.float32)
    tinv = lax.linalg.triangular_solve(eye + lmat, jnp.broadcast_to(eye, lmat.shape), left_side=True, lower=True)
    u = tinv @ (v * beta[..., None])
    w = tinv @ (kb * jnp.exp(gc)[..., None])
    attn = jnp.einsum('bhnid,bhnjd->bhnij', q, k) * decay
    g_last = gc[..., -1]
    k_dec = k * jnp.exp(g_last[..., None] - gc)[..., None]
    q_dec = q * jnp.exp(gc)[..., None]

    def step(state, xs):
        q_i, k_i, u_i, w_i, attn_i, gl_i = xs
        v_new = u_i - jnp.einsum('bhck,bhkv->bhcv', w_i, state)
        o_i = jnp.einsum('bhck,bhkv->bhcv', q_i, state) + jnp.einsum('bhij,bhjv->bhiv', attn_i, v_new)
        state = state * jnp.exp(gl_i)[..., None, None] + jnp.einsum('bhck,bhcv->bhkv', k_i, v_new)
        return state, o_i

    xs = tuple(jnp.moveaxis(t, 2, 0) for t in (q_dec, k_dec, u, w, attn, g_last))
    state0 = jnp.zeros((b, h, dk, dk), jnp.float32)
    _, o = lax.scan(step, state0, xs)
    o = o.transpose(1, 0, 3, 2, 4).reshape(b, s, h, dk)
    o = rms_norm_2(o, norm_w) * jax.nn.silu(z.astype(jnp.float32).reshape(b, s, h, dk))
    return o.reshape(b, s, DN_DIM)

def second_inputs(seed: int = 0) -> dict:
    key = jax.random.key(seed)
    ks = jax.random.split(key, 24)

    def nrm(k, shape, fan_in):
        return jax.random.normal(k, shape, jnp.float32) * fan_in ** -0.5

    def gain(k, shape):
        return 1.0 + 0.02 * jax.random.normal(k, shape, jnp.float32)

    dt = jnp.exp(jax.random.uniform(ks[5], (DEPTH_2, DN_HEADS), jnp.float32, math.log(1e-3), math.log(1e-1)))
    return {
        'x': jax.random.normal(ks[0], (BATCH, SEQ, D_MODEL), jnp.float32),
        'norm1_w': gain(ks[1], (DEPTH_2, D_MODEL)),
        'w_in': nrm(ks[2], (DEPTH_2, D_MODEL, N_IN), D_MODEL),
        'conv_w': nrm(ks[3], (DEPTH_2, CONV_K, 1, 3 * DN_DIM), CONV_K),
        'a_log': jnp.log(jax.random.uniform(ks[4], (DEPTH_2, DN_HEADS), jnp.float32, 1.0, 16.0)),
        'dt_bias': dt + jnp.log(-jnp.expm1(-dt)),
        'dn_norm_w': gain(ks[6], (DEPTH_2, DN_HEAD_DIM)),
        'cmp_pe_k': 0.02 * jax.random.normal(ks[7], (DEPTH_2, CMP_BLOCK, HEAD_DIM), jnp.float32),
        'cmp_w1_k': nrm(ks[8], (DEPTH_2, CMP_BLOCK * HEAD_DIM, HEAD_DIM), CMP_BLOCK * HEAD_DIM),
        'cmp_w2_k': nrm(ks[9], (DEPTH_2, HEAD_DIM, HEAD_DIM), HEAD_DIM),
        'cmp_pe_v': 0.02 * jax.random.normal(ks[10], (DEPTH_2, CMP_BLOCK, HEAD_DIM), jnp.float32),
        'cmp_w1_v': nrm(ks[11], (DEPTH_2, CMP_BLOCK * HEAD_DIM, HEAD_DIM), CMP_BLOCK * HEAD_DIM),
        'cmp_w2_v': nrm(ks[12], (DEPTH_2, HEAD_DIM, HEAD_DIM), HEAD_DIM),
        'w_up_nsa': nrm(ks[13], (DEPTH_2, NSA_DIM, D_MODEL), NSA_DIM),
        'w_up_dn': nrm(ks[14], (DEPTH_2, DN_DIM, D_MODEL), DN_DIM),
        'w_o': nrm(ks[15], (DEPTH_2, D_MODEL, D_MODEL), D_MODEL),
        'norm2_w': gain(ks[16], (DEPTH_2, D_MODEL)),
        'w_ffn_gate': nrm(ks[17], (DEPTH_2, D_MODEL, D_FF), D_MODEL),
        'w_ffn_up': nrm(ks[18], (DEPTH_2, D_MODEL, D_FF), D_MODEL),
        'w_ffn_down': nrm(ks[19], (DEPTH_2, D_FF, D_MODEL), D_FF),
        'norm_f_w': gain(ks[20], (D_MODEL,)),
    }

def second_block(x, norm1_w, w_in, conv_w, a_log, dt_bias, dn_norm_w, cmp_pe_k, cmp_w1_k, cmp_w2_k,
              cmp_pe_v, cmp_w1_v, cmp_w2_v, w_up_nsa, w_up_dn, w_o, norm2_w, w_ffn_gate, w_ffn_up,
              w_ffn_down, norm_f_w):
    b, s, _ = x.shape
    cos, sin = rope_tables(s)
    for l in range(DEPTH_2):
        h = rms_norm_2(x, norm1_w[l])
        proj = h @ w_in[l]
        nsa_q, nsa_kv, nsa_g, dn_qkv, dn_z, dn_a, dn_b, merge_g = jnp.split(proj, split_points(), axis=-1)
        q = apply_rope(nsa_q.reshape(b, s, NSA_HEADS, HEAD_DIM), cos, sin)
        o_nsa = nsa_mixer(q, nsa_kv, nsa_g, cmp_pe_k[l], cmp_w1_k[l], cmp_w2_k[l],
                          cmp_pe_v[l], cmp_w1_v[l], cmp_w2_v[l], cos, sin).astype(x.dtype)
        o_dn = gated_deltanet(dn_qkv, dn_z, dn_a, dn_b, conv_w[l], a_log[l], dt_bias[l], dn_norm_w[l]).astype(x.dtype)
        g_nsa, g_dn = jnp.split(jax.nn.sigmoid(merge_g), 2, axis=-1)
        mixed = g_nsa * (o_nsa @ w_up_nsa[l]) + g_dn * (o_dn @ w_up_dn[l])
        x = x + mixed @ w_o[l]
        h2 = rms_norm_2(x, norm2_w[l])
        x = x + (jax.nn.silu(h2 @ w_ffn_gate[l]) * (h2 @ w_ffn_up[l])) @ w_ffn_down[l]
    return rms_norm_2(x, norm_f_w)


def setup_inputs(seed=0):
    out = dict(first_inputs(seed))
    for name, value in second_inputs(seed + 1).items():
        if name != "x":
            out[name + "_2"] = value
    return out


def reference(
    x, positions, l0_pre_norm, l0_gla_w_in, l0_gla_w_gk2, l0_gla_b_gk, l0_gla_g_onorm,
    l0_gla_w_out, l0_post_norm, l1_pre_norm, l1_mla_w_in, l1_mla_g_qa, l1_mla_w_qb,
    l1_mla_g_kva, l1_mla_w_kvb, l1_mla_w_out, l1_post_norm, norm1_w_2, w_in_2, conv_w_2,
    a_log_2, dt_bias_2, dn_norm_w_2, cmp_pe_k_2, cmp_w1_k_2, cmp_w2_k_2, cmp_pe_v_2, cmp_w1_v_2,
    cmp_w2_v_2, w_up_nsa_2, w_up_dn_2, w_o_2, norm2_w_2, w_ffn_gate_2, w_ffn_up_2, w_ffn_down_2,
    norm_f_w_2,
):
    x = first_block(
        x, positions, l0_pre_norm, l0_gla_w_in, l0_gla_w_gk2, l0_gla_b_gk, l0_gla_g_onorm,
        l0_gla_w_out, l0_post_norm, l1_pre_norm, l1_mla_w_in, l1_mla_g_qa, l1_mla_w_qb,
        l1_mla_g_kva, l1_mla_w_kvb, l1_mla_w_out, l1_post_norm,
    )
    return second_block(
        x, norm1_w_2, w_in_2, conv_w_2, a_log_2, dt_bias_2, dn_norm_w_2, cmp_pe_k_2, cmp_w1_k_2,
        cmp_w2_k_2, cmp_pe_v_2, cmp_w1_v_2, cmp_w2_v_2, w_up_nsa_2, w_up_dn_2, w_o_2, norm2_w_2,
        w_ffn_gate_2, w_ffn_up_2, w_ffn_down_2, norm_f_w_2,
    )


_drawn_inputs = setup_inputs


def setup_inputs(seed=0):
    import zlib

    import numpy as np

    out = dict(_drawn_inputs(seed))
    spreads = {}
    factors = {'norm1_w_2': 8.0,
     'dn_norm_w_2': 8.0,
     'cmp_pe_k_2': 41.469,
     'cmp_w1_k_2': 2.915,
     'cmp_w2_k_2': 2.987,
     'cmp_pe_v_2': 200.0,
     'norm2_w_2': 17.622,
     'norm_f_w_2': 22.086}
    for name, (base, spread) in spreads.items():
        noise = np.random.default_rng([zlib.crc32(name.encode()), seed]).standard_normal(out[name].shape)
        drawn = base * np.exp(spread * noise) if base else spread * noise
        out[name] = __import__('jax').numpy.asarray(drawn.astype(out[name].dtype))
    for name, factor in factors.items():
        out[name] = (out[name] * factor).astype(out[name].dtype)
    return out
```

```python
from contextlib import ExitStack

import numpy as np
import concourse.bass as bass
from concourse import mybir
from concourse.alu_op_type import AluOpType as ALU

F32 = mybir.dt.float32
I32 = mybir.dt.int32
ACT = mybir.ActivationFunctionType
AX = mybir.AxisListType.X
ds = bass.ds

P = 128
S = 256
NT = S // P
D = 2048
KD = D // P
EPS = 1e-6
CHUNK = 64
NCH = S // CHUNK
SLOTS = 8
SLOT_K = 2
W = 512
HIDDEN = -1e30

GLA_H, GLA_DK, GLA_DV, GLA_RANK, GLA_TAU = 4, 256, 512, 16, 16.0
GLA_QK, GLA_V = GLA_H * GLA_DK, GLA_H * GLA_DV

MLA_H, MLA_RANK, NOPE, ROPE = 16, 512, 128, 64
MLA_SCALE = float(NOPE + ROPE) ** -0.5
LATENT = 2 * MLA_RANK + ROPE

HD = 128
NSA_H, NSA_KV, NSA_G = 8, 2, 4
NSA_SCALE = float(HD) ** -0.5
CMP_BLOCK, CMP_STRIDE = 32, 16
NCMP = (S - CMP_BLOCK) // CMP_STRIDE + 1
CPAD = NCMP + 1
DN_H = 8
CONV_K = 4
D_FF = 5632
GELU_C, GELU_A = float(np.sqrt(2 / np.pi)), 0.044715


def constant_columns():
    i = np.arange(P)
    same = (i[:, None] // CHUNK) == (i[None, :] // CHUNK)
    upto = same & (i[:, None] <= i[None, :])
    after = same & (i[:, None] > i[None, :])
    out = {"ident": np.eye(P), "upto": upto, "after": after, "ones": np.ones((P, P)),
           "half": (i[:, None] // CHUNK) == np.arange(2)[None, :]}
    levels = []
    for n in range(6):
        b = 1 << n
        levels.append(((i[:, None] // (2 * b)) == (i[None, :] // (2 * b)))
                      & ((i[:, None] // b) % 2 == 0) & ((i[None, :] // b) % 2 == 1))
    out["levels"] = np.concatenate(levels, 1)
    causal = np.where(i[None, :] <= i[:, None], 0.0, HIDDEN)
    out["causal"] = np.concatenate([causal, np.zeros((P, P)), causal], 1)
    tok = (np.arange(NT)[None, :, None] * P + i[:, None, None])
    ends = np.arange(CPAD) * CMP_STRIDE + CMP_BLOCK - 1
    seen = (ends[None, None, :] <= tok) & (np.arange(CPAD) < NCMP)[None, None, :]
    out["cmp_mask"] = np.where(seen, 0.0, HIDDEN).reshape(P, NT * CPAD)
    out["cmp_any"] = seen.any(-1)
    out["cmp_head"] = (i[:, None] // CPAD) == np.arange(NSA_H)[None, :]
    inv = (1.0 / (np.float32(10000.0) ** (np.arange(0, HD, 2, dtype=np.float32) / np.float32(HD)))).astype(np.float32)
    ang = tok.astype(np.float32) * inv[None, None, :]
    out["cos2"] = np.cos(ang).reshape(P, -1)
    out["sin2"] = np.sin(ang).reshape(P, -1)
    inv1 = (np.float32(10000.0) ** (-np.arange(0, ROPE, 2, dtype=np.float32) / np.float32(ROPE))).astype(np.float32)
    out["inv_freq"] = np.broadcast_to(inv1[None, :], (P, ROPE // 2))
    return {k: np.ascontiguousarray(v, dtype=np.float32) for k, v in out.items()}


def program(nc, A):
    with ExitStack() as ctx:
        def sb(name, shape, dt=F32):
            return ctx.enter_context(nc.sbuf_tensor(name, shape, dt))

        def sem(name):
            return ctx.enter_context(nc.semaphore(name))

        X = sb("residual", [P, NT, D])
        HT = sb("hidden_T", [P, KD, S])
        ring = sb("weight_ring", [P, SLOTS, SLOT_K, W])
        proj = sb("projections", [P, 13600])
        scr = sb("scratch", [P, 12800])
        ps = ctx.enter_context(nc.psum_tensor("banks", [P, 8, 512], F32))
        cols, offset = {}, 0
        for name, a in constant_columns().items():
            cols[name] = (offset, a.shape[1])
            offset += a.shape[1]
        const = sb("constants", [P, offset])

        def C(name):
            o, n = cols[name]
            return const[:, o:o + n]

        small = {}
        for name in A["small"]:
            small[name] = sb("c_" + name, list(A["small"][name].shape))
        pos_i = sb("positions_i", [P, NT], I32)
        gk2 = sb("gla_gate_weight", [GLA_RANK, GLA_QK])
        w2k = sb("cmp_w2_k", [P, HD])
        w2v = sb("cmp_w2_v", [P, HD])
        stat = sb("statistics", [P, 64])
        tab = sb("mla_rope_tables", [P, 2, NT, ROPE // 2])
        ident, upto, after, ones = C("ident"), C("upto"), C("after"), C("ones")

        v_step, a_step = sem("vector_step"), sem("scalar_step")
        steps = {"v": 0, "a": 0}

        def V(ins):
            steps["v"] += 1
            ins.then_inc(v_step, 1)
            nc.vector.wait_ge(v_step, steps["v"])

        def Sc(ins):
            steps["a"] += 1
            ins.then_inc(a_step, 1)
            nc.scalar.wait_ge(a_step, steps["a"])

        landed = [sem(f"weights_landed_{n}") for n in range(SLOTS)]
        used = sem("weights_used")
        chunk_done = [sem("chunk_done_even"), sem("chunk_done_odd")]
        chunk_evicted = [sem("chunk_evicted_even"), sem("chunk_evicted_odd")]
        planned = {"use": 0, "chunk": 0, "turned": 0, "copied_v": 0, "copied_s": 0, "norm": 0}

        class Product:

            def __init__(self, chunks, rounds=1):
                self.chunks, self.rounds = chunks, rounds
                self.use0, self.chunk0 = planned["use"], planned["chunk"]
                self.uses = sum(c[1] // SLOT_K for c in chunks)
                planned["use"] += self.uses * rounds
                planned["chunk"] += len(chunks) * rounds
                assert rounds == 1 or (self.uses % SLOTS == 0 and len(chunks) % 2 == 0)

            def over(self, eng, body):
                first = 0
                if self.use0 == 0:
                    body(0)
                    first = 1
                if self.rounds - first > 1:
                    with eng.Fori(first, self.rounds) as i:
                        body(i)
                elif self.rounds - first == 1:
                    body(first)

            def load(self, sp):
                def body(i):
                    u = self.use0
                    for w, kt, col0, step, width, _, _ in self.chunks:
                        for k in range(0, kt, SLOT_K):
                            if not (isinstance(i, int) and u + i * self.uses < SLOTS):
                                sp.wait_ge(used, i * self.uses + (u - SLOTS + 1))
                            if isinstance(i, int):
                                at = slice(col0 + i * step, col0 + i * step + width)
                            else:
                                at = ds(i * step + col0, width)
                            if callable(w):
                                dst, src = w(ring[:, u % SLOTS, :, :], k)
                            else:
                                dst = ring[:, u % SLOTS, :, 0:width]
                                src = w[k * P:(k + SLOT_K) * P, at].rearrange("(k p) n -> p k n", p=P)
                            sp.dma_start(dst, src).then_inc(landed[u % SLOTS], 16)
                            u += 1
                self.over(sp, body)

            def tensor(self, pe):
                def body(i):
                    u, c = self.use0, self.chunk0
                    for w, kt, _, _, width, acts, turned in self.chunks:
                        if not (isinstance(i, int) and c + i * len(self.chunks) < 2):
                            pe.wait_ge(chunk_evicted[c % 2], i * (len(self.chunks) // 2) + c // 2)
                        b = 2 * (c % 2)
                        for k0 in range(0, kt, SLOT_K):
                            pe.wait_ge(landed[u % SLOTS],
                                       i * (16 * self.uses // SLOTS) + 16 * (u // SLOTS + 1))
                            if callable(w):
                                last = acts(ring[:, u % SLOTS, :, :], k0, b)
                            elif turned:
                                for kk in range(SLOT_K):
                                    k = k0 + kk
                                    for f in range(W // P):
                                        last = pe.matmul(
                                            ps[:, b + f // 2, (f % 2) * S:(f % 2) * S + S],
                                            ring[:, u % SLOTS, kk, f * P:(f + 1) * P], acts(k),
                                            start=(k == 0 and f % 2 == 0), stop=(k == kt - 1),
                                            skip_group_check=True)
                            else:
                                for t in range(NT):
                                    for kk in range(SLOT_K):
                                        k = k0 + kk
                                        last = pe.matmul(ps[:, b + t, 0:width], acts(k)[:, t * P:(t + 1) * P],
                                                         ring[:, u % SLOTS, kk, 0:width],
                                                         start=(k == 0), stop=(k == kt - 1))
                            last.then_inc(used, 1)
                            u += 1
                        pe.wait_ge(used, i * self.uses + u)
                        pe.sem_inc(chunk_done[c % 2], 1)
                        c += 1
                self.over(pe, body)

            def wait_evicted(self, eng):
                end = self.chunk0 + len(self.chunks) * self.rounds
                eng.wait_ge(chunk_evicted[0], (end + 1) // 2)
                if end > 1:
                    eng.wait_ge(chunk_evicted[1], end // 2)

            def evict(self, eng, which, body_of):
                def body(i):
                    for n in which:
                        c = self.chunk0 + n
                        eng.wait_ge(chunk_done[c % 2], i * (len(self.chunks) // 2) + c // 2 + 1)
                        body_of(i, n, 2 * (c % 2)).then_inc(chunk_evicted[c % 2], 1)
                self.over(eng, body)

        def piece(i, step, off, n):
            return slice(off + i * step, off + i * step + n) if isinstance(i, int) else ds(i * step + off, n)

        def turn_hidden(k):
            return HT[:, k, :]

        def wide(weights, kt, n, col0, acts):
            per = 4 if kt == 4 else 2
            return Product([(weights, kt, col0 + m * W, per * W, W, acts, False) for m in range(per)], n // per)

        def evict_wide(prod, dst, off):
            per = len(prod.chunks)

            def body(i, n, b):
                for t in range(NT):
                    last = nc.scalar.copy(dst[:, t, piece(i, per * W, off + n * W, W)], ps[:, b + t, :])
                return last
            prod.evict(nc.scalar, range(per), body)

        turned = sem("group_turned")
        copied_out = [sem("turned_copied_by_vector"), sem("turned_copied_by_scalar")]
        squares, inverse, scaled = sem("norm_squares"), sem("norm_inverse"), sem("norm_scaled")

        class Turn:

            def __init__(self, name, groups):
                self.groups = groups

            def place(self):
                self.turned0, self.out0 = planned["turned"], [planned["copied_v"], planned["copied_s"]]
                n = len(self.groups)
                planned["turned"] += n
                planned["copied_v"] += (n + 1) // 2
                planned["copied_s"] += n // 2

            def tensor(self, pe):
                for g, (tiles, _) in enumerate(self.groups):
                    if g >= 4:
                        pe.wait_ge(copied_out[g % 2], self.out0[g % 2] + (g - 4) // 2 + 1)
                    for src, col in tiles:
                        rows, width = src.shape[0], src.shape[1]
                        last = pe.transpose(ps[0:width, 4 + g % 4, col:col + rows], src, ident[0:rows, 0:rows])
                    last.then_inc(turned, 1)

            def copies(self, eng, which):
                for g, (_, copies) in enumerate(self.groups):
                    if g % 2 != which:
                        continue
                    eng.wait_ge(turned, self.turned0 + g + 1)
                    for dst, src, scale in copies:
                        if which == 0:
                            last = nc.vector.tensor_copy(dst, src(4 + g % 4)) if scale is None else \
                                nc.vector.tensor_scalar(dst, src(4 + g % 4), scale, None, ALU.mult)
                        else:
                            last = nc.scalar.copy(dst, src(4 + g % 4)) if scale is None else \
                                nc.scalar.activation(dst, src(4 + g % 4), ACT.Copy, scale=scale)
                    last.then_inc(copied_out[which], 1)

            def vector(self):
                self.copies(nc.vector, 0)

            def scalar(self):
                self.copies(nc.scalar, 1)

            def wait(self, eng):
                eng.wait_ge(copied_out[0], self.out0[0] + (len(self.groups) + 1) // 2)
                if len(self.groups) > 1:
                    eng.wait_ge(copied_out[1], self.out0[1] + len(self.groups) // 2)

        def whole(rows, a, n):
            return lambda b: ps[0:rows, b, a:a + n]

        def turn_tokens(name, src, n_tiles, dst, gain=None):
            groups = []
            for k in range(0, n_tiles, 2):
                tiles = [(src(t, k + kk), kk * S + t * P) for kk in range(2) for t in range(NT)]
                copies = [(dst(k + kk), whole(P, kk * S, S), None if gain is None else gain(k + kk))
                          for kk in range(2)]
                groups.append((tiles, copies))
            return Turn(name, groups)

        class Norm:

            def __init__(self, name, src, n, rstd, junk, dst=None):
                self.src, self.n, self.rstd, self.junk, self.dst = src, n, rstd, junk, dst

            def place(self):
                planned["norm"] += 1
                self.nth = planned["norm"]

            def scalar(self):
                for t in range(NT):
                    Sc(nc.scalar.activation(self.junk, self.src(t), ACT.Square, accum_out=self.rstd[:, t:t + 1]))
                nc.scalar.sem_inc(squares, 1)
                nc.scalar.wait_ge(inverse, self.nth)
                Sc(nc.scalar.activation(self.rstd, self.rstd, ACT.Sqrt))
                if self.dst is not None:
                    for t in range(NT):
                        Sc(nc.scalar.activation(self.dst(t), self.src(t), ACT.Copy, scale=self.rstd[:, t:t + 1]))
                nc.scalar.sem_inc(scaled, 1)

            def vector(self):
                nc.vector.wait_ge(squares, self.nth)
                V(nc.vector.tensor_scalar(self.rstd, self.rstd, 1.0 / self.n, EPS, ALU.mult, ALU.add))
                V(nc.vector.reciprocal(self.rstd, self.rstd))
                nc.vector.sem_inc(inverse, 1)

        def view(buf, off, *dims):
            n = int(np.prod(dims))
            v = buf[:, off:off + n]
            if len(dims) == 2:
                return v.rearrange("p (a b) -> p a b", a=dims[0])
            if len(dims) == 3:
                return v.rearrange("p (a b c) -> p a b c", a=dims[0], b=dims[1])
            if len(dims) == 4:
                return v.rearrange("p (a b c d) -> p a b c d", a=dims[0], b=dims[1], c=dims[2])
            return v

        def junk_q(buf):
            return buf[:, 12288:12288 + MLA_RANK]

        class Attention:

            def __init__(self, name, heads, parts, value, scale, buf, finish):
                self.h, self.parts, self.value, self.scale, self.finish = heads, parts, value, scale, finish
                self.s = view(buf, 0, 2, 3 * P)
                self.p = view(buf, 6 * P, 2, 3 * P)
                self.pt = view(buf, 12 * P, 2, 3 * P)
                self.st = view(buf, 18 * P, 2, 2, 2)
                self.sum = view(buf, 18 * P + 8, 2, 2)
                names = ("_scores", "_masked", "_probs", "_turned", "_turned_copied", "_mixed", "_finished")
                (self.scored, self.masked, self.probs, self.turned, self.copied, self.mixed,
                 self.finished) = (sem(name + n) for n in names)
                self.span = [(0, P), (P, 3 * P)]

            def tensor(self, pe):
                def score(h):
                    if h >= 2:
                        pe.wait_ge(self.masked, h - 1)
                    for t in range(NT):
                        a, b = self.span[t]
                        parts = self.parts(h, t)
                        for n, (q, k) in enumerate(parts):
                            last = pe.matmul(ps[:, 4 + h % 2, a:b], q, k, start=(n == 0), stop=(n == len(parts) - 1))
                    last.then_inc(self.scored, 1)
                score(0)
                for h in range(self.h):
                    if h + 1 < self.h:
                        score(h + 1)
                    pe.wait_ge(self.probs, h + 1)
                    if h >= 1:
                        pe.wait_ge(self.copied, h)
                    for n in range(3):
                        last = pe.transpose(ps[:, 6, n * P:(n + 1) * P], self.p[:, h % 2, n * P:(n + 1) * P], ident)
                    last.then_inc(self.turned, 1)
                    pe.wait_ge(self.copied, h + 1)
                    if h >= 1:
                        pe.wait_ge(self.finished, h)
                    pt = self.pt[:, h % 2, :]
                    pe.matmul(ps[:, 7, 0:P], pt[:, 0:P], self.value(h, 0), start=True, stop=True)
                    pe.matmul(ps[:, 7, P:2 * P], pt[:, P:2 * P], self.value(h, 0), start=True, stop=False)
                    pe.matmul(ps[:, 7, P:2 * P], pt[:, 2 * P:3 * P], self.value(h, 1), start=False, stop=True)\
                        .then_inc(self.mixed, 1)

            def vector(self):
                def mask(h):
                    nc.vector.wait_ge(self.scored, h + 1)
                    if h >= 2:
                        nc.vector.wait_ge(self.probs, h - 1)
                    V(nc.vector.scalar_tensor_tensor(out=self.s[:, h % 2, :], in0=ps[:, 4 + h % 2, 0:3 * P],
                                                     scalar=self.scale, in1=C("causal"), op0=ALU.mult, op1=ALU.add))
                    for t in range(NT):
                        a, b = self.span[t]
                        ins = nc.vector.tensor_reduce(self.st[:, h % 2, 0, t:t + 1], self.s[:, h % 2, a:b], AX, ALU.max)
                        V(ins)
                    V(nc.vector.tensor_scalar(self.st[:, h % 2, 1, :], self.st[:, h % 2, 0, :], -1.0, None, ALU.mult))
                    nc.vector.sem_inc(self.masked, 1)
                mask(0)
                for h in range(self.h):
                    if h + 1 < self.h:
                        mask(h + 1)
                    nc.vector.wait_ge(self.mixed, h + 1)
                    V(nc.vector.reciprocal(self.sum[:, h % 2, :], self.sum[:, h % 2, :]))
                    self.finish(h, 7, self.sum[:, h % 2, :])
                    nc.vector.sem_inc(self.finished, 1)

            def scalar(self):
                for h in range(self.h):
                    nc.scalar.wait_ge(self.masked, h + 1)
                    if h >= 2:
                        nc.scalar.wait_ge(self.turned, h - 1)
                        nc.scalar.wait_ge(self.finished, h - 1)
                    for t in range(NT):
                        a, b = self.span[t]
                        Sc(nc.scalar.activation(self.p[:, h % 2, a:b], self.s[:, h % 2, a:b], ACT.Exp,
                                                bias=self.st[:, h % 2, 1, t:t + 1],
                                                accum_out=self.sum[:, h % 2, t:t + 1]))
                    nc.scalar.sem_inc(self.probs, 1)
                    nc.scalar.wait_ge(self.turned, h + 1)
                    if h >= 2:
                        nc.scalar.wait_ge(self.mixed, h - 1)
                    nc.scalar.copy(self.pt[:, h % 2, :], ps[:, 6, 0:3 * P]).then_inc(self.copied, 1)

        s_x, s_const, s_pos = sem("x_landed"), sem("constants_landed"), sem("positions_landed")
        s_row = [sem("gain_row_landed_0"), sem("gain_row_landed_1"), sem("gain_row_landed_2")]
        row_free = [sem("gain_row_free_1"), sem("gain_row_free_2")]
        out_landed = sem("output_landed")
        out_ready = sem("output_ready")
        n_const = 4 + len(small)

        g_proj = view(proj, 0, NT, 6160)
        G_K, G_V, G_G, G_LOW = GLA_QK, 2 * GLA_QK, 2 * GLA_QK + GLA_V, 2 * GLA_QK + 2 * GLA_V
        y_tok = view(scr, 0, NT, D)
        gain_row = scr[:, 2 * D:3 * D]
        normed = view(scr, 3 * D, NT, D)
        junk = scr[:, 5 * D:6 * D]

        stat_x = stat[:, 0:2]
        stat_q, stat_kv = stat[:, 2:4], stat[:, 4:6]

        def x_norm(name, gain):
            n = Norm(name, lambda t: X[:, t, :], D, stat_x, junk, lambda t: normed[:, t, :])
            tr = turn_tokens(name + "_x", lambda t, k: normed[:, t, k * P:(k + 1) * P], KD, turn_hidden,
                             lambda k: small[gain][:, k:k + 1])
            return n, tr

        norm0, turn0 = x_norm("norm0", "l0_pre")
        norm1, turn1 = x_norm("norm1", "l1_pre")
        norm2, turn2 = x_norm("norm2", "norm1")
        norm3, turn3 = x_norm("norm3", "norm2")
        post0 = Norm("post0", lambda t: y_tok[:, t, :], D, stat_x, junk)
        post1 = Norm("post1", lambda t: y_tok[:, t, :], D, stat_x, junk)
        postf = Norm("postf", lambda t: X[:, t, :], D, stat_x, junk)

        la = view(scr, 0, NT, GLA_QK)
        tmp_a = view(scr, 2048, NT, GLA_QK)
        kl = view(scr, 2048, NT, GLA_QK)
        qeT = view(scr, 4096, 8, NT, 2, P)
        keT = view(scr, 8192, 8, S)
        gst = view(HT[:, :, :].rearrange("p k n -> p (k n)"), 0, GLA_H, 2, GLA_DV)
        gst2 = sb("gla_state_odd", [P, GLA_H, 2, GLA_DV])

        def gst_in(ch):
            return gst if ch % 2 else gst2

        g_o = view(proj, 0, NT, 6160)[:, :, 0:D]
        lowT = scr[:, 10240:10240 + S]
        dlT = view(scr, 10496, 8, NCH)
        gAT = view(scr, 10560, 2, P)
        gst_r = stat[:, 8:16]

        prod_gla = wide(A["w_gla_in"], KD, 12, 0, turn_hidden)
        prod_gla_low = Product([(A["w_gla_in"], KD, G_LOW, 0, GLA_RANK, turn_hidden, False)])
        turn_low = Turn("gla_low", [([(g_proj[:, t, G_LOW:G_LOW + GLA_RANK], t * P) for t in range(NT)],
                                     [(lowT[0:GLA_RANK, :], whole(GLA_RANK, 0, S), None)])])
        gk_done, gk_used = sem("gla_gate_done"), sem("gla_gate_used")
        gk_exp, gk_dec = sem("gla_gate_exp"), sem("gla_decay_ready")
        gk_abs = sem("gla_gate_abs")
        cum_done, cum_exp, cum_free = sem("gla_cumulated"), sem("gla_cumulated_exp"), sem("gla_cumulated_used")
        groups = []
        for k in range(8):
            tiles = [(g_proj[:, t, k * P:(k + 1) * P], t * P) for t in range(NT)]
            copies = [(qeT[:, k, t, par, par * CHUNK:(par + 1) * CHUNK],
                       whole(P, t * P + par * CHUNK, CHUNK), None) for t in range(NT) for par in range(2)]
            groups.append((tiles, copies))
        for k in range(8):
            tiles = [(g_proj[:, t, G_K + k * P:G_K + (k + 1) * P], t * P) for t in range(NT)]
            groups.append((tiles, [(keT[:, k, :], whole(P, 0, S), None)]))
        turn_qk = Turn("gla_qk", groups)
        qk_ready = sem("gla_scaled_ready")
        zeroed = sem("gla_zeroed")
        dl_done, dl_ready = sem("gla_chunk_decay_done"), sem("gla_chunk_decay_ready")
        ga_done, ga_masked = sem("gla_scores"), sem("gla_scores_masked")
        go_done, go_out = sem("gla_output_done"), sem("gla_output_evicted")
        gs_done, gs_out = sem("gla_update_done"), sem("gla_state_ready")
        gate_act = sem("gla_gate_activated")
        gn_sq, gn_inv, gn_rs, gn_out = sem("gla_norm_squares"), sem("gla_norm_inverse"), sem("gla_norm_ready"), sem("gla_gated")
        turn_go = turn_tokens("gla_out", lambda t, k: g_o[:, t, k * P:(k + 1) * P], KD, turn_hidden)
        prod_gla_out = wide(A["w_gla_out"], KD, 4, 0, turn_hidden)

        def gla_tensor(pe):
            prod_gla_low.wait_evicted(pe)
            turn_low.tensor(pe)
            turn_low.wait(pe)
            for t in range(NT):
                for n in range(2):
                    last = pe.matmul(ps[:, 2 * t + n, :], lowT[0:GLA_RANK, t * P:(t + 1) * P],
                                     gk2[:, n * W:(n + 1) * W], start=True, stop=True)
            last.then_inc(gk_done, 1)
            pe.wait_ge(gk_dec, 1)
            for t in range(NT):
                for n in range(2):
                    pe.matmul(ps[:, 2 * t + n, :], upto, la[:, t, n * W:(n + 1) * W], start=True, stop=True)
                    last = pe.matmul(ps[:, 4 + 2 * t + n, :], after, la[:, t, n * W:(n + 1) * W], start=True, stop=True)
            last.then_inc(cum_done, 1)
            pe.wait_ge(cum_free, 2)
            for k in range(8):
                for t in range(NT):
                    last = pe.matmul(ps[:, 0, k * NCH + 2 * t:k * NCH + 2 * t + 2], la[:, t, k * P:(k + 1) * P],
                                     C("half"), start=True, stop=True)
            last.then_inc(dl_done, 1)
            pe.wait_ge(qk_ready, 1)
            pe.wait_ge(zeroed, 1)
            turn_qk.tensor(pe)
            turn_qk.wait(pe)
            pe.wait_ge(dl_ready, 1)
            n = 0
            m = 0
            for t in range(NT):
                for par in range(2):
                    ch = 2 * t + par
                    rows = slice(par * CHUNK, (par + 1) * CHUNK)
                    if ch < NCH - 1:
                        for h in range(GLA_H):
                            for j in range(2):
                                k = 2 * h + j
                                if m >= 2:
                                    pe.wait_ge(gs_out, m - 1)
                                pe.matmul(ps[:, 6 + m % 2, :], kl[rows, t, k * P:(k + 1) * P],
                                          g_proj[rows, t, G_V + h * GLA_DV:G_V + (h + 1) * GLA_DV],
                                          start=True, stop=True).then_inc(gs_done, 1)
                                m += 1
                    if par == 0:
                        for h in range(GLA_H):
                            a = t * GLA_H + h
                            if a >= 2:
                                pe.wait_ge(ga_masked, a - 1)
                            for j in range(2):
                                k = 2 * h + j
                                for half in range(2):
                                    hs = slice(half * CHUNK, (half + 1) * CHUNK)
                                    last = pe.matmul(ps[:, 4 + a % 2, hs], keT[:, k, t * P:(t + 1) * P],
                                                     qeT[:, k, t, half, hs], start=(j == 0 and half == 0),
                                                     stop=(j == 1), skip_group_check=True)
                            last.then_inc(ga_done, 1)
                            pe.wait_ge(ga_masked, a + 1)
                            if t == 1:
                                pe.wait_ge(go_out, h + 1)
                            pe.matmul(ps[:, h, :], gAT[:, a % 2, :],
                                      g_proj[:, t, G_V + h * GLA_DV:G_V + (h + 1) * GLA_DV], start=True, stop=False)
                    for h in range(GLA_H):
                        for j in range(2):
                            k = 2 * h + j
                            if ch > 0:
                                pe.wait_ge(gs_out, 8 * (ch - 1) + k + 1)
                                last = pe.matmul(ps[:, h, :], qeT[:, k, t, par, :], gst_in(ch)[:, h, j, :],
                                                 start=False, stop=(par == 1 and j == 1))
                        if par == 1:
                            last.then_inc(go_done, 1)


        def gla_scalar():
            turn_low.scalar()
            act = nc.scalar
            act.wait_ge(gk_abs, 1)
            Sc(act.activation(tmp_a, tmp_a, ACT.Exp, scale=-1.0))
            Sc(act.activation(tmp_a, tmp_a, ACT.Ln, bias=1.0))
            act.sem_inc(gk_exp, 1)
            act.wait_ge(cum_done, 1)
            act.wait_ge(gk_used, 1)
            for t in range(NT):
                for n in range(2):
                    e = tmp_a[:, t, n * W:(n + 1) * W]
                    Sc(act.activation(e, ps[:, 2 * t + n, :], ACT.Exp, scale=-1.0))
                    Sc(act.activation(ps[:, 2 * t + n, :], ps[:, 2 * t + n, :], ACT.Exp))
                    Sc(act.activation(ps[:, 4 + 2 * t + n, :], ps[:, 4 + 2 * t + n, :], ACT.Exp))
            act.sem_inc(cum_exp, 1)
            act.wait_ge(dl_done, 1)
            Sc(act.activation(dlT, ps[:, 0, 0:8 * NCH].rearrange("p (k c) -> p k c", k=8), ACT.Exp))
            act.sem_inc(dl_ready, 1)
            turn_qk.scalar()
            for t in range(NT):
                Sc(act.activation(g_proj[:, t, G_G:G_G + GLA_V], g_proj[:, t, G_G:G_G + GLA_V], ACT.Silu))
            act.sem_inc(gate_act, 1)
            for t in range(NT):
                for h in range(GLA_H):
                    act.wait_ge(go_done, t * GLA_H + h + 1)
                    act.copy(g_o[:, t, h * GLA_DV:(h + 1) * GLA_DV], ps[:, h, :]).then_inc(go_out, 1)
            act.wait_ge(go_out, NT * GLA_H)
            for t in range(NT):
                for h in range(GLA_H):
                    Sc(act.activation(tmp_a[:, 0, 0:GLA_DV], g_o[:, t, h * GLA_DV:(h + 1) * GLA_DV], ACT.Square,
                                      accum_out=gst_r[:, t * GLA_H + h:t * GLA_H + h + 1]))
            act.sem_inc(gn_sq, 1)
            act.wait_ge(gn_inv, 1)
            Sc(act.activation(gst_r, gst_r, ACT.Sqrt))
            act.sem_inc(gn_rs, 1)
            turn_go.scalar()

        def gla_vector():
            v = nc.vector
            prod_gla_low.wait_evicted(v)
            V(v.memset(qeT, 0.0))
            v.sem_inc(zeroed, 1)
            turn_low.vector()
            v.wait_ge(gk_done, 1)
            for t in range(NT):
                for n in range(2):
                    V(v.tensor_tensor(la[:, t, n * W:(n + 1) * W], ps[:, 2 * t + n, :],
                                      small["gla_bias"][:, n * W:(n + 1) * W], ALU.add))
            V(v.scalar_tensor_tensor(out=tmp_a, in0=la, scalar=-1.0, in1=la, op0=ALU.mult, op1=ALU.max))
            v.sem_inc(gk_abs, 1)
            V(v.tensor_scalar(la, la, 0.0, 1.0 / GLA_TAU, ALU.min, ALU.mult))
            v.wait_ge(gk_exp, 1)
            V(v.scalar_tensor_tensor(out=la, in0=tmp_a, scalar=-1.0 / GLA_TAU, in1=la, op0=ALU.mult, op1=ALU.add))
            v.sem_inc(gk_dec, 1)
            v.sem_inc(gk_used, 1)
            v.wait_ge(cum_exp, 1)
            for t in range(NT):
                for n in range(2):
                    c = slice(n * W, (n + 1) * W)
                    q = g_proj[:, t, n * W:(n + 1) * W]
                    k = g_proj[:, t, G_K + n * W:G_K + (n + 1) * W]
                    V(v.scalar_tensor_tensor(out=q, in0=q, scalar=float(GLA_DK) ** -0.5, in1=ps[:, 2 * t + n, :],
                                             op0=ALU.mult, op1=ALU.mult))
                    V(v.tensor_tensor(keT_tmp[:, 0:W], k, ps[:, 4 + 2 * t + n, :], ALU.mult))
                    V(v.tensor_tensor(k, k, tmp_a[:, t, c], ALU.mult))
                    V(v.tensor_copy(kl[:, t, c], keT_tmp[:, 0:W]))
                    if n == 1:
                        v.sem_inc(cum_free, 1)
            v.sem_inc(qk_ready, 1)
            turn_qk.vector()
            v.wait_ge(dl_ready, 1)
            m = 0
            for t in range(NT):
                for par in range(2):
                    ch = 2 * t + par
                    if ch < NCH - 1:
                        for h in range(GLA_H):
                            for j in range(2):
                                k = 2 * h + j
                                v.wait_ge(gs_done, m + 1)
                                if ch == 0:
                                    V(v.tensor_copy(gst_in(1)[:, h, j, :], ps[:, 6 + m % 2, :]))
                                else:
                                    V(v.scalar_tensor_tensor(out=gst_in(ch + 1)[:, h, j, :], in0=gst_in(ch)[:, h, j, :],
                                                             scalar=dlT[:, k, ch:ch + 1], in1=ps[:, 6 + m % 2, :],
                                                             op0=ALU.mult, op1=ALU.add))
                                v.sem_inc(gs_out, 1)
                                m += 1
                    if par == 0:
                        for h in range(GLA_H):
                            a = t * GLA_H + h
                            v.wait_ge(ga_done, a + 1)
                            V(v.tensor_tensor(gAT[:, a % 2, :], ps[:, 4 + a % 2, 0:P], upto, ALU.mult))
                            v.sem_inc(ga_masked, 1)
            v.wait_ge(gn_sq, 1)
            V(v.tensor_scalar(gst_r, gst_r, 1.0 / GLA_DV, EPS, ALU.mult, ALU.add))
            V(v.reciprocal(gst_r, gst_r))
            v.sem_inc(gn_inv, 1)
            v.wait_ge(gn_rs, 1)
            v.wait_ge(gate_act, 1)
            for t in range(NT):
                for h in range(GLA_H):
                    o = g_o[:, t, h * GLA_DV:(h + 1) * GLA_DV]
                    V(v.scalar_tensor_tensor(out=o, in0=o, scalar=gst_r[:, t * GLA_H + h:t * GLA_H + h + 1],
                                             in1=small["gla_onorm"][:, :], op0=ALU.mult, op1=ALU.mult))
                V(v.tensor_tensor(g_o[:, t, :], g_o[:, t, :], g_proj[:, t, G_G:G_G + GLA_V], ALU.mult))
            v.sem_inc(gn_out, 1)
            turn_go.vector()

        keT_tmp = view(scr, 8192, 8 * S)

        def over(ap, shape):
            return ap.to_broadcast(shape)

        m_proj = view(proj, 0, NT, 3136)
        M_G = LATENT
        m_q = view(proj, 6272, NT, 3072)
        m_kv = view(scr, 0, NT, 2 * D)
        m_norm = view(scr, 8192, NT, 2, MLA_RANK)
        cqT = view(scr, 10240, 4, S)
        ckvT = view(scr, 11264, 4, S)
        m_qr = view(scr, 0, NT, MLA_H * ROPE)
        m_tmp = view(scr, 2048, 2, NT, MLA_H * ROPE // 2)
        m_kr = view(scr, 4096, NT, 2 * ROPE)
        m_angle = view(scr, 4352, 4, NT, ROPE // 2)
        m_qT = HT[:, :, :]
        m_qrT = view(scr, 8192, MLA_H // 2, S)
        m_krT = scr[:, 12288:12288 + S]
        m_kT = view(proj, 6272, MLA_H, S)
        m_buf = proj[:, 10368:13600]

        prod_mla = wide(A["w_mla_in"], KD, 6, 0, turn_hidden)
        prod_mla_tail = Product([(A["w_mla_in"], KD, 3072, 0, 64, turn_hidden, False)])
        norm_q = Norm("norm_q", lambda t: m_proj[:, t, 0:MLA_RANK], MLA_RANK, stat_q, junk_q(scr),
                      lambda t: m_norm[:, t, 0, :])
        norm_kv = Norm("norm_kv", lambda t: m_proj[:, t, MLA_RANK:2 * MLA_RANK], MLA_RANK, stat_kv, junk_q(scr),
                       lambda t: m_norm[:, t, 1, :])
        turn_cq = turn_tokens("cq", lambda t, k: m_norm[:, t, 0, k * P:(k + 1) * P], 4, lambda k: cqT[:, k, :],
                              lambda k: small["qa"][:, k:k + 1])
        turn_ckv = turn_tokens("ckv", lambda t, k: m_norm[:, t, 1, k * P:(k + 1) * P], 4, lambda k: ckvT[:, k, :],
                               lambda k: small["kva"][:, k:k + 1])
        prod_q = Product([(A["w_qb"], 4, n * W, 0, W, lambda k: cqT[:, k, :], False) for n in range(6)])
        prod_kv = wide(A["w_kvb"], 4, 8, 0, lambda k: ckvT[:, k, :])
        q_turned = turn_tokens("mla_q", lambda t, k: m_q[:, t, k * 192:k * 192 + NOPE], MLA_H, lambda k: m_qT[:, k, :])
        qr_groups = turn_tokens("mla_unused", lambda t, k: m_qr[:, t, k * P:(k + 1) * P], 8, lambda k: m_qrT[:, k, :]).groups
        qr_groups = qr_groups + [([(m_kr[:, t, :], t * P) for t in range(NT)], [(m_krT, whole(P, 0, S), None)])]
        qr_turned = Turn("mla_rope", qr_groups)
        k_turned = turn_tokens("mla_k", lambda t, k: m_kv[:, t, k * 256:k * 256 + NOPE], MLA_H, lambda k: m_kT[:, k, :])
        angles, tables, rotated, m_gate = (sem("mla_" + n) for n in ("angles", "tables", "rotated", "gate_activated"))
        m_done = sem("mla_gated")

        def mla_parts(h, t):
            q = slice(t * P, (t + 1) * P)
            half = slice(ROPE * (h % 2), ROPE * (h % 2) + ROPE)
            return [(m_qT[:, h, q], m_kT[:, h, 0:(t + 1) * P]),
                    (m_qrT[half, h // 2, q], m_krT[half, 0:(t + 1) * P])]

        def mla_finish(h, bank, inv):
            for t in range(NT):
                g = m_proj[:, t, M_G + h * P:M_G + (h + 1) * P]
                V(nc.vector.scalar_tensor_tensor(out=g, in0=ps[:, bank, t * P:(t + 1) * P], scalar=inv[:, t:t + 1],
                                                 in1=g, op0=ALU.mult, op1=ALU.mult))

        attend = Attention("mla", MLA_H, mla_parts, lambda h, t: m_kv[:, t, h * 256 + NOPE:h * 256 + 256],
                           MLA_SCALE, m_buf, mla_finish)
        turn_mo = turn_tokens("mla_out", lambda t, k: m_proj[:, t, M_G + k * P:M_G + (k + 1) * P], KD, turn_hidden)
        prod_mla_out = wide(A["w_mla_out"], KD, 4, 0, turn_hidden)

        def rotate(x1, x2, c, s, t1, t2, out1, out2):
            v = nc.vector
            V(v.tensor_tensor(t1, x1, s, ALU.mult))
            V(v.tensor_tensor(t2, x2, s, ALU.mult))
            V(v.tensor_tensor(out1, x1, c, ALU.mult))
            V(v.tensor_tensor(out1, out1, t2, ALU.subtract))
            V(v.tensor_tensor(out2, x2, c, ALU.mult))
            V(v.tensor_tensor(out2, out2, t1, ALU.add))

        def mla_tables_vector():
            v = nc.vector
            n_ang, ang, cosang, ge = (m_angle[:, j] for j in range(4))
            v.wait_ge(s_pos, 16)
            V(v.tensor_copy(stat[:, 6:8], pos_i[:, :]))
            for t in range(NT):
                V(v.tensor_scalar(ang[:, t, :], C("inv_freq"), stat[:, 6 + t:7 + t], None, ALU.mult))
            rounder = 1.5 * 2.0 ** 23
            V(v.tensor_scalar(n_ang, ang, 1.0 / (2 * np.pi), rounder, ALU.mult, ALU.add))
            V(v.tensor_scalar(n_ang, n_ang, -rounder, None, ALU.add))
            p1 = 6.28125
            p2 = float(np.float32(np.round((2 * np.pi - p1) * 2 ** 21) / 2 ** 21))
            p3 = float(np.float32(2 * np.pi - p1 - p2))
            for part in (p1, p2, p3):
                V(v.scalar_tensor_tensor(out=ang, in0=n_ang, scalar=-part, in1=ang, op0=ALU.mult, op1=ALU.add))
            V(v.tensor_scalar(cosang, ang, float(np.pi / 2), None, ALU.add))
            V(v.tensor_scalar(ge, cosang, float(np.pi), -2 * float(np.pi), ALU.is_gt, ALU.mult))
            V(v.tensor_tensor(cosang, cosang, ge, ALU.add))
            for a in (ang, cosang):
                V(v.tensor_scalar(a, a, 3.14159, -3.14159, ALU.min, ALU.max))
            v.sem_inc(angles, 1)

        def mla_tables_scalar():
            nc.scalar.wait_ge(angles, 1)
            Sc(nc.scalar.activation(tab[:, 0, :, :], m_angle[:, 2], ACT.Sin))
            Sc(nc.scalar.activation(tab[:, 1, :, :], m_angle[:, 1], ACT.Sin))
            nc.scalar.sem_inc(tables, 1)

        def mla_rotate():
            v = nc.vector
            v.wait_ge(tables, 1)
            prod_q.wait_evicted(v)
            H2 = ROPE // 2
            for t in range(NT):
                q = m_q[:, t, :].rearrange("p (h d) -> p h d", h=MLA_H)
                out = m_qr[:, t, :].rearrange("p (h d) -> p h d", h=MLA_H)
                t1, t2 = (m_tmp[:, j, t, :].rearrange("p (h d) -> p h d", h=MLA_H) for j in range(2))
                c, s = (over(tab[:, j, t:t + 1, :], [P, MLA_H, H2]) for j in range(2))
                rotate(q[:, :, NOPE:NOPE + H2], q[:, :, NOPE + H2:], c, s, t1, t2, out[:, :, 0:H2], out[:, :, H2:])
                k = m_proj[:, t, 2 * MLA_RANK:2 * MLA_RANK + ROPE]
                kr = m_kr[:, t, :]
                rotate(k[:, 0:H2], k[:, H2:], tab[:, 0, t, :], tab[:, 1, t, :], m_tmp[:, 0, t, 0:H2], m_tmp[:, 1, t, 0:H2],
                       kr[:, 0:H2], kr[:, H2:ROPE])
                V(v.tensor_copy(kr[:, ROPE:], kr[:, 0:ROPE]))
            v.sem_inc(rotated, 1)

        NQ, NKVW = NSA_H * HD, 6 * NSA_KV * HD
        O_G = NQ + NKVW
        O_DN = O_G + 3 * NSA_H
        O_Z = O_DN + 3 * DN_H * HD
        O_AB = O_Z + DN_H * HD
        O_M = O_AB + 2 * DN_H
        z_tok = view(proj, 0, NT, DN_H * HD)
        n_g = view(proj, 2048, NT, 3 * NSA_H)
        d_ab = view(proj, 2096, NT, 2 * DN_H)
        n_qkv = view(proj, 2128, NT, NQ + NKVW)
        RAWW = S + CONV_K - 1
        raw = view(proj, 2128 + 5120, 3 * DN_H, RAWW)
        convd = view(scr, 0, 3 * DN_H, S)
        n_oT = view(scr, 6144, NSA_H, S)
        d_oT = view(scr, 8192, DN_H, S)
        n_qT = view(scr, 0, NSA_H, S)
        n_kT = view(scr, 2048, 4, NSA_KV, S)
        n_blk = view(scr, 4096, 2, CMP_BLOCK, NSA_KV * NCMP)
        n_buf = scr[:, 8192:10512]
        n_tmp = view(scr, 10240, 2, NSA_H * HD // 2)
        c_s = view(scr, 11264, NT, NSA_H, CPAD)
        c_p = view(scr, 11520, NT, NSA_H, CPAD)
        c_pT = view(scr, 11776, NT, P)
        c_v = view(scr, 10240, NSA_H, HD)
        c_g = view(scr, 12032, 2, NSA_KV, CPAD)
        c_u = view(scr, 12096, 2, NSA_KV * NCMP)
        c_h = view(scr, 12156, 2, NSA_KV * NCMP)
        c_k = view(scr, 12216, NSA_KV, CPAD)
        c_gx = view(scr, 12248, NSA_H, CPAD)
        c_max = view(scr, 12376, NT, NSA_H)
        c_sum = view(scr, 12392, NT, NSA_H)
        c_fac = scr[:, 12408:12410]

        prod_n = Product([(A["w_in2"], KD, n * W, 0, W, turn_hidden, False) for n in range(5)])
        prod_ng = Product([(A["w_in2"], KD, O_G, 0, 3 * NSA_H, turn_hidden, False)])
        prod_z = wide(A["w_in2"], KD, 2, O_Z, turn_hidden)
        prod_ab = Product([(A["w_in2"], KD, O_AB, 0, 2 * DN_H, turn_hidden, False)])
        prod_dn = Product([(A["w_in2"], KD, O_DN + n * W, 2 * W, W, turn_hidden, True) for n in range(2)], 3)

        def cmp_weights(w):
            def pair(slot, k0):
                r = k0 * (W // HD)
                return (slot.rearrange("p a b -> p (a b)").rearrange("p (r f) -> p r f", f=HD),
                        w[r * P:(r + 8) * P, :].rearrange("(r p) f -> p r f", p=P))
            return pair

        def cmp_multiply(j):
            def mm(slot, k0, b):
                flat = slot.rearrange("p a b -> p (a b)")
                for r in range(8):
                    rr = k0 * (W // HD) + r
                    last = nc.tensor.matmul(ps[:, b, 0:NSA_KV * NCMP], flat[:, r * HD:(r + 1) * HD], n_blk[:, j, rr, :],
                                            start=(rr == 0), stop=(rr == CMP_BLOCK - 1))
                return last
            return mm

        prod_cmp = Product([(cmp_weights(A["cmp_w1"][j]), 8, 0, 0, W, cmp_multiply(j), False) for j in range(2)])

        n_rot, n_gates, blk_ready = sem("nsa_rotated"), sem("nsa_gates_ready"), sem("nsa_blocks_ready")
        groups = turn_tokens("nsa_unused", lambda t, k: n_qkv[:, t, k * P:(k + 1) * P], NSA_H, lambda k: n_qT[:, k, :]).groups
        for j, idx in enumerate((0, 1, 2, 4)):
            tiles = [(n_qkv[:, t, NQ + (2 * idx + hk) * HD:NQ + (2 * idx + hk + 1) * HD], hk * S + t * P)
                     for hk in range(NSA_KV) for t in range(NT)]
            groups.append((tiles, [(n_kT[:, j, hk, :], whole(P, hk * S, S), None) for hk in range(NSA_KV)]))
        turn_n = Turn("nsa_qk", groups)
        c_lin, c_tanh, c_act, c_proj, c_keys = (sem("cmp_" + n) for n in ("cubic", "tanh", "activated", "projected", "keys_ready"))
        c_scored, c_centred, c_exped, c_probs = (sem("cmp_" + n) for n in ("scored", "centred", "exped", "probs"))
        turn_cp = Turn("cmp_probs", [([(c_p[:, t, :, :].rearrange("p h c -> p (h c)"), t * P) for t in range(NT)],
                                      [(c_pT.rearrange("p t n -> p (t n)"), whole(P, 0, S), None)])])
        c_mixed, c_out = sem("cmp_mixed"), sem("cmp_out")

        def nsa_parts(h, t):
            which, hh = h // NSA_H, h % NSA_H
            return [(n_qT[:, hh, t * P:(t + 1) * P], n_kT[:, 2 + which, hh // NSA_G, 0:(t + 1) * P])]

        def nsa_value(h, t):
            which, hh = h // NSA_H, h % NSA_H
            o = NQ + (2 * (3 + 2 * which) + hh // NSA_G) * HD
            return n_qkv[:, t, o:o + HD]

        def nsa_finish(h, bank, inv):
            which, hh = h // NSA_H, h % NSA_H
            for t in range(NT):
                g = n_g[:, t, 3 * hh + 1 + which:3 * hh + 2 + which]
                V(nc.vector.tensor_tensor(c_fac[:, t:t + 1], inv[:, t:t + 1], g, ALU.mult))
                o = n_qkv[:, t, hh * HD:(hh + 1) * HD]
                V(nc.vector.scalar_tensor_tensor(out=o, in0=ps[:, bank, t * P:(t + 1) * P], scalar=c_fac[:, t:t + 1],
                                                 in1=o, op0=ALU.mult, op1=ALU.add))

        attend2 = Attention("nsa", 2 * NSA_H, nsa_parts, nsa_value, NSA_SCALE, n_buf, nsa_finish)
        turn_no = turn_tokens("nsa_out", lambda t, k: n_qkv[:, t, k * P:(k + 1) * P], NSA_H, lambda k: n_oT[:, k, :])

        def nsa_tensor(pe):
            pe.wait_ge(n_rot, 1)
            turn_n.tensor(pe)
            pe.wait_ge(blk_ready, 1)
            prod_cmp.tensor(pe)
            pe.wait_ge(c_act, 1)
            pe.matmul(ps[:, 4, 0:NSA_KV * CPAD], w2k[:, :], c_g[:, 0, :, :].rearrange("p a b -> p (a b)"), start=True, stop=True)
            pe.matmul(ps[:, 5, 0:HD], c_gx.rearrange("p h c -> p (h c)"), w2v[:, :], start=True, stop=True).then_inc(c_proj, 1)
            pe.wait_ge(c_keys, 1)
            for t in range(NT):
                for h in range(NSA_H):
                    o = (t * NSA_H + h) * CPAD
                    last = pe.matmul(ps[:, 6, o:o + CPAD], n_qT[:, h, t * P:(t + 1) * P], c_k[:, h // NSA_G, :],
                                     start=True, stop=True)
            last.then_inc(c_scored, 1)
            pe.wait_ge(c_probs, 1)
            turn_cp.tensor(pe)
            turn_cp.wait(pe)
            for t in range(NT):
                for n in range(2):
                    last = pe.matmul(ps[:, 4 + 2 * t + n, :], c_pT[:, t, :],
                                     c_v[:, 4 * n:4 * n + 4, :].rearrange("p h d -> p (h d)"), start=True, stop=True)
            last.then_inc(c_mixed, 1)
            pe.wait_ge(c_out, 1)
            attend2.tensor(pe)
            pe.wait_ge(attend2.finished, 2 * NSA_H)
            turn_no.tensor(pe)

        def nsa_scalar():
            act = nc.scalar
            Sc(act.activation(n_g, n_g, ACT.Sigmoid))
            act.sem_inc(n_gates, 1)
            turn_n.scalar()
            act.wait_ge(c_lin, 1)
            Sc(act.activation(c_u, c_u, ACT.Tanh, scale=GELU_C))
            act.sem_inc(c_tanh, 1)
            act.wait_ge(c_centred, 1)
            Sc(act.activation(c_p, c_s, ACT.Exp))
            act.sem_inc(c_exped, 1)
            attend2.scalar()
            turn_no.scalar()

        def nsa_vector():
            v = nc.vector
            cos, sin = (C(n).rearrange("p (t f) -> p t f", t=NT) for n in ("cos2", "sin2"))
            prod_ng.wait_evicted(v)
            H2 = HD // 2
            for t in range(NT):
                q = n_qkv[:, t, 0:NQ].rearrange("p (h d) -> p h d", h=NSA_H)
                sets = [(q, NSA_H)]
                for idx in (0, 2, 4):
                    o = NQ + 2 * idx * HD
                    sets.append((n_qkv[:, t, o:o + 2 * HD].rearrange("p (h d) -> p h d", h=2), 2))
                for x, n in sets:
                    t1, t2 = (n_tmp[:, j, 0:n * H2].rearrange("p (h d) -> p h d", h=n) for j in range(2))
                    c, s = (over(a[:, t:t + 1, :], [P, n, H2]) for a in (cos, sin))
                    rotate(x[:, :, 0:H2], x[:, :, H2:], c, s, t1, t2, x[:, :, 0:H2], x[:, :, H2:])
            v.sem_inc(n_rot, 1)
            turn_n.vector()
            turn_n.wait(v)
            for j in range(2):
                pe_t = small["cmp_pe"][:, j * CMP_BLOCK:(j + 1) * CMP_BLOCK].unsqueeze(2)
                for hk in range(NSA_KV):
                    base = n_kT[:, j, hk, 0:NCMP * CMP_STRIDE].rearrange("p (c r) -> p r c", r=CMP_STRIDE)
                    next_ = n_kT[:, j, hk, CMP_STRIDE:(NCMP + 1) * CMP_STRIDE].rearrange("p (c r) -> p r c", r=CMP_STRIDE)
                    for half, src in enumerate((base, next_)):
                        r = slice(half * CMP_STRIDE, (half + 1) * CMP_STRIDE)
                        V(v.tensor_tensor(n_blk[:, j, r, hk * NCMP:(hk + 1) * NCMP], src,
                                          over(pe_t[:, r, :], [P, CMP_STRIDE, NCMP]), ALU.add))
            v.sem_inc(blk_ready, 1)
            V(v.memset(c_g, 0.0))

            def copy_hidden(i, n, b):
                return v.tensor_copy(c_h[:, n, :], ps[:, b, 0:NSA_KV * NCMP])
            prod_cmp.evict(v, range(2), copy_hidden)
            prod_cmp.wait_evicted(v)
            V(v.tensor_tensor(c_u, c_h, c_h, ALU.mult))
            V(v.tensor_scalar(c_u, c_u, GELU_A, 1.0, ALU.mult, ALU.add))
            V(v.tensor_tensor(c_u, c_u, c_h, ALU.mult))
            v.sem_inc(c_lin, 1)
            v.wait_ge(c_tanh, 1)
            V(v.scalar_tensor_tensor(out=c_u, in0=c_u, scalar=1.0, in1=c_h, op0=ALU.add, op1=ALU.mult))
            for j in range(2):
                V(v.tensor_scalar(c_g[:, j, :, 0:NCMP], c_u[:, j, :].rearrange("p (a b) -> p a b", a=NSA_KV), 0.5, None, ALU.mult))
            for hk in range(NSA_KV):
                V(v.tensor_copy(c_gx[:, hk * NSA_G:(hk + 1) * NSA_G, :], over(c_g[:, 1, hk:hk + 1, :], [P, NSA_G, CPAD])))
            v.sem_inc(c_act, 1)
            v.wait_ge(c_proj, 1)
            V(v.tensor_copy(c_k, ps[:, 4, 0:NSA_KV * CPAD].rearrange("p (a b) -> p a b", a=NSA_KV)))
            for h in range(NSA_H):
                V(v.tensor_scalar(c_v[:, h, :], ps[:, 5, 0:HD], C("cmp_head")[:, h:h + 1], None, ALU.mult))
            v.sem_inc(c_keys, 1)
            v.wait_ge(c_scored, 1)
            mask = C("cmp_mask").rearrange("p (t c) -> p t c", t=NT)
            for t in range(NT):
                V(v.scalar_tensor_tensor(out=c_s[:, t, :, :],
                                         in0=ps[:, 6, t * P:(t + 1) * P].rearrange("p (h c) -> p h c", h=NSA_H),
                                         scalar=NSA_SCALE, in1=over(mask[:, t:t + 1, :], [P, NSA_H, CPAD]),
                                         op0=ALU.mult, op1=ALU.add))
                V(v.tensor_reduce(c_max[:, t, :], c_s[:, t, :, :], AX, ALU.max))
                V(v.tensor_tensor(c_s[:, t, :, :], c_s[:, t, :, :], over(c_max[:, t, :].unsqueeze(2), [P, NSA_H, CPAD]),
                                  ALU.subtract))
            v.sem_inc(c_centred, 1)
            v.wait_ge(c_exped, 1)
            for t in range(NT):
                V(v.tensor_reduce(c_sum[:, t, :], c_p[:, t, :, :], AX, ALU.add))
            V(v.reciprocal(c_sum, c_sum))
            v.wait_ge(n_gates, 1)
            for t in range(NT):
                V(v.scalar_tensor_tensor(out=c_sum[:, t, :], in0=c_sum[:, t, :], scalar=C("cmp_any")[:, t:t + 1],
                                         in1=n_g[:, t, :].rearrange("p (h j) -> p h j", j=3)[:, :, 0],
                                         op0=ALU.mult, op1=ALU.mult))
                V(v.tensor_tensor(c_p[:, t, :, :], c_p[:, t, :, :], over(c_sum[:, t, :].unsqueeze(2), [P, NSA_H, CPAD]), ALU.mult))
            v.sem_inc(c_probs, 1)
            turn_cp.vector()
            v.wait_ge(c_mixed, 1)
            for t in range(NT):
                for n in range(2):
                    V(v.tensor_copy(n_qkv[:, t, n * W:(n + 1) * W], ps[:, 4 + 2 * t + n, :]))
            v.sem_inc(c_out, 1)
            attend2.vector()
            turn_no.vector()

        HB = 4
        NM = HB * NT
        base = 2128
        def mats(n):
            return view(proj, base + n * NM * P, NM, P)
        (d_u0, d_ct, d_er, d_dt, d_at, d_lt, d_x, d_xt, d_kg, d_kd, d_vb) = (mats(n) for n in range(11))
        d_vn, d_os = d_u0, d_ct
        d_s = view(scr, 10240, HB, HD)
        d_uu, d_w = d_dt, d_lt
        d_sq = view(scr, 10752, 2, S)
        d_st = view(scr, 11264, 8, NT, DN_H)
        d_beta, d_dec, d_gc, d_egc, d_eleft, d_t0, d_t1 = (d_st[:, n] for n in range(7))
        d_nst = stat[:, 16:16 + NM]
        pad_ready = sem("dn_pad_ready")
        conv_done, conv_act = sem("dn_convolved"), sem("dn_conv_activated")
        l2_sq, l2_sum, l2_root, l2_free, l2_inv = (sem("l2_" + n) for n in ("squares", "sums", "roots", "sums_read", "inverted"))
        ab_sig, ab_abs, ab_exp, ab_dec, ab_cum, ab_cexp = (sem("dn_" + n) for n in ("beta", "abs", "softplus", "decays", "cumulated", "decay_exps"))
        l2_done = sem("dn_normalised")
        (b_rows, b_rowed, b_erow, b_clamped, b_dexp, b_kk, b_lt, b_tok, b_tokd) = (sem("dn_" + n) for n in (
            "row_inputs", "rows", "row_exps", "clamped", "decay_ready", "products", "systems_ready", "tokens", "tokens_ready"))
        (b_ct, b_t1, b_t1c, b_x, b_xd) = (sem("dn_inv_" + n) for n in ("corner", "corner_times", "corner_times_copied", "update", "updated"))
        (b_uw, b_uwc, b_sc, b_vn, b_sn, b_si, b_in, b_ind) = (sem("dn_" + n) for n in (
            "uw", "uw_copied", "state_read", "values_new", "state_update", "state_ready", "within", "outputs"))
        b_inc, b_nsq, b_ninv, b_nrs, b_fin = (sem("dn_" + n) for n in ("scan_started", "norm_squares", "norm_inverse", "norm_ready", "normed"))
        turn_do = []
        for bt in range(DN_H // HB):
            turn_do.append(turn_tokens(f"dn_out{bt}", lambda t, k: d_os[:, k * NT + t, :], HB,
                                       lambda k, bt=bt: d_oT[:, bt * HB + k, :]))
        BANK = lambda a: ps[:, a:a + 2, :].rearrange("p a (m n) -> p (a m) n", n=P)

        def dn_tensor(pe):
            for g in range(DN_H):
                pe.wait_ge(l2_sq, g + 1)
                if g >= 2:
                    pe.wait_ge(l2_free, g - 1)
                pe.matmul(ps[:, 4 + g % 2, :], ones, d_sq2(g), start=True, stop=True).then_inc(l2_sum, 1)
            pe.wait_ge(ab_dec, 1)
            for t in range(NT):
                pe.matmul(ps[:, 6, t * 8:t * 8 + 8], upto, d_dec[:, t, :], start=True, stop=True)
                last = pe.matmul(ps[:, 6, 16 + t * 8:24 + t * 8], after, d_dec[:, t, :], start=True, stop=True)
            last.then_inc(ab_cum, 1)
            pe.wait_ge(l2_done, 1)
            for bt in range(DN_H // HB):
                def kq(which, m):
                    return convd[:, which * DN_H + bt * HB + m // NT, (m % NT) * P:(m % NT + 1) * P]
                pe.wait_ge(b_rows, bt + 1)
                for m in range(NM):
                    pe.matmul(BANK(0)[:, m, :], ones, d_u0[:, m, :], start=True, stop=True)
                    last = pe.matmul(BANK(2)[:, m, :], ones, d_ct[:, m, :], start=True, stop=True)
                last.then_inc(b_rowed, 1)
                for m in range(NM):
                    pe.matmul(BANK(4)[:, m, :], kq(1, m), kq(1, m), start=True, stop=True)
                    last = pe.matmul(BANK(6)[:, m, :], kq(1, m), kq(0, m), start=True, stop=True)
                last.then_inc(b_kk, 1)
                pe.wait_ge(b_lt, bt + 1)
                for m in range(NM):
                    pe.transpose(BANK(4)[:, m, :], kq(1, m), ident)
                    last = pe.transpose(BANK(6)[:, m, :], kq(2, m), ident)
                last.then_inc(b_tok, 1)
                pe.wait_ge(b_tokd, bt + 1)
                for lv in range(6):
                    pe.wait_ge(b_ct, 6 * bt + lv + 1)
                    for m in range(NM):
                        last = pe.matmul(BANK(0)[:, m, :], d_ct[:, m, :], d_x[:, m, :], start=True, stop=True)
                    last.then_inc(b_t1, 1)
                    pe.wait_ge(b_t1c, 6 * bt + lv + 1)
                    for m in range(NM):
                        pe.matmul(BANK(4)[:, m, :], d_xt[:, m, :], d_u0[:, m, :], start=True, stop=True)
                        last = pe.matmul(BANK(6)[:, m, :], d_u0[:, m, :], d_xt[:, m, :], start=True, stop=True)
                    last.then_inc(b_x, 1)
                pe.wait_ge(b_xd, 6 * (bt + 1))
                for m in range(NM):
                    pe.matmul(BANK(0)[:, m, :], d_xt[:, m, :], d_vb[:, m, :], start=True, stop=True)
                    last = pe.matmul(BANK(2)[:, m, :], d_kg[:, m, :], d_xt[:, m, :], start=True, stop=True)
                last.then_inc(b_uw, 1)
                pe.wait_ge(b_uwc, bt + 1)
                for ch in range(NCH):
                    t, par = ch // 2, ch % 2
                    rows = slice(par * CHUNK, (par + 1) * CHUNK)
                    if ch > 0:
                        pe.wait_ge(b_si, 3 * bt + ch)
                        for hl in range(HB):
                            m = hl * NT + t
                            pe.matmul(ps[:, 4, hl * P:(hl + 1) * P], d_w[:, m, :], d_s[:, hl, :], start=True, stop=True)
                            last = pe.matmul(ps[:, 5, hl * P:(hl + 1) * P], kq(0, m), d_s[:, hl, :], start=True, stop=True)
                        last.then_inc(b_sc, 1)
                    if ch < NCH - 1:
                        pe.wait_ge(b_vn, NCH * bt + ch + 1)
                        for hl in range(HB):
                            m = hl * NT + t
                            last = pe.matmul(ps[:, 6, hl * P:(hl + 1) * P], d_kd[rows, m, :], d_vn[rows, m, :], start=True, stop=True)
                        last.then_inc(b_sn, 1)
                pe.wait_ge(b_vn, NCH * (bt + 1))
                for m in range(NM):
                    last = pe.matmul(BANK(0)[:, m, :], d_at[:, m, :], d_vn[:, m, :], start=True, stop=True)
                last.then_inc(b_in, 1)
                pe.wait_ge(b_fin, bt + 1)
                turn_do[bt].tensor(pe)
                turn_do[bt].wait(pe)

        def d_sq2(g):
            return (d_sq if g % 2 == 0 else d_sqb).rearrange("p a n -> p (a n)")

        d_sqb = view(scr, 11376 + 0, 2, S)

        def dn_scalar():
            act = nc.scalar
            act.wait_ge(conv_done, 1)
            for half in range(3):
                Sc(act.activation(convd[:, half * 8:(half + 1) * 8, :], convd[:, half * 8:(half + 1) * 8, :], ACT.Silu))
            Sc(act.activation(z_tok, z_tok, ACT.Silu))
            Sc(act.activation(d_beta, d_ab[:, :, DN_H:], ACT.Sigmoid))
            act.sem_inc(conv_act, 1)
            for g in range(DN_H):
                if g >= 2:
                    act.wait_ge(l2_sum, g - 1)
                Sc(act.activation(d_sq2(g), convd[:, 2 * g:2 * g + 2, :].rearrange("p a n -> p (a n)"), ACT.Square))
                act.sem_inc(l2_sq, 1)
            for g in range(DN_H):
                act.wait_ge(l2_inv, g + 1)
                Sc(act.activation(d_rt(g), d_rt(g), ACT.Sqrt))
                act.sem_inc(l2_root, 1)
            act.wait_ge(ab_abs, 1)
            Sc(act.activation(d_t0, d_t0, ACT.Exp, scale=-1.0))
            Sc(act.activation(d_t0, d_t0, ACT.Ln, bias=1.0))
            Sc(act.activation(small_alog[:, :], small["alog"][:, :], ACT.Exp))
            act.sem_inc(ab_exp, 1)
            act.wait_ge(ab_cum, 1)
            Sc(act.copy(d_gc, ps[:, 6, 0:16].rearrange("p (t h) -> p t h", t=NT)))
            Sc(act.activation(d_egc, ps[:, 6, 0:16].rearrange("p (t h) -> p t h", t=NT), ACT.Exp))
            Sc(act.activation(d_eleft, ps[:, 6, 16:32].rearrange("p (t h) -> p t h", t=NT), ACT.Exp))
            act.sem_inc(ab_cexp, 1)
            for bt in range(DN_H // HB):
                act.wait_ge(b_rowed, bt + 1)
                Sc(act.activation(d_er.rearrange("p m n -> p (m n)"), ps[:, 0:2, :].rearrange("p a n -> p (a n)"), ACT.Exp))
                act.sem_inc(b_erow, 1)
                act.wait_ge(b_clamped, bt + 1)
                Sc(act.activation(d_dt, d_dt, ACT.Exp))
                act.sem_inc(b_dexp, 1)
                for lv in range(6):
                    act.wait_ge(b_t1, 6 * bt + lv + 1)
                    Sc(act.copy(d_u0, BANK(0)))
                    act.sem_inc(b_t1c, 1)
                act.wait_ge(b_uw, bt + 1)
                Sc(act.copy(d_uu, BANK(0)))
                Sc(act.copy(d_w, BANK(2)))
                act.sem_inc(b_uwc, 1)
                act.wait_ge(b_ind, bt + 1)
                for m in range(NM):
                    Sc(act.activation(d_x[:, 0, :], d_os[:, m, :], ACT.Square, accum_out=d_nst[:, m:m + 1]))
                act.sem_inc(b_nsq, 1)
                act.wait_ge(b_ninv, bt + 1)
                Sc(act.activation(d_nst, d_nst, ACT.Sqrt))
                act.sem_inc(b_nrs, 1)
                turn_do[bt].scalar()

        small_alog = sb("dn_decay_rate", [P, DN_H])

        def d_rt(g):
            return view(proj, base + g * 512, 2, S)

        def dn_vector():
            v = nc.vector
            prod_dn.wait_evicted(v)
            cw = small["conv"]
            for f in range(3 * DN_H):
                V(v.tensor_scalar(convd[:, f, :], raw[:, f, 0:S], cw[:, CONV_K * f:CONV_K * f + 1], None, ALU.mult))
                for j in range(1, CONV_K):
                    V(v.scalar_tensor_tensor(out=convd[:, f, :], in0=raw[:, f, j:j + S],
                                             scalar=cw[:, CONV_K * f + j:CONV_K * f + j + 1], in1=convd[:, f, :],
                                             op0=ALU.mult, op1=ALU.add))
            v.sem_inc(conv_done, 1)
            v.wait_ge(conv_act, 1)
            for t in range(NT):
                V(v.tensor_tensor(d_t1[:, t, :], d_ab[:, t, 0:DN_H], small["dt_bias"][:, :], ALU.add))
            V(v.scalar_tensor_tensor(out=d_t0, in0=d_t1, scalar=-1.0, in1=d_t1, op0=ALU.mult, op1=ALU.max))
            for g in range(DN_H):
                v.wait_ge(l2_sum, g + 1)
                rt = d_rt(g).rearrange("p a n -> p (a n)")
                V(v.tensor_scalar(rt, ps[:, 4 + g % 2, :], EPS, None, ALU.add))
                v.sem_inc(l2_free, 1)
                V(v.reciprocal(rt, rt))
                v.sem_inc(l2_inv, 1)
            for g in range(DN_H):
                v.wait_ge(l2_root, g + 1)
                x = convd[:, 2 * g:2 * g + 2, :]
                V(v.scalar_tensor_tensor(out=x, in0=x, scalar=float(HD) ** -0.5 if g < 4 else 1.0, in1=d_rt(g),
                                         op0=ALU.mult, op1=ALU.mult))
            v.sem_inc(ab_abs, 1)
            v.wait_ge(ab_exp, 1)
            V(v.scalar_tensor_tensor(out=d_t0, in0=d_t1, scalar=0.0, in1=d_t0, op0=ALU.max, op1=ALU.add))
            for t in range(NT):
                V(v.scalar_tensor_tensor(out=d_dec[:, t, :], in0=d_t0[:, t, :], scalar=-1.0, in1=small_alog[:, :],
                                         op0=ALU.mult, op1=ALU.mult))
            v.sem_inc(ab_dec, 1)
            v.sem_inc(l2_done, 1)
            v.wait_ge(ab_cexp, 1)
            for bt in range(DN_H // HB):
                def col(a, m):
                    h = bt * HB + m // NT
                    return a[:, m % NT, h:h + 1]
                for m in range(NM):
                    V(v.tensor_scalar(d_u0[:, m, :], upto, col(d_dec, m), None, ALU.mult))
                    V(v.tensor_scalar(d_ct[:, m, :], ident, col(d_beta, m), None, ALU.mult))
                v.sem_inc(b_rows, 1)
                v.wait_ge(b_rowed, bt + 1)
                v.wait_ge(b_erow, bt + 1)
                for m in range(NM):
                    V(v.tensor_scalar(d_dt[:, m, :], BANK(0)[:, m, :], col(d_gc, m), 0.0, ALU.subtract, ALU.min))
                v.sem_inc(b_clamped, 1)
                v.wait_ge(b_dexp, bt + 1)
                V(v.tensor_tensor(d_dt, d_dt, over(upto.unsqueeze(1), [P, NM, P]), ALU.mult))
                v.wait_ge(b_kk, bt + 1)
                V(v.tensor_tensor(d_at, BANK(6), d_dt, ALU.mult))
                V(v.tensor_tensor(d_lt, BANK(4), d_dt, ALU.mult))
                V(v.tensor_tensor(d_lt, d_lt, BANK(2), ALU.mult))
                v.sem_inc(b_lt, 1)
                v.wait_ge(b_tok, bt + 1)
                for m in range(NM):
                    V(v.tensor_scalar(d_kg[:, m, :], BANK(4)[:, m, :], col(d_beta, m), col(d_egc, m), ALU.mult, ALU.mult))
                    V(v.tensor_scalar(d_kd[:, m, :], BANK(4)[:, m, :], col(d_eleft, m), None, ALU.mult))
                    V(v.tensor_scalar(d_vb[:, m, :], BANK(6)[:, m, :], col(d_beta, m), None, ALU.mult))
                q = convd[:, bt * HB:(bt + 1) * HB, :].rearrange("p h (t n) -> p (h t) n", t=NT)
                V(v.tensor_tensor(q, q, d_er, ALU.mult))
                V(v.tensor_copy(d_x, over(ident.unsqueeze(1), [P, NM, P])))
                V(v.tensor_copy(d_xt, over(ident.unsqueeze(1), [P, NM, P])))
                v.sem_inc(b_tokd, 1)
                for lv in range(6):
                    V(v.tensor_tensor(d_ct, d_lt, over(C("levels")[:, lv * P:(lv + 1) * P].unsqueeze(1), [P, NM, P]), ALU.mult))
                    v.sem_inc(b_ct, 1)
                    v.wait_ge(b_x, 6 * bt + lv + 1)
                    V(v.tensor_tensor(d_x, d_x, BANK(4), ALU.subtract))
                    V(v.tensor_tensor(d_xt, d_xt, BANK(6), ALU.subtract))
                    v.sem_inc(b_xd, 1)
                v.wait_ge(b_uwc, bt + 1)
                er4 = d_er.rearrange("p (h t) n -> p h t n", t=NT)
                split = lambda a: a.rearrange("p (h t) n -> p h t n", t=NT)
                bank = lambda n: ps[:, n, :].rearrange("p (h n) -> p h n", h=HB)
                for ch in range(NCH):
                    t, par = ch // 2, ch % 2
                    rows = slice(par * CHUNK, (par + 1) * CHUNK)
                    vn, uu, os_ = (split(a)[rows, :, t, :] for a in (d_vn, d_uu, d_os))
                    if ch == 0:
                        V(v.tensor_copy(vn, uu))
                        V(v.memset(os_, 0.0))
                    else:
                        v.wait_ge(b_sc, 3 * bt + ch)
                        V(v.tensor_tensor(vn, uu, bank(4)[rows], ALU.subtract))
                        V(v.tensor_copy(os_, bank(5)[rows]))
                    v.sem_inc(b_vn, 1)
                    if ch < NCH - 1:
                        last = par * CHUNK + CHUNK - 1
                        v.wait_ge(b_sn, 3 * bt + ch + 1)
                        if ch == 0:
                            V(v.tensor_copy(d_s, bank(6)))
                        else:
                            V(v.tensor_tensor(d_s, d_s, over(er4[:, :, t, last:last + 1], [P, HB, HD]), ALU.mult))
                            V(v.tensor_tensor(d_s, d_s, bank(6), ALU.add))
                        v.sem_inc(b_si, 1)
                v.wait_ge(b_in, bt + 1)
                V(v.tensor_tensor(d_os, d_os, BANK(0), ALU.add))
                v.sem_inc(b_ind, 1)
                v.wait_ge(b_nsq, bt + 1)
                V(v.tensor_scalar(d_nst, d_nst, 1.0 / HD, EPS, ALU.mult, ALU.add))
                V(v.reciprocal(d_nst, d_nst))
                v.sem_inc(b_ninv, 1)
                v.wait_ge(b_nrs, bt + 1)
                for m in range(NM):
                    h, t = bt * HB + m // NT, m % NT
                    V(v.scalar_tensor_tensor(out=d_os[:, m, :], in0=d_os[:, m, :], scalar=d_nst[:, m:m + 1],
                                             in1=small["dn_norm"][:, :], op0=ALU.mult, op1=ALU.mult))
                    V(v.tensor_tensor(d_os[:, m, :], d_os[:, m, :], z_tok[:, t, h * HD:(h + 1) * HD], ALU.mult))
                v.sem_inc(b_fin, 1)
                turn_do[bt].vector()
                turn_do[bt].wait(v)

        mixed = view(proj, 0, NT, D)
        sig = view(proj, 4096, 2, NT, W)
        prod_merge = Product([(A["w_up"][0], 8, 0, W, W, lambda k: n_oT[:, k, :], False),
                              (A["w_in2"], KD, O_M, W, W, turn_hidden, False),
                              (A["w_up"][1], 8, 0, W, W, lambda k: d_oT[:, k, :], False),
                              (A["w_in2"], KD, O_M + D, W, W, turn_hidden, False)], D // W)
        sig_ready, sig_free = sem("merge_gate_ready"), sem("merge_gate_used")
        turn_mix = turn_tokens("merge", lambda t, k: mixed[:, t, k * P:(k + 1) * P], KD, turn_hidden)
        prod_o = wide(A["w_o"], KD, 4, 0, turn_hidden)
        added = sem("attention_added")

        def merge_scalar():
            def body(i, n, b):
                if n % 2 == 0:
                    for t in range(NT):
                        last = nc.scalar.copy(part2[:, n // 2, t, :], ps[:, b + t, :])
                else:
                    for t in range(NT):
                        last = nc.scalar.activation(sig[:, n // 2, t, :], ps[:, b + t, :], ACT.Sigmoid)
                return last
            pr = prod_merge

            def rounds(i):
                for n in range(4):
                    c = pr.chunk0 + n
                    nc.scalar.wait_ge(chunk_done[c % 2], i * 2 + c // 2 + 1)
                    if n == 0 and not (isinstance(i, int) and i == 0):
                        nc.scalar.wait_ge(sig_free, i)
                    body(i, n, 2 * (c % 2)).then_inc(chunk_evicted[c % 2], 1)
            rounds(0)
            with nc.scalar.Fori(1, pr.rounds) as i:
                rounds(i)

        part2 = view(proj, 6144, 2, NT, W)

        def merge_vector():
            pr = prod_merge
            v = nc.vector

            def rounds(i):
                v.wait_ge(chunk_evicted[0], i * 2 + (pr.chunk0 + 5) // 2)
                v.wait_ge(chunk_evicted[1], i * 2 + (pr.chunk0 + 4) // 2)
                for n in range(2):
                    for t in range(NT):
                        last = v.tensor_tensor(sig[:, n, t, :], sig[:, n, t, :], part2[:, n, t, :], ALU.mult)
                last.then_inc(merge_mul, 1)
                v.wait_ge(merge_mul, i + 1)
                for t in range(NT):
                    last = v.tensor_tensor(mixed[:, t, piece(i, W, 0, W)], sig[:, 0, t, :], sig[:, 1, t, :], ALU.add)
                last.then_inc(sig_free, 1)
            rounds(0)
            with v.Fori(1, pr.rounds) as i:
                rounds(i)
            v.wait_ge(sig_free, pr.rounds)
            v.sem_inc(merged, 1)

        merge_mul, merged = sem("merge_products"), sem("merged")

        NF = D_FF // P
        actT = view(proj, 0, NF, S)
        gateT = view(scr, 0, 4, S)
        prod_ffn = Product([(A["w_gate"], KD, 0, W, W, turn_hidden, True),
                            (A["w_ffn_up"], KD, 0, W, W, turn_hidden, True)], D_FF // W)
        ffn_gate, ffn_prod = sem("ffn_gate_ready"), sem("ffn_gate_used")
        prod_down = Product([(A["w_down"], NF, n * W, 0, W, lambda k: actT[:, k, :], False) for n in range(4)])
        ffn_added = sem("ffn_added")

        def two(b, t):
            return ps[:, b + t, :].rearrange("p (f n) -> p f n", n=S)

        def ffn_scalar():
            pr = prod_ffn

            def rounds(i):
                c = pr.chunk0
                nc.scalar.wait_ge(chunk_done[c % 2], i + c // 2 + 1)
                if not (isinstance(i, int) and i == 0):
                    nc.scalar.wait_ge(ffn_prod, i)
                for t in range(2):
                    last = nc.scalar.activation(gateT[:, 2 * t:2 * t + 2, :], two(2 * (c % 2), t), ACT.Silu)
                last.then_inc(chunk_evicted[c % 2], 1)
            rounds(0)
            with nc.scalar.Fori(1, pr.rounds) as i:
                rounds(i)

        def ffn_vector():
            pr = prod_ffn
            v = nc.vector

            def rounds(i):
                c = pr.chunk0
                v.wait_ge(chunk_evicted[c % 2], i + c // 2 + 1)
                c += 1
                v.wait_ge(chunk_done[c % 2], i + c // 2 + 1)
                for t in range(2):
                    last = v.tensor_tensor(actT[:, piece(i, 4, 2 * t, 2), :], two(2 * (c % 2), t),
                                           gateT[:, 2 * t:2 * t + 2, :], ALU.mult)
                last.then_inc(chunk_evicted[c % 2], 1)
                v.wait_ge(chunk_evicted[c % 2], i + c // 2 + 1)
                v.sem_inc(ffn_prod, 1)
            rounds(0)
            with v.Fori(1, pr.rounds) as i:
                rounds(i)

        def add_residual(prod, signal):
            per = len(prod.chunks)

            def body(i, n, b):
                for t in range(NT):
                    x = X[:, t, piece(i, per * W, n * W, W)]
                    last = nc.vector.tensor_tensor(x, ps[:, b + t, :], x, ALU.add)
                return last
            prod.evict(nc.vector, range(per), body)
            prod.wait_evicted(nc.vector)
            nc.vector.sem_inc(signal, 1)

        res_ready = [sem("residual_ready_0"), sem("residual_ready_1")]

        def post_vector(post, n):
            v = nc.vector
            post.vector()
            v.wait_ge(scaled, post.nth)
            v.wait_ge(s_row[n], 16)
            for t in range(NT):
                V(v.scalar_tensor_tensor(out=y_tok[:, t, :], in0=y_tok[:, t, :], scalar=stat_x[:, t:t + 1], in1=gain_row,
                                         op0=ALU.mult, op1=ALU.mult))
                V(v.tensor_tensor(X[:, t, :], X[:, t, :], y_tok[:, t, :], ALU.add))
            v.sem_inc(res_ready[n], 1)

        for stage in (norm0, turn0, turn_low, turn_qk, turn_go, post0, norm1, turn1, norm_q, norm_kv, turn_cq, turn_ckv,
                      q_turned, qr_turned, k_turned, turn_mo, post1, norm2, turn2, turn_n, turn_cp, turn_no,
                      turn_do[0], turn_do[1], turn_mix, norm3, turn3, postf):
            stage.place()

        block = ctx.enter_context(nc.Block())

        @block.sync
        def _(sp):
            sp.dma_start(X[:, :, :], A["x"].rearrange("(t p) d -> p t d", p=P)).then_inc(s_x, 16)
            for p in (prod_gla, prod_gla_low, prod_gla_out, prod_mla, prod_mla_tail, prod_q, prod_kv, prod_mla_out,
                      prod_n, prod_ng, prod_z, prod_ab, prod_dn, prod_cmp, prod_merge, prod_o, prod_ffn, prod_down):
                p.load(sp)
            sp.wait_ge(out_ready, 1)
            sp.dma_start(A["out"].rearrange("(t p) d -> p t d", p=P), y_tok).then_inc(out_landed, 16)
            sp.wait_ge(out_landed, 16)

        @block.gpsimd
        def _(pool):
            pool.dma_start(const[:, :], A["const"]).then_inc(s_const, 16)
            pool.dma_start(pos_i[:, :], A["positions"]).then_inc(s_pos, 16)
            pool.dma_start(gk2[:, :], A["gk2"]).then_inc(s_const, 16)
            pool.dma_start(w2k[:, :], A["w2k"]).then_inc(s_const, 16)
            pool.dma_start(w2v[:, :], A["w2v"]).then_inc(s_const, 16)
            for name, buf in small.items():
                src = A["small"][name]
                pool.dma_start(buf[:, :], src).then_inc(s_const, 16)

        @block.scalar
        def _(act):
            act.wait_ge(s_x, 16)
            act.wait_ge(s_const, 16 * n_const)
            norm0.scalar()
            turn0.scalar()
            evict_wide(prod_gla, g_proj, 0)
            prod_gla_low.evict(act, [0], lambda i, n, b: [
                act.copy(g_proj[:, t, G_LOW:G_LOW + GLA_RANK], ps[:, b + t, 0:GLA_RANK]) for t in range(NT)][-1])
            gla_scalar()
            act.dma_start(gain_row, A["l0_post"].to_broadcast([P, D])).then_inc(s_row[0], 16)
            evict_wide(prod_gla_out, y_tok, 0)
            prod_gla_out.wait_evicted(act)
            post0.scalar()
            act.wait_ge(res_ready[0], 1)
            norm1.scalar()
            turn1.scalar()
            mla_tables_scalar()
            evict_wide(prod_mla, m_proj, 0)
            prod_mla_tail.evict(act, [0], lambda i, n, b: [
                act.copy(m_proj[:, t, 3072:3136], ps[:, b + t, 0:64]) for t in range(NT)][-1])
            prod_mla_tail.wait_evicted(act)
            norm_q.scalar()
            norm_kv.scalar()
            turn_cq.scalar()
            turn_ckv.scalar()
            for t in range(NT):
                Sc(act.activation(m_proj[:, t, M_G:M_G + D], m_proj[:, t, M_G:M_G + D], ACT.Silu))
            act.sem_inc(m_gate, 1)
            evict_wide(prod_q, m_q, 0)
            q_turned.scalar()
            qr_turned.scalar()
            evict_wide(prod_kv, m_kv, 0)
            k_turned.scalar()
            attend.scalar()
            turn_mo.scalar()
            act.dma_start(gain_row, A["l1_post"].to_broadcast([P, D])).then_inc(s_row[1], 16)
            evict_wide(prod_mla_out, y_tok, 0)
            prod_mla_out.wait_evicted(act)
            post1.scalar()
            act.wait_ge(res_ready[1], 1)
            norm2.scalar()
            turn2.scalar()
            evict_wide(prod_n, n_qkv, 0)

            def tail(prod, dst, n):
                prod.evict(act, [0], lambda i, m, b: [act.copy(dst[:, t, :], ps[:, b + t, 0:n]) for t in range(NT)][-1])
            tail(prod_ng, n_g, 3 * NSA_H)
            evict_wide(prod_z, z_tok, 0)
            tail(prod_ab, d_ab, 2 * DN_H)
            act.wait_ge(pad_ready, 1)

            def to_raw(i, n, b):
                for t in range(2):
                    last = act.copy(raw[:, piece(i, 8, 4 * n + 2 * t, 2), CONV_K - 1:], two(b, t))
                return last
            prod_dn.evict(act, range(2), to_raw)
            prod_dn.wait_evicted(act)
            nsa_scalar()
            dn_scalar()
            merge_scalar()
            turn_mix.scalar()
            act.wait_ge(added, 1)
            norm3.scalar()
            turn3.scalar()
            ffn_scalar()
            act.dma_start(gain_row, A["norm_f"].to_broadcast([P, D])).then_inc(s_row[2], 16)
            act.wait_ge(ffn_added, 1)
            postf.scalar()

        @block.vector
        def _(v):
            v.wait_ge(s_const, 16 * n_const)
            norm0.vector()
            turn0.vector()
            gla_vector()
            post_vector(post0, 0)
            norm1.vector()
            turn1.vector()
            mla_tables_vector()
            norm_q.vector()
            norm_kv.vector()
            turn_cq.vector()
            turn_ckv.vector()
            mla_rotate()
            q_turned.vector()
            qr_turned.vector()
            k_turned.vector()
            v.wait_ge(m_gate, 1)
            attend.vector()
            v.sem_inc(m_done, 1)
            turn_mo.vector()
            post_vector(post1, 1)
            norm2.vector()
            turn2.vector()
            V(v.memset(raw[:, :, 0:CONV_K - 1], 0.0))
            v.sem_inc(pad_ready, 1)
            nsa_vector()
            dn_vector()
            merge_vector()
            turn_mix.vector()
            add_residual(prod_o, added)
            norm3.vector()
            turn3.vector()
            ffn_vector()
            add_residual(prod_down, ffn_added)
            postf.vector()
            v.wait_ge(scaled, postf.nth)
            v.wait_ge(s_row[2], 16)
            for t in range(NT):
                V(v.scalar_tensor_tensor(out=y_tok[:, t, :], in0=X[:, t, :], scalar=stat_x[:, t:t + 1], in1=gain_row,
                                         op0=ALU.mult, op1=ALU.mult))
            v.sem_inc(out_ready, 1)

        @block.tensor
        def _(pe):
            pe.wait_ge(s_const, 16 * n_const)
            pe.wait_ge(scaled, norm0.nth)
            turn0.tensor(pe)
            turn0.wait(pe)
            prod_gla.tensor(pe)
            prod_gla_low.tensor(pe)
            gla_tensor(pe)
            pe.wait_ge(gn_out, 1)
            turn_go.tensor(pe)
            turn_go.wait(pe)
            prod_gla_out.tensor(pe)
            pe.wait_ge(scaled, norm1.nth)
            turn1.tensor(pe)
            turn1.wait(pe)
            prod_mla.tensor(pe)
            prod_mla_tail.tensor(pe)
            pe.wait_ge(scaled, norm_q.nth)
            pe.wait_ge(scaled, norm_kv.nth)
            turn_cq.tensor(pe)
            turn_cq.wait(pe)
            turn_ckv.tensor(pe)
            turn_ckv.wait(pe)
            prod_q.tensor(pe)
            pe.wait_ge(rotated, 1)
            q_turned.tensor(pe)
            q_turned.wait(pe)
            qr_turned.tensor(pe)
            qr_turned.wait(pe)
            prod_kv.tensor(pe)
            prod_kv.wait_evicted(pe)
            k_turned.tensor(pe)
            k_turned.wait(pe)
            attend.tensor(pe)
            pe.wait_ge(m_done, 1)
            turn_mo.tensor(pe)
            turn_mo.wait(pe)
            prod_mla_out.tensor(pe)
            pe.wait_ge(scaled, norm2.nth)
            turn2.tensor(pe)
            turn2.wait(pe)
            for p in (prod_n, prod_ng, prod_z, prod_ab, prod_dn):
                p.tensor(pe)
            nsa_tensor(pe)
            turn_no.wait(pe)
            dn_tensor(pe)
            prod_merge.tensor(pe)
            pe.wait_ge(merged, 1)
            turn_mix.tensor(pe)
            turn_mix.wait(pe)
            prod_o.tensor(pe)
            pe.wait_ge(scaled, norm3.nth)
            turn3.tensor(pe)
            turn3.wait(pe)
            prod_ffn.tensor(pe)
            prod_ffn.wait_evicted(pe)
            prod_down.tensor(pe)


def kernel(**inputs):
    import concourse.bacc as bacc
    from concourse.bass_utils import run_bass_kernel_spmd

    a = {k: np.asarray(v) for k, v in inputs.items()}

    def tiles(v):
        return np.ascontiguousarray(v.reshape(-1, P).T)

    def rows(v):
        return np.ascontiguousarray(np.broadcast_to(v.reshape(1, -1), (P, v.size)))

    conv = a["conv_w_2"][0, :, 0, :]
    small = {
        "l0_pre": tiles(a["l0_pre_norm"]), "l1_pre": tiles(a["l1_pre_norm"]),
        "norm1": tiles(a["norm1_w_2"][0]), "norm2": tiles(a["norm2_w_2"][0]),
        "qa": tiles(a["l1_mla_g_qa"]), "kva": tiles(a["l1_mla_g_kva"]),
        "gla_bias": rows(a["l0_gla_b_gk"]), "gla_onorm": rows(a["l0_gla_g_onorm"]),
        "dn_norm": rows(a["dn_norm_w_2"][0]), "alog": rows(a["a_log_2"][0]), "dt_bias": rows(a["dt_bias_2"][0]),
        "conv": np.ascontiguousarray(conv.reshape(CONV_K, -1, P).transpose(2, 1, 0).reshape(P, -1)),
        "cmp_pe": np.ascontiguousarray(np.concatenate([a["cmp_pe_k_2"][0].T, a["cmp_pe_v_2"][0].T], 1)),
    }
    consts = np.concatenate(list(constant_columns().values()), 1)
    arrays = {
        "x": a["x"][0], "positions": np.ascontiguousarray(a["positions"][0].reshape(NT, P).T),
        "const": consts, "gk2": a["l0_gla_w_gk2"], "w2k": a["cmp_w2_k_2"][0], "w2v": a["cmp_w2_v_2"][0],
        "l0_post": a["l0_post_norm"].reshape(1, D), "l1_post": a["l1_post_norm"].reshape(1, D),
        "norm_f": a["norm_f_w_2"].reshape(1, D),
        "w_gla_in": a["l0_gla_w_in"], "w_gla_out": a["l0_gla_w_out"], "w_mla_in": a["l1_mla_w_in"],
        "w_qb": a["l1_mla_w_qb"], "w_kvb": a["l1_mla_w_kvb"], "w_mla_out": a["l1_mla_w_out"],
        "w_in2": a["w_in_2"][0], "cmp_w1_k": a["cmp_w1_k_2"][0], "cmp_w1_v": a["cmp_w1_v_2"][0],
        "w_up_nsa": a["w_up_nsa_2"][0], "w_up_dn": a["w_up_dn_2"][0], "w_o": a["w_o_2"][0],
        "w_gate": a["w_ffn_gate_2"][0], "w_ffn_up": a["w_ffn_up_2"][0], "w_down": a["w_ffn_down_2"][0],
    }
    arrays.update({"small_" + k: v for k, v in small.items()})
    nc = bacc.Bacc("TRN2", target_bir_lowering=False, num_devices=1)
    feed, A = {}, {"small": {}}
    for name, v in arrays.items():
        v = np.ascontiguousarray(v)
        feed["in_" + name] = v
        ap = nc.dram_tensor("in_" + name, v.shape, mybir.dt.from_np(v.dtype), kind="ExternalInput").ap()
        if name.startswith("small_"):
            A["small"][name[6:]] = ap
        else:
            A[name] = ap
    A["cmp_w1"] = [A["cmp_w1_k"], A["cmp_w1_v"]]
    A["w_up"] = [A["w_up_nsa"], A["w_up_dn"]]
    A["out"] = nc.dram_tensor("out_y", (S, D), F32, kind="ExternalOutput").ap()
    program(nc, A)
    r = run_bass_kernel_spmd(nc, [feed], core_ids=[0])
    return r.results[0]["out_y"].reshape(1, S, D)
```

```python
from contextlib import ExitStack

import numpy as np
import concourse.bass as bass
from concourse import mybir
from concourse.alu_op_type import AluOpType as ALU

F32 = mybir.dt.float32
F32R = mybir.dt.float32r
I32 = mybir.dt.int32
ACT = mybir.ActivationFunctionType
AX = mybir.AxisListType.X
ds = bass.ds

P = 128
S = 256
NT = S // P
D = 2048
KD = D // P
EPS = 1e-6
CHUNK = 64
NCH = S // CHUNK
SLOTS = 4
SLOT_K = 2
PARTS = 4
W = 512
HIDDEN = -1e30

GLA_H, GLA_DK, GLA_DV, GLA_RANK, GLA_TAU = 4, 256, 512, 16, 16.0
GLA_QK, GLA_V = GLA_H * GLA_DK, GLA_H * GLA_DV

MLA_H, MLA_RANK, NOPE, ROPE = 16, 512, 128, 64
MLA_SCALE = float(NOPE + ROPE) ** -0.5
LATENT = 2 * MLA_RANK + ROPE

HD = 128
NSA_H, NSA_KV, NSA_G = 8, 2, 4
NSA_SCALE = float(HD) ** -0.5
CMP_BLOCK, CMP_STRIDE = 32, 16
NCMP = (S - CMP_BLOCK) // CMP_STRIDE + 1
CPAD = NCMP + 1
DN_H = 8
CONV_K = 4
D_FF = 5632
GELU_C, GELU_A = float(np.sqrt(2 / np.pi)), 0.044715


def constant_columns():
    i = np.arange(P)
    same = (i[:, None] // CHUNK) == (i[None, :] // CHUNK)
    upto = same & (i[:, None] <= i[None, :])
    after = same & (i[:, None] > i[None, :])
    out = {"ident": np.eye(P), "upto": upto, "after": after, "ones": np.ones((P, P)),
           "half": (i[:, None] // CHUNK) == np.arange(2)[None, :]}
    levels = []
    for n in range(6):
        b = 1 << n
        levels.append(((i[:, None] // (2 * b)) == (i[None, :] // (2 * b)))
                      & ((i[:, None] // b) % 2 == 0) & ((i[None, :] // b) % 2 == 1))
    out["levels"] = np.concatenate(levels, 1)
    causal = np.where(i[None, :] <= i[:, None], 0.0, HIDDEN)
    out["causal"] = np.concatenate([causal, np.zeros((P, P)), causal], 1)
    tok = (np.arange(NT)[None, :, None] * P + i[:, None, None])
    ends = np.arange(CPAD) * CMP_STRIDE + CMP_BLOCK - 1
    seen = (ends[None, None, :] <= tok) & (np.arange(CPAD) < NCMP)[None, None, :]
    out["cmp_mask"] = np.where(seen, 0.0, HIDDEN).reshape(P, NT * CPAD)
    out["cmp_any"] = seen.any(-1)
    out["cmp_head"] = (i[:, None] // CPAD) == np.arange(NSA_H)[None, :]
    inv = (1.0 / (np.float32(10000.0) ** (np.arange(0, HD, 2, dtype=np.float32) / np.float32(HD)))).astype(np.float32)
    ang = tok.astype(np.float32) * inv[None, None, :]
    out["cos2"] = np.cos(ang).reshape(P, -1)
    out["sin2"] = np.sin(ang).reshape(P, -1)
    inv1 = (np.float32(10000.0) ** (-np.arange(0, ROPE, 2, dtype=np.float32) / np.float32(ROPE))).astype(np.float32)
    out["inv_freq"] = np.broadcast_to(inv1[None, :], (P, ROPE // 2))
    return {k: np.ascontiguousarray(v, dtype=np.float32) for k, v in out.items()}


def program(nc, A):
    with ExitStack() as ctx:
        def sb(name, shape, dt=F32):
            return ctx.enter_context(nc.sbuf_tensor(name, shape, dt))

        def sem(name):
            return ctx.enter_context(nc.semaphore(name))

        X = sb("residual", [P, NT, D])
        with nc.sbuf_tensor("hidden_T_high", [P, KD, S], F32R) as high, \
                nc.sbuf_tensor("hidden_T_low", [P, KD, S], F32R) as low:
            HT = (high, low)
        spare = sb("spare", [P, 2 * KD * S])
        ring = sb("weight_ring", [P, SLOTS, SLOT_K, W])
        w_high = sb("weights_high", [P, PARTS, W], F32R)
        w_low = sb("weights_low", [P, PARTS, W], F32R)
        NF = D_FF // P
        with nc.sbuf_tensor("ffn_high", [P, NF, S], F32R) as act_high, \
                nc.sbuf_tensor("ffn_low", [P, NF, S], F32R) as act_low:
            pass
        proj = sb("projections", [P, 13600])
        scr = sb("scratch", [P, 9216])
        gate_stage = sb("gate_stage", [P, 2, NT, W])
        extra = sb("extra", [P, 4096])
        gates_dram = nc.dram_tensor("merge_gates", (P, 2 * D // W, NT * W), F32, kind="Internal").ap()
        ps = ctx.enter_context(nc.psum_tensor("banks", [P, 8, 512], F32))
        cols, offset = {}, 0
        for name, a in constant_columns().items():
            cols[name] = (offset, a.shape[1])
            offset += a.shape[1]
        const = sb("constants", [P, offset])

        def C(name):
            o, n = cols[name]
            return const[:, o:o + n]

        small = {}
        for name in A["small"]:
            if name == "gla_bias":
                small[name] = extra[:, 2048:2048 + GLA_QK]
            elif name == "gla_onorm":
                small[name] = extra[:, 3072:3072 + GLA_DV]
            else:
                small[name] = sb("c_" + name, list(A["small"][name].shape))
        pos_i = sb("positions_i", [P, NT], I32)
        gk2 = proj[0:GLA_RANK, 12416:12416 + GLA_QK]
        w2k = sb("cmp_w2_k", [P, HD])
        w2v = sb("cmp_w2_v", [P, HD])
        stat = sb("statistics", [P, 64])
        tab = sb("mla_rope_tables", [P, 2, NT, ROPE // 2])
        ident, upto, after, ones = C("ident"), C("upto"), C("after"), C("ones")

        v_step, a_step = sem("vector_step"), sem("scalar_step")
        steps = {"v": 0, "a": 0}

        def V(ins):
            steps["v"] += 1
            ins.then_inc(v_step, 1)
            nc.vector.wait_ge(v_step, steps["v"])

        def Sc(ins):
            steps["a"] += 1
            ins.then_inc(a_step, 1)
            nc.scalar.wait_ge(a_step, steps["a"])

        landed = [sem(f"weights_landed_{n}") for n in range(SLOTS)]
        high_ready, low_ready, split_used = sem("weights_high_ready"), sem("weights_low_ready"), sem("split_weights_used")
        native_used = sem("native_weights_used")
        native_done = sem("native_chunk_done")
        chunk_evicted = [sem("chunk_evicted_even"), sem("chunk_evicted_odd")]
        planned = {"use": 0, "chunk": 0, "tile": 0, "native": 0, "native_chunk": 0,
                   "turned": 0, "copied_v": 0, "copied_s": 0, "halved": 0, "norm": 0}
        freed = []

        class Product:

            def __init__(self, chunks, rounds=1, native=False):
                self.chunks, self.rounds, self.native = chunks, rounds, native
                self.use0, self.chunk0, self.tile0 = planned["use"], planned["chunk"], planned["tile"]
                self.uses = sum(c[1] // SLOT_K for c in chunks)
                self.tiles = 0 if native else self.uses * SLOT_K
                self.native0, self.nchunk0 = planned["native"], planned["native_chunk"]
                planned["use"] += self.uses * rounds
                planned["chunk"] += len(chunks) * rounds
                planned["tile"] += self.tiles * rounds
                if native:
                    planned["native"] += self.uses
                    planned["native_chunk"] += len(chunks)
                for n in range(self.uses * rounds):
                    freed.append((native_used, self.native0 + n + 1) if native
                                 else (low_ready, self.tile0 + (n + 1) * SLOT_K))
                assert rounds == 1 or (self.uses % SLOTS == 0 and len(chunks) % 2 == 0 and not native)

            def over(self, eng, body, peel_last=False):
                body(0)
                end = self.rounds - (1 if peel_last else 0)
                if end > 2:
                    with eng.Fori(1, end) as i:
                        body(i)
                elif end == 2:
                    body(1)
                if peel_last and self.rounds > 1:
                    body(self.rounds - 1)

            def load(self, sp):
                def body(i):
                    u = self.use0
                    for w, kt, col0, step, width, _, _ in self.chunks:
                        for k in range(0, kt, SLOT_K):
                            if not isinstance(i, int):
                                sp.wait_ge(low_ready, i * self.tiles + self.tile0 + (u - self.use0 - SLOTS + 1) * SLOT_K)
                            elif u + i * self.uses >= SLOTS:
                                sp.wait_ge(*freed[u + i * self.uses - SLOTS])
                            if isinstance(i, int):
                                at = slice(col0 + i * step, col0 + i * step + width)
                            else:
                                at = ds(i * step + col0, width)
                            if callable(w):
                                dst, src = w(ring[:, u % SLOTS, :, :], k)
                            else:
                                dst = ring[:, u % SLOTS, :, 0:width]
                                src = w[k * P:(k + SLOT_K) * P, at].rearrange("(k p) n -> p k n", p=P)
                            sp.dma_start(dst, src).then_inc(landed[u % SLOTS], 16)
                            u += 1
                self.over(sp, body)

            def place_of(self, n, k):
                before = sum(c[1] for c in self.chunks[:n]) + k
                return self.use0 + before // SLOT_K, self.tile0 + before

            def split(self, eng, i, n, k):
                u, q = self.place_of(n, k)
                width = self.chunks[n][4]
                raw = ring[:, u % SLOTS, k % SLOT_K, 0:width]
                hi, lo = w_high[:, q % PARTS, 0:width], w_low[:, q % PARTS, 0:width]
                if eng is nc.scalar:
                    if k % SLOT_K == 0:
                        eng.wait_ge(landed[u % SLOTS], i * (16 * self.uses // SLOTS) + 16 * (u // SLOTS + 1))
                    if not (isinstance(i, int) and q + i * self.tiles < PARTS):
                        eng.wait_ge(split_used, i * self.tiles + (q - PARTS + 1))
                    nc.scalar.copy(hi, raw).then_inc(high_ready, 1)
                else:
                    eng.wait_ge(high_ready, i * self.tiles + q + 1)
                    nc.vector.tensor_tensor(lo, raw, hi.bitcast(F32), ALU.subtract).then_inc(low_ready, 1)

            def prime(self, eng):
                for k in range(PARTS):
                    self.split(eng, 0, 0, k)

            def tensor(self, pe):
                def body(i):
                    c = self.chunk0
                    for n, (w, kt, _, _, width, acts, turned) in enumerate(self.chunks):
                        if not (isinstance(i, int) and c + i * len(self.chunks) < 2):
                            pe.wait_ge(chunk_evicted[c % 2], i * (len(self.chunks) // 2) + c // 2)
                        b = 2 * (c % 2)
                        if self.native:
                            for k0 in range(0, kt, SLOT_K):
                                u, _ = self.place_of(n, k0)
                                pe.wait_ge(landed[u % SLOTS], 16 * (u // SLOTS + 1))
                                acts(ring[:, u % SLOTS, :, :], k0, b).then_inc(native_used, 1)
                            c += 1
                            continue
                        for k in range(kt):
                            _, q = self.place_of(n, k)
                            pe.wait_ge(low_ready, i * self.tiles + q + 1)
                            hi, lo = w_high[:, q % PARTS, 0:width], w_low[:, q % PARTS, 0:width]
                            ahi, alo = acts(k)
                            if turned:
                                for f in range(W // P):
                                    out = ps[:, b + f // 2, (f % 2) * S:(f % 2) * S + S]
                                    fs = slice(f * P, (f + 1) * P)
                                    pe.matmul(out, hi[:, fs], ahi, start=(k == 0 and f % 2 == 0), stop=False,
                                              skip_group_check=True)
                                    pe.matmul(out, hi[:, fs], alo, start=False, stop=False, skip_group_check=True)
                                    last = pe.matmul(out, lo[:, fs], ahi, start=False, stop=(k == kt - 1),
                                                     skip_group_check=True)
                            else:
                                for t in range(NT):
                                    ts_ = slice(t * P, (t + 1) * P)
                                    out = ps[:, b + t, 0:width]
                                    pe.matmul(out, ahi[:, ts_], hi, start=(k == 0), stop=False)
                                    pe.matmul(out, ahi[:, ts_], lo, start=False, stop=False)
                                    last = pe.matmul(out, alo[:, ts_], hi, start=False, stop=(k == kt - 1))
                            last.then_inc(split_used, 1)
                        c += 1
                self.over(pe, body)

            def wait_done(self, eng, i, n):
                if self.native:
                    eng.wait_ge(native_used, self.native0 + sum(c[1] for c in self.chunks[:n + 1]) // SLOT_K)
                else:
                    _, q = self.place_of(n, self.chunks[n][1])
                    eng.wait_ge(split_used, i * self.tiles + q)

            def wait_evicted(self, eng):
                end = self.chunk0 + len(self.chunks) * self.rounds
                eng.wait_ge(chunk_evicted[0], (end + 1) // 2)
                if end > 1:
                    eng.wait_ge(chunk_evicted[1], end // 2)

            def run(self, eng, which=(), body_of=None, after=None):
                def body(i):
                    final = isinstance(i, int) and i == self.rounds - 1
                    for n, chunk in enumerate(self.chunks):
                        if not self.native:
                            for k in range(PARTS, chunk[1]):
                                self.split(eng, i, n, k)
                            if n + 1 < len(self.chunks):
                                for k in range(PARTS):
                                    self.split(eng, i, n + 1, k)
                            elif not final:
                                for k in range(PARTS):
                                    self.split(eng, i + 1, 0, k)
                            elif after is not None:
                                after.prime(eng)
                        if n in which:
                            self.wait_done(eng, i, n)
                            c = self.chunk0 + n
                            last = body_of(i, n, 2 * (c % 2))
                            if last is not None:
                                last.then_inc(chunk_evicted[c % 2], 1)
                self.over(eng, body, peel_last=True)

        def piece(i, step, off, n):
            return slice(off + i * step, off + i * step + n) if isinstance(i, int) else ds(i * step + off, n)

        def hidden(k):
            return HT[0][:, k, :], HT[1][:, k, :]

        def wide(weights, kt, n, col0, acts):
            per = 4 if kt == 4 else 2
            return Product([(weights, kt, col0 + m * W, per * W, W, acts, False) for m in range(per)], n // per)

        def evict_wide(prod, dst, off, after=None):
            per = len(prod.chunks)

            def body(i, n, b):
                for t in range(NT):
                    last = nc.scalar.copy(dst[:, t, piece(i, per * W, off + n * W, W)], ps[:, b + t, :])
                return last
            prod.run(nc.scalar, range(per), body, after)

        def evict_tail(prod, dst, off, n, after=None):
            def body(i, m, b):
                for t in range(NT):
                    last = nc.scalar.copy(dst[:, t, off:off + n], ps[:, b + t, 0:n])
                return last
            prod.run(nc.scalar, [0], body, after)

        turned = sem("group_turned")
        copied_out = [sem("turned_copied_by_vector"), sem("turned_copied_by_scalar")]
        squares, inverse, scaled = sem("norm_squares"), sem("norm_inverse"), sem("norm_scaled")

        class Turn:

            def __init__(self, name, groups):
                self.groups = groups

            def place(self):
                self.turned0, self.out0 = planned["turned"], [planned["copied_v"], planned["copied_s"]]
                n = len(self.groups)
                planned["turned"] += n
                planned["copied_v"] += (n + 1) // 2
                planned["copied_s"] += n // 2

            def tensor(self, pe):
                for g, (tiles, _) in enumerate(self.groups):
                    if g >= 4:
                        pe.wait_ge(copied_out[g % 2], self.out0[g % 2] + (g - 4) // 2 + 1)
                    for src, col in tiles:
                        rows, width = src.shape[0], src.shape[1]
                        last = pe.transpose(ps[0:width, 4 + g % 4, col:col + rows], src, ident[0:rows, 0:rows])
                    last.then_inc(turned, 1)

            def copies(self, eng, which):
                for g, (_, copies) in enumerate(self.groups):
                    if g % 2 != which:
                        continue
                    eng.wait_ge(turned, self.turned0 + g + 1)
                    for dst, src, scale in copies:
                        if which == 0:
                            last = nc.vector.tensor_copy(dst, src(4 + g % 4)) if scale is None else \
                                nc.vector.tensor_scalar(dst, src(4 + g % 4), scale, None, ALU.mult)
                        else:
                            last = nc.scalar.copy(dst, src(4 + g % 4)) if scale is None else \
                                nc.scalar.activation(dst, src(4 + g % 4), ACT.Copy, scale=scale)
                    last.then_inc(copied_out[which], 1)

            def vector(self):
                self.copies(nc.vector, 0)

            def scalar(self):
                self.copies(nc.scalar, 1)

            def wait(self, eng):
                eng.wait_ge(copied_out[0], self.out0[0] + (len(self.groups) + 1) // 2)
                if len(self.groups) > 1:
                    eng.wait_ge(copied_out[1], self.out0[1] + len(self.groups) // 2)

        def whole(rows, a, n):
            return lambda b: ps[0:rows, b, a:a + n]

        def turn_tokens(name, src, n_tiles, dst, gain=None):
            groups = []
            for k in range(0, n_tiles, 2):
                tiles = [(src(t, k + kk), kk * S + t * P) for kk in range(2) for t in range(NT)]
                copies = [(dst(k + kk), whole(P, kk * S, S), None if gain is None else gain(k + kk))
                          for kk in range(2)]
                groups.append((tiles, copies))
            return Turn(name, groups)

        high_out, low_out = sem("activations_high_ready"), sem("activations_low_ready")

        class Halve:

            def __init__(self, src, n_tiles, dst, gain=None):
                self.src, self.n, self.dst, self.gain = src, n_tiles // 2, dst, gain

            def place(self):
                self.turned0, self.first = planned["turned"], planned["halved"]
                planned["turned"] += self.n
                planned["halved"] += self.n

            def tensor(self, pe):
                for g in range(self.n):
                    if g >= 4:
                        pe.wait_ge(low_out, self.first + g - 3)
                    for kk in range(2):
                        for t in range(NT):
                            o = kk * S + t * P
                            last = pe.transpose(ps[:, 4 + g % 4, o:o + P], self.src(t, 2 * g + kk), ident)
                    last.then_inc(turned, 1)

            def scalar(self):
                for g in range(self.n):
                    nc.scalar.wait_ge(turned, self.turned0 + g + 1)
                    for kk in range(2):
                        k = 2 * g + kk
                        x = ps[:, 4 + g % 4, kk * S:(kk + 1) * S]
                        last = nc.scalar.copy(self.dst(k)[0], x) if self.gain is None else \
                            nc.scalar.activation(self.dst(k)[0], x, ACT.Copy, scale=self.gain(k))
                    last.then_inc(high_out, 1)

            def vector(self):
                for g in range(self.n):
                    nc.vector.wait_ge(high_out, self.first + g + 1)
                    for kk in range(2):
                        k = 2 * g + kk
                        x = ps[:, 4 + g % 4, kk * S:(kk + 1) * S]
                        hi, lo = self.dst(k)
                        last = nc.vector.tensor_tensor(lo, x, hi.bitcast(F32), ALU.subtract) if self.gain is None else \
                            nc.vector.scalar_tensor_tensor(out=lo, in0=x, scalar=self.gain(k), in1=hi.bitcast(F32),
                                                           op0=ALU.mult, op1=ALU.subtract)
                    last.then_inc(low_out, 1)

            def wait(self, eng):
                eng.wait_ge(low_out, self.first + self.n)

        class Norm:

            def __init__(self, name, src, n, rstd, junk, dst=None):
                self.src, self.n, self.rstd, self.junk, self.dst = src, n, rstd, junk, dst

            def place(self):
                planned["norm"] += 1
                self.nth = planned["norm"]

            def scalar(self):
                for t in range(NT):
                    Sc(nc.scalar.activation(self.junk, self.src(t), ACT.Square, accum_out=self.rstd[:, t:t + 1]))
                nc.scalar.sem_inc(squares, 1)
                nc.scalar.wait_ge(inverse, self.nth)
                Sc(nc.scalar.activation(self.rstd, self.rstd, ACT.Sqrt))
                if self.dst is not None:
                    for t in range(NT):
                        Sc(nc.scalar.activation(self.dst(t), self.src(t), ACT.Copy, scale=self.rstd[:, t:t + 1]))
                nc.scalar.sem_inc(scaled, 1)

            def vector(self):
                nc.vector.wait_ge(squares, self.nth)
                V(nc.vector.tensor_scalar(self.rstd, self.rstd, 1.0 / self.n, EPS, ALU.mult, ALU.add))
                V(nc.vector.reciprocal(self.rstd, self.rstd))
                nc.vector.sem_inc(inverse, 1)

        def view(buf, off, *dims):
            n = int(np.prod(dims))
            v = buf[:, off:off + n]
            if len(dims) == 2:
                return v.rearrange("p (a b) -> p a b", a=dims[0])
            if len(dims) == 3:
                return v.rearrange("p (a b c) -> p a b c", a=dims[0], b=dims[1])
            if len(dims) == 4:
                return v.rearrange("p (a b c d) -> p a b c d", a=dims[0], b=dims[1], c=dims[2])
            return v

        def junk_q():
            return extra[:, 2304:2304 + MLA_RANK]

        class Attention:

            def __init__(self, name, heads, parts, value, scale, buf, finish):
                self.h, self.parts, self.value, self.scale, self.finish = heads, parts, value, scale, finish
                self.s = view(buf, 0, 2, 3 * P)
                self.p = view(buf, 6 * P, 2, 3 * P)
                self.pt = view(buf, 12 * P, 2, 3 * P)
                self.st = view(buf, 18 * P, 2, 2, 2)
                self.sum = view(buf, 18 * P + 8, 2, 2)
                names = ("_scores", "_masked", "_probs", "_turned", "_turned_copied", "_mixed", "_finished")
                (self.scored, self.masked, self.probs, self.turned, self.copied, self.mixed,
                 self.finished) = (sem(name + n) for n in names)
                self.span = [(0, P), (P, 3 * P)]

            def tensor(self, pe):
                def score(h):
                    if h >= 2:
                        pe.wait_ge(self.masked, h - 1)
                    for t in range(NT):
                        a, b = self.span[t]
                        parts = self.parts(h, t)
                        for n, (q, k) in enumerate(parts):
                            last = pe.matmul(ps[:, 4 + h % 2, a:b], q, k, start=(n == 0), stop=(n == len(parts) - 1))
                    last.then_inc(self.scored, 1)
                score(0)
                for h in range(self.h):
                    if h + 1 < self.h:
                        score(h + 1)
                    pe.wait_ge(self.probs, h + 1)
                    if h >= 1:
                        pe.wait_ge(self.copied, h)
                    for n in range(3):
                        last = pe.transpose(ps[:, 6, n * P:(n + 1) * P], self.p[:, h % 2, n * P:(n + 1) * P], ident)
                    last.then_inc(self.turned, 1)
                    pe.wait_ge(self.copied, h + 1)
                    if h >= 1:
                        pe.wait_ge(self.finished, h)
                    pt = self.pt[:, h % 2, :]
                    pe.matmul(ps[:, 7, 0:P], pt[:, 0:P], self.value(h, 0), start=True, stop=True)
                    pe.matmul(ps[:, 7, P:2 * P], pt[:, P:2 * P], self.value(h, 0), start=True, stop=False)
                    pe.matmul(ps[:, 7, P:2 * P], pt[:, 2 * P:3 * P], self.value(h, 1), start=False, stop=True)\
                        .then_inc(self.mixed, 1)

            def vector(self):
                def mask(h):
                    nc.vector.wait_ge(self.scored, h + 1)
                    if h >= 2:
                        nc.vector.wait_ge(self.probs, h - 1)
                    V(nc.vector.scalar_tensor_tensor(out=self.s[:, h % 2, :], in0=ps[:, 4 + h % 2, 0:3 * P],
                                                     scalar=self.scale, in1=C("causal"), op0=ALU.mult, op1=ALU.add))
                    for t in range(NT):
                        a, b = self.span[t]
                        ins = nc.vector.tensor_reduce(self.st[:, h % 2, 0, t:t + 1], self.s[:, h % 2, a:b], AX, ALU.max)
                        V(ins)
                    V(nc.vector.tensor_scalar(self.st[:, h % 2, 1, :], self.st[:, h % 2, 0, :], -1.0, None, ALU.mult))
                    nc.vector.sem_inc(self.masked, 1)
                mask(0)
                for h in range(self.h):
                    if h + 1 < self.h:
                        mask(h + 1)
                    nc.vector.wait_ge(self.mixed, h + 1)
                    V(nc.vector.reciprocal(self.sum[:, h % 2, :], self.sum[:, h % 2, :]))
                    self.finish(h, 7, self.sum[:, h % 2, :])
                    nc.vector.sem_inc(self.finished, 1)

            def scalar(self):
                for h in range(self.h):
                    nc.scalar.wait_ge(self.masked, h + 1)
                    if h >= 2:
                        nc.scalar.wait_ge(self.turned, h - 1)
                        nc.scalar.wait_ge(self.finished, h - 1)
                    for t in range(NT):
                        a, b = self.span[t]
                        Sc(nc.scalar.activation(self.p[:, h % 2, a:b], self.s[:, h % 2, a:b], ACT.Exp,
                                                bias=self.st[:, h % 2, 1, t:t + 1],
                                                accum_out=self.sum[:, h % 2, t:t + 1]))
                    nc.scalar.sem_inc(self.probs, 1)
                    nc.scalar.wait_ge(self.turned, h + 1)
                    if h >= 2:
                        nc.scalar.wait_ge(self.mixed, h - 1)
                    nc.scalar.copy(self.pt[:, h % 2, :], ps[:, 6, 0:3 * P]).then_inc(self.copied, 1)

        s_x, s_const, s_pos = sem("x_landed"), sem("constants_landed"), sem("positions_landed")
        s_row = [sem("gain_row_landed_0"), sem("gain_row_landed_1"), sem("gain_row_landed_2")]
        row_free = [sem("gain_row_free_1"), sem("gain_row_free_2")]
        out_landed = sem("output_landed")
        out_ready = sem("output_ready")
        n_const = 4 + len(small)

        g_proj = view(proj, 0, NT, 6160)
        G_K, G_V, G_G, G_LOW = GLA_QK, 2 * GLA_QK, 2 * GLA_QK + GLA_V, 2 * GLA_QK + 2 * GLA_V
        y_tok = view(scr, 0, NT, D)
        gain_row = scr[:, 2 * D:3 * D]
        normed = view(proj, 0, NT, D)
        junk = proj[:, 2 * D:3 * D]

        stat_x = stat[:, 0:2]
        stat_q, stat_kv = stat[:, 2:4], stat[:, 4:6]

        def x_norm(name, gain):
            n = Norm(name, lambda t: X[:, t, :], D, stat_x, junk, lambda t: normed[:, t, :])
            tr = Halve(lambda t, k: normed[:, t, k * P:(k + 1) * P], KD, hidden, lambda k: small[gain][:, k:k + 1])
            return n, tr

        norm0, turn0 = x_norm("norm0", "l0_pre")
        norm1, turn1 = x_norm("norm1", "l1_pre")
        norm2, turn2 = x_norm("norm2", "norm1")
        norm3, turn3 = x_norm("norm3", "norm2")
        post0 = Norm("post0", lambda t: y_tok[:, t, :], D, stat_x, junk)
        post1 = Norm("post1", lambda t: y_tok[:, t, :], D, stat_x, junk)
        postf = Norm("postf", lambda t: X[:, t, :], D, stat_x, junk)

        la = view(scr, 0, NT, GLA_QK)
        tmp_a = view(scr, 2048, NT, GLA_QK)
        kl = view(scr, 2048, NT, GLA_QK)
        qeT = view(scr, 4096, 8, NT, 2, P)
        keT = view(extra, 0, 8, S)
        gst = view(spare, 0, GLA_H, 2, GLA_DV)
        gst2 = view(spare, 4096, GLA_H, 2, GLA_DV)

        def gst_in(ch):
            return gst if ch % 2 else gst2

        g_o = view(proj, 0, NT, 6160)[:, :, 0:D]
        lowT = scr[:, 8192:8192 + S]
        dlT = view(scr, 8448, 8, NCH)
        gAT = view(scr, 8512, 2, P)
        gst_r = stat[:, 8:16]

        prod_gla = wide(A["w_gla_in"], KD, 12, 0, hidden)
        prod_gla_low = Product([(A["w_gla_in"], KD, G_LOW, 0, GLA_RANK, hidden, False)])
        turn_low = Turn("gla_low", [([(g_proj[:, t, G_LOW:G_LOW + GLA_RANK], t * P) for t in range(NT)],
                                     [(lowT[0:GLA_RANK, :], whole(GLA_RANK, 0, S), None)])])
        gk_done, gk_used = sem("gla_gate_done"), sem("gla_gate_used")
        gk_exp, gk_dec = sem("gla_gate_exp"), sem("gla_decay_ready")
        gk_abs = sem("gla_gate_abs")
        cum_done, cum_exp, cum_free = sem("gla_cumulated"), sem("gla_cumulated_exp"), sem("gla_cumulated_used")
        groups = []
        for k in range(8):
            tiles = [(g_proj[:, t, k * P:(k + 1) * P], t * P) for t in range(NT)]
            copies = [(qeT[:, k, t, par, par * CHUNK:(par + 1) * CHUNK],
                       whole(P, t * P + par * CHUNK, CHUNK), None) for t in range(NT) for par in range(2)]
            groups.append((tiles, copies))
        for k in range(8):
            tiles = [(g_proj[:, t, G_K + k * P:G_K + (k + 1) * P], t * P) for t in range(NT)]
            groups.append((tiles, [(keT[:, k, :], whole(P, 0, S), None)]))
        turn_qk = Turn("gla_qk", groups)
        qk_ready = sem("gla_scaled_ready")
        zeroed = sem("gla_zeroed")
        dl_done, dl_ready = sem("gla_chunk_decay_done"), sem("gla_chunk_decay_ready")
        ga_done, ga_masked = sem("gla_scores"), sem("gla_scores_masked")
        go_done, go_out = sem("gla_output_done"), sem("gla_output_evicted")
        gs_done, gs_out = sem("gla_update_done"), sem("gla_state_ready")
        gate_act = sem("gla_gate_activated")
        gn_sq, gn_inv, gn_rs, gn_out = sem("gla_norm_squares"), sem("gla_norm_inverse"), sem("gla_norm_ready"), sem("gla_gated")
        turn_go = Halve(lambda t, k: g_o[:, t, k * P:(k + 1) * P], KD, hidden)
        prod_gla_out = wide(A["w_gla_out"], KD, 4, 0, hidden)

        def gla_tensor(pe):
            prod_gla_low.wait_evicted(pe)
            turn_low.tensor(pe)
            turn_low.wait(pe)
            for t in range(NT):
                for n in range(2):
                    last = pe.matmul(ps[:, 2 * t + n, :], lowT[0:GLA_RANK, t * P:(t + 1) * P],
                                     gk2[:, n * W:(n + 1) * W], start=True, stop=True)
            last.then_inc(gk_done, 1)
            pe.wait_ge(gk_dec, 1)
            for t in range(NT):
                for n in range(2):
                    pe.matmul(ps[:, 2 * t + n, :], upto, la[:, t, n * W:(n + 1) * W], start=True, stop=True)
                    last = pe.matmul(ps[:, 4 + 2 * t + n, :], after, la[:, t, n * W:(n + 1) * W], start=True, stop=True)
            last.then_inc(cum_done, 1)
            pe.wait_ge(cum_free, 2)
            for k in range(8):
                for t in range(NT):
                    last = pe.matmul(ps[:, 0, k * NCH + 2 * t:k * NCH + 2 * t + 2], la[:, t, k * P:(k + 1) * P],
                                     C("half"), start=True, stop=True)
            last.then_inc(dl_done, 1)
            pe.wait_ge(qk_ready, 1)
            pe.wait_ge(zeroed, 1)
            turn_qk.tensor(pe)
            turn_qk.wait(pe)
            pe.wait_ge(dl_ready, 1)
            n = 0
            m = 0
            for t in range(NT):
                for par in range(2):
                    ch = 2 * t + par
                    rows = slice(par * CHUNK, (par + 1) * CHUNK)
                    if ch < NCH - 1:
                        for h in range(GLA_H):
                            for j in range(2):
                                k = 2 * h + j
                                if m >= 2:
                                    pe.wait_ge(gs_out, m - 1)
                                pe.matmul(ps[:, 6 + m % 2, :], kl[rows, t, k * P:(k + 1) * P],
                                          g_proj[rows, t, G_V + h * GLA_DV:G_V + (h + 1) * GLA_DV],
                                          start=True, stop=True).then_inc(gs_done, 1)
                                m += 1
                    if par == 0:
                        for h in range(GLA_H):
                            a = t * GLA_H + h
                            if a >= 2:
                                pe.wait_ge(ga_masked, a - 1)
                            for j in range(2):
                                k = 2 * h + j
                                for half in range(2):
                                    hs = slice(half * CHUNK, (half + 1) * CHUNK)
                                    last = pe.matmul(ps[:, 4 + a % 2, hs], keT[:, k, t * P:(t + 1) * P],
                                                     qeT[:, k, t, half, hs], start=(j == 0 and half == 0),
                                                     stop=(j == 1), skip_group_check=True)
                            last.then_inc(ga_done, 1)
                            pe.wait_ge(ga_masked, a + 1)
                            if t == 1:
                                pe.wait_ge(go_out, h + 1)
                            pe.matmul(ps[:, h, :], gAT[:, a % 2, :],
                                      g_proj[:, t, G_V + h * GLA_DV:G_V + (h + 1) * GLA_DV], start=True, stop=False)
                    for h in range(GLA_H):
                        for j in range(2):
                            k = 2 * h + j
                            if ch > 0:
                                pe.wait_ge(gs_out, 8 * (ch - 1) + k + 1)
                                last = pe.matmul(ps[:, h, :], qeT[:, k, t, par, :], gst_in(ch)[:, h, j, :],
                                                 start=False, stop=(par == 1 and j == 1))
                        if par == 1:
                            last.then_inc(go_done, 1)


        def gla_scalar():
            turn_low.scalar()
            act = nc.scalar
            act.wait_ge(gk_abs, 1)
            Sc(act.activation(tmp_a, tmp_a, ACT.Exp, scale=-1.0))
            Sc(act.activation(tmp_a, tmp_a, ACT.Ln, bias=1.0))
            act.sem_inc(gk_exp, 1)
            act.wait_ge(cum_done, 1)
            act.wait_ge(gk_used, 1)
            for t in range(NT):
                for n in range(2):
                    e = tmp_a[:, t, n * W:(n + 1) * W]
                    Sc(act.activation(e, ps[:, 2 * t + n, :], ACT.Exp, scale=-1.0))
                    Sc(act.activation(ps[:, 2 * t + n, :], ps[:, 2 * t + n, :], ACT.Exp))
                    Sc(act.activation(ps[:, 4 + 2 * t + n, :], ps[:, 4 + 2 * t + n, :], ACT.Exp))
            act.sem_inc(cum_exp, 1)
            act.wait_ge(dl_done, 1)
            Sc(act.activation(dlT, ps[:, 0, 0:8 * NCH].rearrange("p (k c) -> p k c", k=8), ACT.Exp))
            act.sem_inc(dl_ready, 1)
            turn_qk.scalar()
            for t in range(NT):
                Sc(act.activation(g_proj[:, t, G_G:G_G + GLA_V], g_proj[:, t, G_G:G_G + GLA_V], ACT.Silu))
            act.sem_inc(gate_act, 1)
            for t in range(NT):
                for h in range(GLA_H):
                    act.wait_ge(go_done, t * GLA_H + h + 1)
                    act.copy(g_o[:, t, h * GLA_DV:(h + 1) * GLA_DV], ps[:, h, :]).then_inc(go_out, 1)
            act.wait_ge(go_out, NT * GLA_H)
            for t in range(NT):
                for h in range(GLA_H):
                    Sc(act.activation(tmp_a[:, 0, 0:GLA_DV], g_o[:, t, h * GLA_DV:(h + 1) * GLA_DV], ACT.Square,
                                      accum_out=gst_r[:, t * GLA_H + h:t * GLA_H + h + 1]))
            act.sem_inc(gn_sq, 1)
            act.wait_ge(gn_inv, 1)
            Sc(act.activation(gst_r, gst_r, ACT.Sqrt))
            act.sem_inc(gn_rs, 1)
            turn_go.scalar()

        def gla_vector():
            v = nc.vector
            prod_gla_low.wait_evicted(v)
            V(v.memset(qeT, 0.0))
            v.sem_inc(zeroed, 1)
            turn_low.vector()
            v.wait_ge(gk_done, 1)
            for t in range(NT):
                for n in range(2):
                    V(v.tensor_tensor(la[:, t, n * W:(n + 1) * W], ps[:, 2 * t + n, :],
                                      small["gla_bias"][:, n * W:(n + 1) * W], ALU.add))
            V(v.scalar_tensor_tensor(out=tmp_a, in0=la, scalar=-1.0, in1=la, op0=ALU.mult, op1=ALU.max))
            v.sem_inc(gk_abs, 1)
            V(v.tensor_scalar(la, la, 0.0, 1.0 / GLA_TAU, ALU.min, ALU.mult))
            v.wait_ge(gk_exp, 1)
            V(v.scalar_tensor_tensor(out=la, in0=tmp_a, scalar=-1.0 / GLA_TAU, in1=la, op0=ALU.mult, op1=ALU.add))
            v.sem_inc(gk_dec, 1)
            v.sem_inc(gk_used, 1)
            v.wait_ge(cum_exp, 1)
            for t in range(NT):
                for n in range(2):
                    c = slice(n * W, (n + 1) * W)
                    q = g_proj[:, t, n * W:(n + 1) * W]
                    k = g_proj[:, t, G_K + n * W:G_K + (n + 1) * W]
                    V(v.scalar_tensor_tensor(out=q, in0=q, scalar=float(GLA_DK) ** -0.5, in1=ps[:, 2 * t + n, :],
                                             op0=ALU.mult, op1=ALU.mult))
                    V(v.tensor_tensor(keT_tmp[:, 0:W], k, ps[:, 4 + 2 * t + n, :], ALU.mult))
                    V(v.tensor_tensor(k, k, tmp_a[:, t, c], ALU.mult))
                    V(v.tensor_copy(kl[:, t, c], keT_tmp[:, 0:W]))
                    if n == 1:
                        v.sem_inc(cum_free, 1)
            v.sem_inc(qk_ready, 1)
            turn_qk.vector()
            v.wait_ge(dl_ready, 1)
            m = 0
            for t in range(NT):
                for par in range(2):
                    ch = 2 * t + par
                    if ch < NCH - 1:
                        for h in range(GLA_H):
                            for j in range(2):
                                k = 2 * h + j
                                v.wait_ge(gs_done, m + 1)
                                if ch == 0:
                                    V(v.tensor_copy(gst_in(1)[:, h, j, :], ps[:, 6 + m % 2, :]))
                                else:
                                    V(v.scalar_tensor_tensor(out=gst_in(ch + 1)[:, h, j, :], in0=gst_in(ch)[:, h, j, :],
                                                             scalar=dlT[:, k, ch:ch + 1], in1=ps[:, 6 + m % 2, :],
                                                             op0=ALU.mult, op1=ALU.add))
                                v.sem_inc(gs_out, 1)
                                m += 1
                    if par == 0:
                        for h in range(GLA_H):
                            a = t * GLA_H + h
                            v.wait_ge(ga_done, a + 1)
                            V(v.tensor_tensor(gAT[:, a % 2, :], ps[:, 4 + a % 2, 0:P], upto, ALU.mult))
                            v.sem_inc(ga_masked, 1)
            v.wait_ge(gn_sq, 1)
            V(v.tensor_scalar(gst_r, gst_r, 1.0 / GLA_DV, EPS, ALU.mult, ALU.add))
            V(v.reciprocal(gst_r, gst_r))
            v.sem_inc(gn_inv, 1)
            v.wait_ge(gn_rs, 1)
            v.wait_ge(gate_act, 1)
            for t in range(NT):
                for h in range(GLA_H):
                    o = g_o[:, t, h * GLA_DV:(h + 1) * GLA_DV]
                    V(v.scalar_tensor_tensor(out=o, in0=o, scalar=gst_r[:, t * GLA_H + h:t * GLA_H + h + 1],
                                             in1=small["gla_onorm"][:, :], op0=ALU.mult, op1=ALU.mult))
                V(v.tensor_tensor(g_o[:, t, :], g_o[:, t, :], g_proj[:, t, G_G:G_G + GLA_V], ALU.mult))
            v.sem_inc(gn_out, 1)
            turn_go.vector()

        keT_tmp = extra[:, 0:W]

        def over(ap, shape):
            return ap.to_broadcast(shape)

        m_proj = view(proj, 0, NT, 3136)
        M_G = LATENT
        m_q = view(proj, 6272, NT, 3072)
        m_kv = view(scr, 0, NT, 2 * D)
        m_norm = view(scr, 6144, NT, 2, MLA_RANK)
        m_qr = view(scr, 0, NT, MLA_H * ROPE)
        m_tmp = view(scr, 2048, 2, NT, MLA_H * ROPE // 2)
        m_kr = view(scr, 4096, NT, 2 * ROPE)
        m_angle = view(scr, 4352, 4, NT, ROPE // 2)
        m_qT = lambda h: view(spare, 2048 + 4096 * (h // 8), 8, S)[:, h % 8, :]
        m_qrT = view(extra, 0, MLA_H // 2, S)
        m_krT = extra[:, 2048:2048 + S]
        m_kT = view(proj, 6272, MLA_H, S)
        m_buf = proj[:, 10368:13600]

        prod_mla = wide(A["w_mla_in"], KD, 6, 0, hidden)
        prod_mla_tail = Product([(A["w_mla_in"], KD, 3072, 0, 64, hidden, False)])
        norm_q = Norm("norm_q", lambda t: m_proj[:, t, 0:MLA_RANK], MLA_RANK, stat_q, junk_q(),
                      lambda t: m_norm[:, t, 0, :])
        norm_kv = Norm("norm_kv", lambda t: m_proj[:, t, MLA_RANK:2 * MLA_RANK], MLA_RANK, stat_kv, junk_q(),
                       lambda t: m_norm[:, t, 1, :])
        turn_cq = Halve(lambda t, k: m_norm[:, t, 0, k * P:(k + 1) * P], 4, hidden,
                              lambda k: small["qa"][:, k:k + 1])
        turn_ckv = Halve(lambda t, k: m_norm[:, t, 1, k * P:(k + 1) * P], 4, lambda k: hidden(4 + k),
                               lambda k: small["kva"][:, k:k + 1])
        prod_q = Product([(A["w_qb"], 4, n * W, 0, W, hidden, False) for n in range(6)])
        prod_kv = wide(A["w_kvb"], 4, 8, 0, lambda k: hidden(4 + k))
        q_turned = turn_tokens("mla_q", lambda t, k: m_q[:, t, k * 192:k * 192 + NOPE], MLA_H, m_qT)
        qr_groups = turn_tokens("mla_unused", lambda t, k: m_qr[:, t, k * P:(k + 1) * P], 8, lambda k: m_qrT[:, k, :]).groups
        qr_groups = qr_groups + [([(m_kr[:, t, :], t * P) for t in range(NT)], [(m_krT, whole(P, 0, S), None)])]
        qr_turned = Turn("mla_rope", qr_groups)
        k_turned = turn_tokens("mla_k", lambda t, k: m_kv[:, t, k * 256:k * 256 + NOPE], MLA_H, lambda k: m_kT[:, k, :])
        angles, tables, rotated, m_gate = (sem("mla_" + n) for n in ("angles", "tables", "rotated", "gate_activated"))
        m_done = sem("mla_gated")

        def mla_parts(h, t):
            q = slice(t * P, (t + 1) * P)
            half = slice(ROPE * (h % 2), ROPE * (h % 2) + ROPE)
            return [(m_qT(h)[:, q], m_kT[:, h, 0:(t + 1) * P]),
                    (m_qrT[half, h // 2, q], m_krT[half, 0:(t + 1) * P])]

        def mla_finish(h, bank, inv):
            for t in range(NT):
                g = m_proj[:, t, M_G + h * P:M_G + (h + 1) * P]
                V(nc.vector.scalar_tensor_tensor(out=g, in0=ps[:, bank, t * P:(t + 1) * P], scalar=inv[:, t:t + 1],
                                                 in1=g, op0=ALU.mult, op1=ALU.mult))

        attend = Attention("mla", MLA_H, mla_parts, lambda h, t: m_kv[:, t, h * 256 + NOPE:h * 256 + 256],
                           MLA_SCALE, m_buf, mla_finish)
        turn_mo = Halve(lambda t, k: m_proj[:, t, M_G + k * P:M_G + (k + 1) * P], KD, hidden)
        prod_mla_out = wide(A["w_mla_out"], KD, 4, 0, hidden)

        def rotate(x1, x2, c, s, t1, t2, out1, out2):
            v = nc.vector
            V(v.tensor_tensor(t1, x1, s, ALU.mult))
            V(v.tensor_tensor(t2, x2, s, ALU.mult))
            V(v.tensor_tensor(out1, x1, c, ALU.mult))
            V(v.tensor_tensor(out1, out1, t2, ALU.subtract))
            V(v.tensor_tensor(out2, x2, c, ALU.mult))
            V(v.tensor_tensor(out2, out2, t1, ALU.add))

        def mla_tables_vector():
            v = nc.vector
            n_ang, ang, cosang, ge = (m_angle[:, j] for j in range(4))
            v.wait_ge(s_pos, 16)
            V(v.tensor_copy(stat[:, 6:8], pos_i[:, :]))
            for t in range(NT):
                V(v.tensor_scalar(ang[:, t, :], C("inv_freq"), stat[:, 6 + t:7 + t], None, ALU.mult))
            rounder = 1.5 * 2.0 ** 23
            V(v.tensor_scalar(n_ang, ang, 1.0 / (2 * np.pi), rounder, ALU.mult, ALU.add))
            V(v.tensor_scalar(n_ang, n_ang, -rounder, None, ALU.add))
            p1 = 6.28125
            p2 = float(np.float32(np.round((2 * np.pi - p1) * 2 ** 21) / 2 ** 21))
            p3 = float(np.float32(2 * np.pi - p1 - p2))
            for part in (p1, p2, p3):
                V(v.scalar_tensor_tensor(out=ang, in0=n_ang, scalar=-part, in1=ang, op0=ALU.mult, op1=ALU.add))
            V(v.tensor_scalar(cosang, ang, float(np.pi / 2), None, ALU.add))
            V(v.tensor_scalar(ge, cosang, float(np.pi), -2 * float(np.pi), ALU.is_gt, ALU.mult))
            V(v.tensor_tensor(cosang, cosang, ge, ALU.add))
            for a in (ang, cosang):
                V(v.tensor_scalar(a, a, 3.14159, -3.14159, ALU.min, ALU.max))
            v.sem_inc(angles, 1)

        def mla_tables_scalar():
            nc.scalar.wait_ge(angles, 1)
            Sc(nc.scalar.activation(tab[:, 0, :, :], m_angle[:, 2], ACT.Sin))
            Sc(nc.scalar.activation(tab[:, 1, :, :], m_angle[:, 1], ACT.Sin))
            nc.scalar.sem_inc(tables, 1)

        def mla_rotate():
            v = nc.vector
            v.wait_ge(tables, 1)
            prod_q.wait_evicted(v)
            H2 = ROPE // 2
            for t in range(NT):
                q = m_q[:, t, :].rearrange("p (h d) -> p h d", h=MLA_H)
                out = m_qr[:, t, :].rearrange("p (h d) -> p h d", h=MLA_H)
                t1, t2 = (m_tmp[:, j, t, :].rearrange("p (h d) -> p h d", h=MLA_H) for j in range(2))
                c, s = (over(tab[:, j, t:t + 1, :], [P, MLA_H, H2]) for j in range(2))
                rotate(q[:, :, NOPE:NOPE + H2], q[:, :, NOPE + H2:], c, s, t1, t2, out[:, :, 0:H2], out[:, :, H2:])
                k = m_proj[:, t, 2 * MLA_RANK:2 * MLA_RANK + ROPE]
                kr = m_kr[:, t, :]
                rotate(k[:, 0:H2], k[:, H2:], tab[:, 0, t, :], tab[:, 1, t, :], m_tmp[:, 0, t, 0:H2], m_tmp[:, 1, t, 0:H2],
                       kr[:, 0:H2], kr[:, H2:ROPE])
                V(v.tensor_copy(kr[:, ROPE:], kr[:, 0:ROPE]))
            v.sem_inc(rotated, 1)

        NQ, NKVW = NSA_H * HD, 6 * NSA_KV * HD
        O_G = NQ + NKVW
        O_DN = O_G + 3 * NSA_H
        O_Z = O_DN + 3 * DN_H * HD
        O_AB = O_Z + DN_H * HD
        O_M = O_AB + 2 * DN_H
        z_tok = view(proj, 0, NT, DN_H * HD)
        n_g = view(proj, 2048, NT, 3 * NSA_H)
        d_ab = view(proj, 2096, NT, 2 * DN_H)
        n_qkv = view(proj, 2128, NT, NQ + NKVW)
        RAWW = S + CONV_K - 1
        raw = view(proj, 2128 + 5120, 3 * DN_H, RAWW)
        convd = view(scr, 0, 3 * DN_H, S)
        n_qT = view(scr, 0, NSA_H, S)
        n_kT = view(scr, 2048, 4, NSA_KV, S)
        n_blk = view(scr, 4096, 2, CMP_BLOCK, NSA_KV * NCMP)
        n_buf = scr[:, 6144:8464]
        n_tmp = view(extra, 0, 2, NSA_H * HD // 2)
        c_s = view(extra, 1024, NT, NSA_H, CPAD)
        c_p = view(extra, 1280, NT, NSA_H, CPAD)
        c_pT = view(extra, 1536, NT, P)
        c_v = view(extra, 0, NSA_H, HD)
        c_g = view(extra, 1792, 2, NSA_KV, CPAD)
        c_u = view(extra, 1856, 2, NSA_KV * NCMP)
        c_h = view(extra, 1916, 2, NSA_KV * NCMP)
        c_k = view(extra, 1976, NSA_KV, CPAD)
        c_gx = view(extra, 2008, NSA_H, CPAD)
        c_max = view(extra, 2136, NT, NSA_H)
        c_sum = view(extra, 2152, NT, NSA_H)
        c_fac = extra[:, 2168:2170]

        prod_n = Product([(A["w_in2"], KD, n * W, 0, W, hidden, False) for n in range(5)])
        prod_ng = Product([(A["w_in2"], KD, O_G, 0, 3 * NSA_H, hidden, False)])
        prod_z = wide(A["w_in2"], KD, 2, O_Z, hidden)
        prod_ab = Product([(A["w_in2"], KD, O_AB, 0, 2 * DN_H, hidden, False)])
        prod_dn = Product([(A["w_in2"], KD, O_DN + n * W, 2 * W, W, hidden, True) for n in range(2)], 3)

        def cmp_weights(w):
            def pair(slot, k0):
                r = k0 * (W // HD)
                return (slot.rearrange("p a b -> p (a b)").rearrange("p (r f) -> p r f", f=HD),
                        w[r * P:(r + 8) * P, :].rearrange("(r p) f -> p r f", p=P))
            return pair

        def cmp_multiply(j):
            def mm(slot, k0, b):
                flat = slot.rearrange("p a b -> p (a b)")
                for r in range(8):
                    rr = k0 * (W // HD) + r
                    last = nc.tensor.matmul(ps[:, b, 0:NSA_KV * NCMP], flat[:, r * HD:(r + 1) * HD], n_blk[:, j, rr, :],
                                            start=(rr == 0), stop=(rr == CMP_BLOCK - 1))
                return last
            return mm

        prod_gates = wide(A["w_in2"], KD, 8, O_M, hidden)
        prod_cmp = Product([(cmp_weights(A["cmp_w1"][j]), 8, 0, 0, W, cmp_multiply(j), False) for j in range(2)], native=True)

        n_rot, n_gates, blk_ready = sem("nsa_rotated"), sem("nsa_gates_ready"), sem("nsa_blocks_ready")
        groups = turn_tokens("nsa_unused", lambda t, k: n_qkv[:, t, k * P:(k + 1) * P], NSA_H, lambda k: n_qT[:, k, :]).groups
        for j, idx in enumerate((0, 1, 2, 4)):
            tiles = [(n_qkv[:, t, NQ + (2 * idx + hk) * HD:NQ + (2 * idx + hk + 1) * HD], hk * S + t * P)
                     for hk in range(NSA_KV) for t in range(NT)]
            groups.append((tiles, [(n_kT[:, j, hk, :], whole(P, hk * S, S), None) for hk in range(NSA_KV)]))
        turn_n = Turn("nsa_qk", groups)
        c_lin, c_tanh, c_act, c_proj, c_keys = (sem("cmp_" + n) for n in ("cubic", "tanh", "activated", "projected", "keys_ready"))
        c_scored, c_centred, c_exped, c_probs = (sem("cmp_" + n) for n in ("scored", "centred", "exped", "probs"))
        turn_cp = Turn("cmp_probs", [([(c_p[:, t, :, :].rearrange("p h c -> p (h c)"), t * P) for t in range(NT)],
                                      [(c_pT.rearrange("p t n -> p (t n)"), whole(P, 0, S), None)])])
        c_mixed, c_out = sem("cmp_mixed"), sem("cmp_out")

        def nsa_parts(h, t):
            which, hh = h // NSA_H, h % NSA_H
            return [(n_qT[:, hh, t * P:(t + 1) * P], n_kT[:, 2 + which, hh // NSA_G, 0:(t + 1) * P])]

        def nsa_value(h, t):
            which, hh = h // NSA_H, h % NSA_H
            o = NQ + (2 * (3 + 2 * which) + hh // NSA_G) * HD
            return n_qkv[:, t, o:o + HD]

        def nsa_finish(h, bank, inv):
            which, hh = h // NSA_H, h % NSA_H
            for t in range(NT):
                g = n_g[:, t, 3 * hh + 1 + which:3 * hh + 2 + which]
                V(nc.vector.tensor_tensor(c_fac[:, t:t + 1], inv[:, t:t + 1], g, ALU.mult))
                o = n_qkv[:, t, hh * HD:(hh + 1) * HD]
                V(nc.vector.scalar_tensor_tensor(out=o, in0=ps[:, bank, t * P:(t + 1) * P], scalar=c_fac[:, t:t + 1],
                                                 in1=o, op0=ALU.mult, op1=ALU.add))

        attend2 = Attention("nsa", 2 * NSA_H, nsa_parts, nsa_value, NSA_SCALE, n_buf, nsa_finish)
        turn_no = Halve(lambda t, k: n_qkv[:, t, k * P:(k + 1) * P], NSA_H, hidden)

        def nsa_tensor(pe):
            pe.wait_ge(n_rot, 1)
            turn_n.tensor(pe)
            pe.wait_ge(blk_ready, 1)
            prod_cmp.tensor(pe)
            pe.wait_ge(c_act, 1)
            pe.matmul(ps[:, 4, 0:NSA_KV * CPAD], w2k[:, :], c_g[:, 0, :, :].rearrange("p a b -> p (a b)"), start=True, stop=True)
            pe.matmul(ps[:, 5, 0:HD], c_gx.rearrange("p h c -> p (h c)"), w2v[:, :], start=True, stop=True).then_inc(c_proj, 1)
            pe.wait_ge(c_keys, 1)
            for t in range(NT):
                for h in range(NSA_H):
                    o = (t * NSA_H + h) * CPAD
                    last = pe.matmul(ps[:, 6, o:o + CPAD], n_qT[:, h, t * P:(t + 1) * P], c_k[:, h // NSA_G, :],
                                     start=True, stop=True)
            last.then_inc(c_scored, 1)
            pe.wait_ge(c_probs, 1)
            turn_cp.tensor(pe)
            turn_cp.wait(pe)
            for t in range(NT):
                for n in range(2):
                    last = pe.matmul(ps[:, 4 + 2 * t + n, :], c_pT[:, t, :],
                                     c_v[:, 4 * n:4 * n + 4, :].rearrange("p h d -> p (h d)"), start=True, stop=True)
            last.then_inc(c_mixed, 1)
            pe.wait_ge(c_out, 1)
            attend2.tensor(pe)
            pe.wait_ge(attend2.finished, 2 * NSA_H)
            turn_no.tensor(pe)

        def nsa_scalar():
            act = nc.scalar
            Sc(act.activation(n_g, n_g, ACT.Sigmoid))
            act.sem_inc(n_gates, 1)
            turn_n.scalar()
            act.wait_ge(c_lin, 1)
            Sc(act.activation(c_u, c_u, ACT.Tanh, scale=GELU_C))
            act.sem_inc(c_tanh, 1)
            act.wait_ge(c_centred, 1)
            Sc(act.activation(c_p, c_s, ACT.Exp))
            act.sem_inc(c_exped, 1)
            attend2.scalar()
            turn_no.scalar()

        def nsa_vector():
            v = nc.vector
            cos, sin = (C(n).rearrange("p (t f) -> p t f", t=NT) for n in ("cos2", "sin2"))
            prod_ng.wait_evicted(v)
            H2 = HD // 2
            for t in range(NT):
                q = n_qkv[:, t, 0:NQ].rearrange("p (h d) -> p h d", h=NSA_H)
                sets = [(q, NSA_H)]
                for idx in (0, 2, 4):
                    o = NQ + 2 * idx * HD
                    sets.append((n_qkv[:, t, o:o + 2 * HD].rearrange("p (h d) -> p h d", h=2), 2))
                for x, n in sets:
                    t1, t2 = (n_tmp[:, j, 0:n * H2].rearrange("p (h d) -> p h d", h=n) for j in range(2))
                    c, s = (over(a[:, t:t + 1, :], [P, n, H2]) for a in (cos, sin))
                    rotate(x[:, :, 0:H2], x[:, :, H2:], c, s, t1, t2, x[:, :, 0:H2], x[:, :, H2:])
            v.sem_inc(n_rot, 1)
            turn_n.vector()
            turn_n.wait(v)
            for j in range(2):
                pe_t = small["cmp_pe"][:, j * CMP_BLOCK:(j + 1) * CMP_BLOCK].unsqueeze(2)
                for hk in range(NSA_KV):
                    base = n_kT[:, j, hk, 0:NCMP * CMP_STRIDE].rearrange("p (c r) -> p r c", r=CMP_STRIDE)
                    next_ = n_kT[:, j, hk, CMP_STRIDE:(NCMP + 1) * CMP_STRIDE].rearrange("p (c r) -> p r c", r=CMP_STRIDE)
                    for half, src in enumerate((base, next_)):
                        r = slice(half * CMP_STRIDE, (half + 1) * CMP_STRIDE)
                        V(v.tensor_tensor(n_blk[:, j, r, hk * NCMP:(hk + 1) * NCMP], src,
                                          over(pe_t[:, r, :], [P, CMP_STRIDE, NCMP]), ALU.add))
            v.sem_inc(blk_ready, 1)
            V(v.memset(c_g, 0.0))

            def copy_hidden(i, n, b):
                return v.tensor_copy(c_h[:, n, :], ps[:, b, 0:NSA_KV * NCMP])
            prod_cmp.run(v, range(2), copy_hidden)
            prod_cmp.wait_evicted(v)
            V(v.tensor_tensor(c_u, c_h, c_h, ALU.mult))
            V(v.tensor_scalar(c_u, c_u, GELU_A, 1.0, ALU.mult, ALU.add))
            V(v.tensor_tensor(c_u, c_u, c_h, ALU.mult))
            v.sem_inc(c_lin, 1)
            v.wait_ge(c_tanh, 1)
            V(v.scalar_tensor_tensor(out=c_u, in0=c_u, scalar=1.0, in1=c_h, op0=ALU.add, op1=ALU.mult))
            for j in range(2):
                V(v.tensor_scalar(c_g[:, j, :, 0:NCMP], c_u[:, j, :].rearrange("p (a b) -> p a b", a=NSA_KV), 0.5, None, ALU.mult))
            for hk in range(NSA_KV):
                V(v.tensor_copy(c_gx[:, hk * NSA_G:(hk + 1) * NSA_G, :], over(c_g[:, 1, hk:hk + 1, :], [P, NSA_G, CPAD])))
            v.sem_inc(c_act, 1)
            v.wait_ge(c_proj, 1)
            V(v.tensor_copy(c_k, ps[:, 4, 0:NSA_KV * CPAD].rearrange("p (a b) -> p a b", a=NSA_KV)))
            for h in range(NSA_H):
                V(v.tensor_scalar(c_v[:, h, :], ps[:, 5, 0:HD], C("cmp_head")[:, h:h + 1], None, ALU.mult))
            v.sem_inc(c_keys, 1)
            v.wait_ge(c_scored, 1)
            mask = C("cmp_mask").rearrange("p (t c) -> p t c", t=NT)
            for t in range(NT):
                V(v.scalar_tensor_tensor(out=c_s[:, t, :, :],
                                         in0=ps[:, 6, t * P:(t + 1) * P].rearrange("p (h c) -> p h c", h=NSA_H),
                                         scalar=NSA_SCALE, in1=over(mask[:, t:t + 1, :], [P, NSA_H, CPAD]),
                                         op0=ALU.mult, op1=ALU.add))
                V(v.tensor_reduce(c_max[:, t, :], c_s[:, t, :, :], AX, ALU.max))
                V(v.tensor_tensor(c_s[:, t, :, :], c_s[:, t, :, :], over(c_max[:, t, :].unsqueeze(2), [P, NSA_H, CPAD]),
                                  ALU.subtract))
            v.sem_inc(c_centred, 1)
            v.wait_ge(c_exped, 1)
            for t in range(NT):
                V(v.tensor_reduce(c_sum[:, t, :], c_p[:, t, :, :], AX, ALU.add))
            V(v.reciprocal(c_sum, c_sum))
            v.wait_ge(n_gates, 1)
            for t in range(NT):
                V(v.scalar_tensor_tensor(out=c_sum[:, t, :], in0=c_sum[:, t, :], scalar=C("cmp_any")[:, t:t + 1],
                                         in1=n_g[:, t, :].rearrange("p (h j) -> p h j", j=3)[:, :, 0],
                                         op0=ALU.mult, op1=ALU.mult))
                V(v.tensor_tensor(c_p[:, t, :, :], c_p[:, t, :, :], over(c_sum[:, t, :].unsqueeze(2), [P, NSA_H, CPAD]), ALU.mult))
            v.sem_inc(c_probs, 1)
            turn_cp.vector()
            v.wait_ge(c_mixed, 1)
            for t in range(NT):
                for n in range(2):
                    V(v.tensor_copy(n_qkv[:, t, n * W:(n + 1) * W], ps[:, 4 + 2 * t + n, :]))
            v.sem_inc(c_out, 1)
            attend2.vector()
            turn_no.vector()

        HB = 4
        NM = HB * NT
        base = 2128
        def mats(n):
            return view(proj, base + n * NM * P, NM, P)
        (d_u0, d_ct, d_er, d_dt, d_at, d_lt, d_x, d_xt, d_kg, d_kd, d_vb) = (mats(n) for n in range(11))
        d_vn, d_os = d_u0, d_ct
        d_s = view(scr, 6144, HB, HD)
        d_uu, d_w = d_dt, d_lt
        d_sq = view(scr, 6656, 2, S)
        d_st = view(scr, 7680, 8, NT, DN_H)
        d_beta, d_dec, d_gc, d_egc, d_eleft, d_t0, d_t1 = (d_st[:, n] for n in range(7))
        d_nst = stat[:, 16:16 + NM]
        pad_ready = sem("dn_pad_ready")
        conv_done, conv_act = sem("dn_convolved"), sem("dn_conv_activated")
        l2_sq, l2_sum, l2_root, l2_free, l2_inv = (sem("l2_" + n) for n in ("squares", "sums", "roots", "sums_read", "inverted"))
        ab_sig, ab_abs, ab_exp, ab_dec, ab_cum, ab_cexp = (sem("dn_" + n) for n in ("beta", "abs", "softplus", "decays", "cumulated", "decay_exps"))
        l2_done = sem("dn_normalised")
        (b_rows, b_rowed, b_erow, b_clamped, b_dexp, b_kk, b_lt, b_tok, b_tokd) = (sem("dn_" + n) for n in (
            "row_inputs", "rows", "row_exps", "clamped", "decay_ready", "products", "systems_ready", "tokens", "tokens_ready"))
        (b_ct, b_t1, b_t1c, b_x, b_xd) = (sem("dn_inv_" + n) for n in ("corner", "corner_times", "corner_times_copied", "update", "updated"))
        (b_uw, b_uwc, b_sc, b_vn, b_sn, b_si, b_in, b_ind) = (sem("dn_" + n) for n in (
            "uw", "uw_copied", "state_read", "values_new", "state_update", "state_ready", "within", "outputs"))
        b_inc, b_nsq, b_ninv, b_nrs, b_fin = (sem("dn_" + n) for n in ("scan_started", "norm_squares", "norm_inverse", "norm_ready", "normed"))
        turn_do = []
        for bt in range(DN_H // HB):
            turn_do.append(Halve(lambda t, k: d_os[:, k * NT + t, :], HB,
                                 lambda k, bt=bt: hidden(NSA_H + bt * HB + k)))
        BANK = lambda a: ps[:, a:a + 2, :].rearrange("p a (m n) -> p (a m) n", n=P)

        def dn_tensor(pe):
            for g in range(DN_H):
                pe.wait_ge(l2_sq, g + 1)
                if g >= 2:
                    pe.wait_ge(l2_free, g - 1)
                pe.matmul(ps[:, 4 + g % 2, :], ones, d_sq2(g), start=True, stop=True).then_inc(l2_sum, 1)
            pe.wait_ge(ab_dec, 1)
            for t in range(NT):
                pe.matmul(ps[:, 6, t * 8:t * 8 + 8], upto, d_dec[:, t, :], start=True, stop=True)
                last = pe.matmul(ps[:, 6, 16 + t * 8:24 + t * 8], after, d_dec[:, t, :], start=True, stop=True)
            last.then_inc(ab_cum, 1)
            pe.wait_ge(l2_done, 1)
            for bt in range(DN_H // HB):
                def kq(which, m):
                    return convd[:, which * DN_H + bt * HB + m // NT, (m % NT) * P:(m % NT + 1) * P]
                pe.wait_ge(b_rows, bt + 1)
                for m in range(NM):
                    pe.matmul(BANK(0)[:, m, :], ones, d_u0[:, m, :], start=True, stop=True)
                    last = pe.matmul(BANK(2)[:, m, :], ones, d_ct[:, m, :], start=True, stop=True)
                last.then_inc(b_rowed, 1)
                for m in range(NM):
                    pe.matmul(BANK(4)[:, m, :], kq(1, m), kq(1, m), start=True, stop=True)
                    last = pe.matmul(BANK(6)[:, m, :], kq(1, m), kq(0, m), start=True, stop=True)
                last.then_inc(b_kk, 1)
                pe.wait_ge(b_lt, bt + 1)
                for m in range(NM):
                    pe.transpose(BANK(4)[:, m, :], kq(1, m), ident)
                    last = pe.transpose(BANK(6)[:, m, :], kq(2, m), ident)
                last.then_inc(b_tok, 1)
                pe.wait_ge(b_tokd, bt + 1)
                for lv in range(6):
                    pe.wait_ge(b_ct, 6 * bt + lv + 1)
                    for m in range(NM):
                        last = pe.matmul(BANK(0)[:, m, :], d_ct[:, m, :], d_x[:, m, :], start=True, stop=True)
                    last.then_inc(b_t1, 1)
                    pe.wait_ge(b_t1c, 6 * bt + lv + 1)
                    for m in range(NM):
                        pe.matmul(BANK(4)[:, m, :], d_xt[:, m, :], d_u0[:, m, :], start=True, stop=True)
                        last = pe.matmul(BANK(6)[:, m, :], d_u0[:, m, :], d_xt[:, m, :], start=True, stop=True)
                    last.then_inc(b_x, 1)
                pe.wait_ge(b_xd, 6 * (bt + 1))
                for m in range(NM):
                    pe.matmul(BANK(0)[:, m, :], d_xt[:, m, :], d_vb[:, m, :], start=True, stop=True)
                    last = pe.matmul(BANK(2)[:, m, :], d_kg[:, m, :], d_xt[:, m, :], start=True, stop=True)
                last.then_inc(b_uw, 1)
                pe.wait_ge(b_uwc, bt + 1)
                for ch in range(NCH):
                    t, par = ch // 2, ch % 2
                    rows = slice(par * CHUNK, (par + 1) * CHUNK)
                    if ch > 0:
                        pe.wait_ge(b_si, 3 * bt + ch)
                        for hl in range(HB):
                            m = hl * NT + t
                            pe.matmul(ps[:, 4, hl * P:(hl + 1) * P], d_w[:, m, :], d_s[:, hl, :], start=True, stop=True)
                            last = pe.matmul(ps[:, 5, hl * P:(hl + 1) * P], kq(0, m), d_s[:, hl, :], start=True, stop=True)
                        last.then_inc(b_sc, 1)
                    if ch < NCH - 1:
                        pe.wait_ge(b_vn, NCH * bt + ch + 1)
                        for hl in range(HB):
                            m = hl * NT + t
                            last = pe.matmul(ps[:, 6, hl * P:(hl + 1) * P], d_kd[rows, m, :], d_vn[rows, m, :], start=True, stop=True)
                        last.then_inc(b_sn, 1)
                pe.wait_ge(b_vn, NCH * (bt + 1))
                for m in range(NM):
                    last = pe.matmul(BANK(0)[:, m, :], d_at[:, m, :], d_vn[:, m, :], start=True, stop=True)
                last.then_inc(b_in, 1)
                pe.wait_ge(b_fin, bt + 1)
                turn_do[bt].tensor(pe)
                turn_do[bt].wait(pe)

        def d_sq2(g):
            return (d_sq if g % 2 == 0 else d_sqb).rearrange("p a n -> p (a n)")

        d_sqb = view(scr, 7168, 2, S)

        def dn_scalar():
            act = nc.scalar
            act.wait_ge(conv_done, 1)
            for half in range(3):
                Sc(act.activation(convd[:, half * 8:(half + 1) * 8, :], convd[:, half * 8:(half + 1) * 8, :], ACT.Silu))
            Sc(act.activation(z_tok, z_tok, ACT.Silu))
            Sc(act.activation(d_beta, d_ab[:, :, DN_H:], ACT.Sigmoid))
            act.sem_inc(conv_act, 1)
            for g in range(DN_H):
                if g >= 2:
                    act.wait_ge(l2_sum, g - 1)
                Sc(act.activation(d_sq2(g), convd[:, 2 * g:2 * g + 2, :].rearrange("p a n -> p (a n)"), ACT.Square))
                act.sem_inc(l2_sq, 1)
            for g in range(DN_H):
                act.wait_ge(l2_inv, g + 1)
                Sc(act.activation(d_rt(g), d_rt(g), ACT.Sqrt))
                act.sem_inc(l2_root, 1)
            act.wait_ge(ab_abs, 1)
            Sc(act.activation(d_t0, d_t0, ACT.Exp, scale=-1.0))
            Sc(act.activation(d_t0, d_t0, ACT.Ln, bias=1.0))
            Sc(act.activation(small_alog[:, :], small["alog"][:, :], ACT.Exp))
            act.sem_inc(ab_exp, 1)
            act.wait_ge(ab_cum, 1)
            Sc(act.copy(d_gc, ps[:, 6, 0:16].rearrange("p (t h) -> p t h", t=NT)))
            Sc(act.activation(d_egc, ps[:, 6, 0:16].rearrange("p (t h) -> p t h", t=NT), ACT.Exp))
            Sc(act.activation(d_eleft, ps[:, 6, 16:32].rearrange("p (t h) -> p t h", t=NT), ACT.Exp))
            act.sem_inc(ab_cexp, 1)
            for bt in range(DN_H // HB):
                act.wait_ge(b_rowed, bt + 1)
                Sc(act.activation(d_er.rearrange("p m n -> p (m n)"), ps[:, 0:2, :].rearrange("p a n -> p (a n)"), ACT.Exp))
                act.sem_inc(b_erow, 1)
                act.wait_ge(b_clamped, bt + 1)
                Sc(act.activation(d_dt, d_dt, ACT.Exp))
                act.sem_inc(b_dexp, 1)
                for lv in range(6):
                    act.wait_ge(b_t1, 6 * bt + lv + 1)
                    Sc(act.copy(d_u0, BANK(0)))
                    act.sem_inc(b_t1c, 1)
                act.wait_ge(b_uw, bt + 1)
                Sc(act.copy(d_uu, BANK(0)))
                Sc(act.copy(d_w, BANK(2)))
                act.sem_inc(b_uwc, 1)
                act.wait_ge(b_ind, bt + 1)
                for m in range(NM):
                    Sc(act.activation(d_x[:, 0, :], d_os[:, m, :], ACT.Square, accum_out=d_nst[:, m:m + 1]))
                act.sem_inc(b_nsq, 1)
                act.wait_ge(b_ninv, bt + 1)
                Sc(act.activation(d_nst, d_nst, ACT.Sqrt))
                act.sem_inc(b_nrs, 1)
                turn_do[bt].scalar()

        small_alog = sb("dn_decay_rate", [P, DN_H])

        def d_rt(g):
            return view(proj, base + g * 512, 2, S)

        def dn_vector():
            v = nc.vector
            prod_dn.wait_evicted(v)
            cw = small["conv"]
            for f in range(3 * DN_H):
                V(v.tensor_scalar(convd[:, f, :], raw[:, f, 0:S], cw[:, CONV_K * f:CONV_K * f + 1], None, ALU.mult))
                for j in range(1, CONV_K):
                    V(v.scalar_tensor_tensor(out=convd[:, f, :], in0=raw[:, f, j:j + S],
                                             scalar=cw[:, CONV_K * f + j:CONV_K * f + j + 1], in1=convd[:, f, :],
                                             op0=ALU.mult, op1=ALU.add))
            v.sem_inc(conv_done, 1)
            v.wait_ge(conv_act, 1)
            for t in range(NT):
                V(v.tensor_tensor(d_t1[:, t, :], d_ab[:, t, 0:DN_H], small["dt_bias"][:, :], ALU.add))
            V(v.scalar_tensor_tensor(out=d_t0, in0=d_t1, scalar=-1.0, in1=d_t1, op0=ALU.mult, op1=ALU.max))
            for g in range(DN_H):
                v.wait_ge(l2_sum, g + 1)
                rt = d_rt(g).rearrange("p a n -> p (a n)")
                V(v.tensor_scalar(rt, ps[:, 4 + g % 2, :], EPS, None, ALU.add))
                v.sem_inc(l2_free, 1)
                V(v.reciprocal(rt, rt))
                v.sem_inc(l2_inv, 1)
            for g in range(DN_H):
                v.wait_ge(l2_root, g + 1)
                x = convd[:, 2 * g:2 * g + 2, :]
                V(v.scalar_tensor_tensor(out=x, in0=x, scalar=float(HD) ** -0.5 if g < 4 else 1.0, in1=d_rt(g),
                                         op0=ALU.mult, op1=ALU.mult))
            v.sem_inc(ab_abs, 1)
            v.wait_ge(ab_exp, 1)
            V(v.scalar_tensor_tensor(out=d_t0, in0=d_t1, scalar=0.0, in1=d_t0, op0=ALU.max, op1=ALU.add))
            for t in range(NT):
                V(v.scalar_tensor_tensor(out=d_dec[:, t, :], in0=d_t0[:, t, :], scalar=-1.0, in1=small_alog[:, :],
                                         op0=ALU.mult, op1=ALU.mult))
            v.sem_inc(ab_dec, 1)
            v.sem_inc(l2_done, 1)
            v.wait_ge(ab_cexp, 1)
            for bt in range(DN_H // HB):
                def col(a, m):
                    h = bt * HB + m // NT
                    return a[:, m % NT, h:h + 1]
                for m in range(NM):
                    V(v.tensor_scalar(d_u0[:, m, :], upto, col(d_dec, m), None, ALU.mult))
                    V(v.tensor_scalar(d_ct[:, m, :], ident, col(d_beta, m), None, ALU.mult))
                v.sem_inc(b_rows, 1)
                v.wait_ge(b_rowed, bt + 1)
                v.wait_ge(b_erow, bt + 1)
                for m in range(NM):
                    V(v.tensor_scalar(d_dt[:, m, :], BANK(0)[:, m, :], col(d_gc, m), 0.0, ALU.subtract, ALU.min))
                v.sem_inc(b_clamped, 1)
                v.wait_ge(b_dexp, bt + 1)
                V(v.tensor_tensor(d_dt, d_dt, over(upto.unsqueeze(1), [P, NM, P]), ALU.mult))
                v.wait_ge(b_kk, bt + 1)
                V(v.tensor_tensor(d_at, BANK(6), d_dt, ALU.mult))
                V(v.tensor_tensor(d_lt, BANK(4), d_dt, ALU.mult))
                V(v.tensor_tensor(d_lt, d_lt, BANK(2), ALU.mult))
                v.sem_inc(b_lt, 1)
                v.wait_ge(b_tok, bt + 1)
                for m in range(NM):
                    V(v.tensor_scalar(d_kg[:, m, :], BANK(4)[:, m, :], col(d_beta, m), col(d_egc, m), ALU.mult, ALU.mult))
                    V(v.tensor_scalar(d_kd[:, m, :], BANK(4)[:, m, :], col(d_eleft, m), None, ALU.mult))
                    V(v.tensor_scalar(d_vb[:, m, :], BANK(6)[:, m, :], col(d_beta, m), None, ALU.mult))
                q = convd[:, bt * HB:(bt + 1) * HB, :].rearrange("p h (t n) -> p (h t) n", t=NT)
                V(v.tensor_tensor(q, q, d_er, ALU.mult))
                V(v.tensor_copy(d_x, over(ident.unsqueeze(1), [P, NM, P])))
                V(v.tensor_copy(d_xt, over(ident.unsqueeze(1), [P, NM, P])))
                v.sem_inc(b_tokd, 1)
                for lv in range(6):
                    V(v.tensor_tensor(d_ct, d_lt, over(C("levels")[:, lv * P:(lv + 1) * P].unsqueeze(1), [P, NM, P]), ALU.mult))
                    v.sem_inc(b_ct, 1)
                    v.wait_ge(b_x, 6 * bt + lv + 1)
                    V(v.tensor_tensor(d_x, d_x, BANK(4), ALU.subtract))
                    V(v.tensor_tensor(d_xt, d_xt, BANK(6), ALU.subtract))
                    v.sem_inc(b_xd, 1)
                v.wait_ge(b_uwc, bt + 1)
                er4 = d_er.rearrange("p (h t) n -> p h t n", t=NT)
                split = lambda a: a.rearrange("p (h t) n -> p h t n", t=NT)
                bank = lambda n: ps[:, n, :].rearrange("p (h n) -> p h n", h=HB)
                for ch in range(NCH):
                    t, par = ch // 2, ch % 2
                    rows = slice(par * CHUNK, (par + 1) * CHUNK)
                    vn, uu, os_ = (split(a)[rows, :, t, :] for a in (d_vn, d_uu, d_os))
                    if ch == 0:
                        V(v.tensor_copy(vn, uu))
                        V(v.memset(os_, 0.0))
                    else:
                        v.wait_ge(b_sc, 3 * bt + ch)
                        V(v.tensor_tensor(vn, uu, bank(4)[rows], ALU.subtract))
                        V(v.tensor_copy(os_, bank(5)[rows]))
                    v.sem_inc(b_vn, 1)
                    if ch < NCH - 1:
                        last = par * CHUNK + CHUNK - 1
                        v.wait_ge(b_sn, 3 * bt + ch + 1)
                        if ch == 0:
                            V(v.tensor_copy(d_s, bank(6)))
                        else:
                            V(v.tensor_tensor(d_s, d_s, over(er4[:, :, t, last:last + 1], [P, HB, HD]), ALU.mult))
                            V(v.tensor_tensor(d_s, d_s, bank(6), ALU.add))
                        v.sem_inc(b_si, 1)
                v.wait_ge(b_in, bt + 1)
                V(v.tensor_tensor(d_os, d_os, BANK(0), ALU.add))
                v.sem_inc(b_ind, 1)
                v.wait_ge(b_nsq, bt + 1)
                V(v.tensor_scalar(d_nst, d_nst, 1.0 / HD, EPS, ALU.mult, ALU.add))
                V(v.reciprocal(d_nst, d_nst))
                v.sem_inc(b_ninv, 1)
                v.wait_ge(b_nrs, bt + 1)
                for m in range(NM):
                    h, t = bt * HB + m // NT, m % NT
                    V(v.scalar_tensor_tensor(out=d_os[:, m, :], in0=d_os[:, m, :], scalar=d_nst[:, m:m + 1],
                                             in1=small["dn_norm"][:, :], op0=ALU.mult, op1=ALU.mult))
                    V(v.tensor_tensor(d_os[:, m, :], d_os[:, m, :], z_tok[:, t, h * HD:(h + 1) * HD], ALU.mult))
                v.sem_inc(b_fin, 1)
                turn_do[bt].vector()
                turn_do[bt].wait(v)

        mixed = view(proj, 0, NT, D)
        part = view(proj, 4096, 2, NT, W)
        prod_up = Product([(A["w_up"][0], 8, 0, W, W, hidden, False),
                           (A["w_up"][1], 8, 0, W, W, lambda k: hidden(NSA_H + k), False)], D // W)
        sig_landed = [sem("gates_landed_even"), sem("gates_landed_odd")]
        stage_ready = sem("gates_staged")
        stored = [sem("gates_stored_even"), sem("gates_stored_odd")]
        mul_done, sum_done = sem("merge_products"), sem("merge_sums")
        merged = sem("merged")
        turn_mix = Halve(lambda t, k: mixed[:, t, k * P:(k + 1) * P], KD, hidden)
        prod_o = wide(A["w_o"], KD, 4, 0, hidden)
        added = sem("attention_added")

        def stage_gates(after):
            def body(i, n, b):
                c = 2 * i + n
                if isinstance(i, int) and i == 0:
                    pass
                else:
                    nc.scalar.wait_ge(stored[n], 16 * i)
                for t in range(NT):
                    last = nc.scalar.activation(gate_stage[:, n, t, :], ps[:, b + t, :], ACT.Sigmoid)
                return last
            prod_gates.run(nc.scalar, range(2), body, after)

        def gates_of(r):
            return [view(extra, 2048 * (r % 2) + 1024 * j, NT, W) for j in range(2)]

        def merge_vector(after):
            v = nc.vector

            def body(i, n, b):
                if n == 0:
                    v.wait_ge(sig_landed[i % 2], 32 * (i // 2 + 1))
                    if i > 0:
                        v.wait_ge(sum_done, i)
                for t in range(NT):
                    last = v.tensor_tensor(part[:, n, t, :], ps[:, b + t, :], gates_of(i)[n][:, t, :], ALU.mult)
                return last
            pr = prod_up
            for i in range(pr.rounds):
                for n in range(2):
                    for k in range(PARTS, 8):
                        pr.split(v, i, n, k)
                    if n == 0:
                        for k in range(PARTS):
                            pr.split(v, i, 1, k)
                    elif i + 1 < pr.rounds:
                        for k in range(PARTS):
                            pr.split(v, i + 1, 0, k)
                    else:
                        after.prime(v)
                    pr.wait_done(v, i, n)
                    c = pr.chunk0 + n
                    body(i, n, 2 * (c % 2)).then_inc(chunk_evicted[c % 2], 1)
                end = pr.chunk0 + 2 * (i + 1)
                v.wait_ge(chunk_evicted[0], (end + 1) // 2)
                v.wait_ge(chunk_evicted[1], end // 2)
                for t in range(NT):
                    last = v.tensor_tensor(mixed[:, t, i * W:(i + 1) * W], part[:, 0, t, :], part[:, 1, t, :], ALU.add)
                last.then_inc(sum_done, 1)
            v.wait_ge(sum_done, pr.rounds)
            v.sem_inc(merged, 1)

        gateT = view(extra, 0, 4, S)
        ffn_act = view(extra, 1024, 4, S)
        prod_ffn = Product([(A["w_gate"], KD, 0, W, W, hidden, True),
                            (A["w_ffn_up"], KD, 0, W, W, hidden, True)], D_FF // W)
        ffn_high, ffn_prod = sem("ffn_high_ready"), sem("ffn_low_ready")
        prod_down = Product([(A["w_down"], NF, n * W, 0, W, lambda k: (act_high[:, k, :], act_low[:, k, :]), False)
                             for n in range(4)])
        ffn_added = sem("ffn_added")

        def two(b, t):
            return ps[:, b + t, :].rearrange("p (f n) -> p f n", n=S)

        def ffn_scalar(after):
            def body(i, n, b):
                if not (isinstance(i, int) and i == 0):
                    nc.scalar.wait_ge(ffn_prod, i)
                for t in range(2):
                    last = nc.scalar.activation(gateT[:, 2 * t:2 * t + 2, :], two(b, t), ACT.Silu)
                return last
            prod_ffn.run(nc.scalar, [0], body, after)

        def ffn_vector(after):
            v = nc.vector
            c0 = prod_ffn.chunk0

            def body(i, n, b):
                v.wait_ge(chunk_evicted[c0 % 2], i + c0 // 2 + 1)
                for t in range(2):
                    last = v.tensor_tensor(ffn_act[:, 2 * t:2 * t + 2, :], two(b, t), gateT[:, 2 * t:2 * t + 2, :], ALU.mult)
                last.then_inc(chunk_evicted[(c0 + 1) % 2], 1)
                v.wait_ge(chunk_evicted[(c0 + 1) % 2], i + (c0 + 1) // 2 + 1)
                v.tensor_copy(act_high[:, piece(i, 4, 0, 4), :], ffn_act).then_inc(ffn_high, 1)
                v.wait_ge(ffn_high, i + 1)
                v.tensor_tensor(act_low[:, piece(i, 4, 0, 4), :], ffn_act, act_high[:, piece(i, 4, 0, 4), :].bitcast(F32),
                                ALU.subtract).then_inc(ffn_prod, 1)
                return None
            prod_ffn.run(v, [1], body, after)

        def add_residual(prod, signal, after=None):
            per = len(prod.chunks)

            def body(i, n, b):
                for t in range(NT):
                    x = X[:, t, piece(i, per * W, n * W, W)]
                    last = nc.vector.tensor_tensor(x, ps[:, b + t, :], x, ALU.add)
                return last
            prod.run(nc.vector, range(per), body, after)
            prod.wait_evicted(nc.vector)
            nc.vector.sem_inc(signal, 1)

        res_ready = [sem("residual_ready_0"), sem("residual_ready_1")]

        def post_vector(post, n):
            v = nc.vector
            post.vector()
            v.wait_ge(scaled, post.nth)
            v.wait_ge(s_row[n], 16)
            for t in range(NT):
                V(v.scalar_tensor_tensor(out=y_tok[:, t, :], in0=y_tok[:, t, :], scalar=stat_x[:, t:t + 1], in1=gain_row,
                                         op0=ALU.mult, op1=ALU.mult))
                V(v.tensor_tensor(X[:, t, :], X[:, t, :], y_tok[:, t, :], ALU.add))
            v.sem_inc(res_ready[n], 1)

        for stage in (norm0, turn0, turn_low, turn_qk, turn_go, post0, norm1, turn1, norm_q, norm_kv, turn_cq, turn_ckv,
                      q_turned, qr_turned, k_turned, turn_mo, post1, norm2, turn2, turn_n, turn_cp, turn_no,
                      turn_do[0], turn_do[1], turn_mix, norm3, turn3, postf):
            stage.place()

        block = ctx.enter_context(nc.Block())

        @block.sync
        def _(sp):
            sp.dma_start(X[:, :, :], A["x"].rearrange("(t p) d -> p t d", p=P)).then_inc(s_x, 16)
            for p in (prod_gla, prod_gla_low, prod_gla_out, prod_mla, prod_mla_tail, prod_q, prod_kv, prod_mla_out,
                      prod_n, prod_ng, prod_z, prod_ab, prod_dn, prod_gates, prod_cmp, prod_up, prod_o, prod_ffn,
                      prod_down):
                p.load(sp)
            sp.wait_ge(out_ready, 1)
            sp.dma_start(A["out"].rearrange("(t p) d -> p t d", p=P), y_tok).then_inc(out_landed, 16)
            sp.wait_ge(out_landed, 16)

        @block.gpsimd
        def _(pool):
            pool.dma_start(const[:, :], A["const"]).then_inc(s_const, 16)
            pool.dma_start(pos_i[:, :], A["positions"]).then_inc(s_pos, 16)
            pool.dma_start(gk2, A["gk2"]).then_inc(s_const, 16)
            pool.dma_start(w2k[:, :], A["w2k"]).then_inc(s_const, 16)
            pool.dma_start(w2v[:, :], A["w2v"]).then_inc(s_const, 16)
            for name, buf in small.items():
                src = A["small"][name]
                pool.dma_start(buf[:, :], src).then_inc(s_const, 16)
            for m in range(2 * D // W):
                c = prod_gates.chunk0 + m
                pool.wait_ge(chunk_evicted[c % 2], c // 2 + 1)
                pool.dma_start(gates_dram[:, m, :], gate_stage[:, m % 2, :, :].rearrange("p t n -> p (t n)"))\
                    .then_inc(stored[m % 2], 16)
            for n in range(2):
                pool.wait_ge(stored[n], 16 * (D // W))
            pool.wait_ge(attend2.finished, 2 * NSA_H)
            for r in range(D // W):
                if r >= 2:
                    pool.wait_ge(sum_done, r - 1)
                for j in range(2):
                    pool.dma_start(gates_of(r)[j].rearrange("p t n -> p (t n)"), gates_dram[:, r + j * (D // W), :])\
                        .then_inc(sig_landed[r % 2], 16)

        @block.scalar
        def _(act):
            act.wait_ge(s_x, 16)
            act.wait_ge(s_const, 16 * n_const)
            norm0.scalar()
            prod_gla.prime(act)
            turn0.scalar()
            evict_wide(prod_gla, g_proj, 0, prod_gla_low)
            evict_tail(prod_gla_low, g_proj, G_LOW, GLA_RANK, prod_gla_out)
            gla_scalar()
            act.dma_start(gain_row, A["l0_post"].to_broadcast([P, D])).then_inc(s_row[0], 16)
            evict_wide(prod_gla_out, y_tok, 0, prod_mla)
            prod_gla_out.wait_evicted(act)
            post0.scalar()
            act.wait_ge(res_ready[0], 1)
            norm1.scalar()
            turn1.scalar()
            mla_tables_scalar()
            evict_wide(prod_mla, m_proj, 0, prod_mla_tail)
            evict_tail(prod_mla_tail, m_proj, 3072, 64, prod_q)
            prod_mla_tail.wait_evicted(act)
            norm_q.scalar()
            norm_kv.scalar()
            turn_cq.scalar()
            turn_ckv.scalar()
            evict_wide(prod_q, m_q, 0, prod_kv)
            for t in range(NT):
                Sc(act.activation(m_proj[:, t, M_G:M_G + D], m_proj[:, t, M_G:M_G + D], ACT.Silu))
            act.sem_inc(m_gate, 1)
            q_turned.scalar()
            qr_turned.scalar()
            evict_wide(prod_kv, m_kv, 0, prod_mla_out)
            k_turned.scalar()
            attend.scalar()
            turn_mo.scalar()
            act.dma_start(gain_row, A["l1_post"].to_broadcast([P, D])).then_inc(s_row[1], 16)
            evict_wide(prod_mla_out, y_tok, 0, prod_n)
            prod_mla_out.wait_evicted(act)
            post1.scalar()
            act.wait_ge(res_ready[1], 1)
            norm2.scalar()
            turn2.scalar()
            evict_wide(prod_n, n_qkv, 0, prod_ng)
            evict_tail(prod_ng, n_g, 0, 3 * NSA_H, prod_z)
            evict_wide(prod_z, z_tok, 0, prod_ab)
            evict_tail(prod_ab, d_ab, 0, 2 * DN_H, prod_dn)
            act.wait_ge(pad_ready, 1)

            def to_raw(i, n, b):
                for t in range(2):
                    last = act.copy(raw[:, piece(i, 8, 4 * n + 2 * t, 2), CONV_K - 1:], two(b, t))
                return last
            prod_dn.run(act, range(2), to_raw, prod_gates)
            prod_dn.wait_evicted(act)
            stage_gates(None)
            nsa_scalar()
            prod_up.prime(act)
            dn_scalar()
            prod_up.run(act, after=prod_o)
            turn_mix.scalar()
            prod_o.run(act, after=prod_ffn)
            act.wait_ge(added, 1)
            norm3.scalar()
            turn3.scalar()
            ffn_scalar(prod_down)
            prod_down.run(act)
            act.wait_ge(ffn_added, 1)
            act.dma_start(gain_row, A["norm_f"].to_broadcast([P, D])).then_inc(s_row[2], 16)
            postf.scalar()

        @block.vector
        def _(v):
            v.wait_ge(s_const, 16 * n_const)
            norm0.vector()
            prod_gla.prime(v)
            turn0.vector()
            prod_gla.run(v, after=prod_gla_low)
            prod_gla_low.run(v, after=prod_gla_out)
            gla_vector()
            prod_gla_out.run(v, after=prod_mla)
            post_vector(post0, 0)
            norm1.vector()
            turn1.vector()
            mla_tables_vector()
            prod_mla.run(v, after=prod_mla_tail)
            prod_mla_tail.run(v, after=prod_q)
            norm_q.vector()
            norm_kv.vector()
            turn_cq.vector()
            turn_ckv.vector()
            prod_q.run(v, after=prod_kv)
            mla_rotate()
            q_turned.vector()
            qr_turned.vector()
            prod_kv.run(v, after=prod_mla_out)
            k_turned.vector()
            v.wait_ge(m_gate, 1)
            attend.vector()
            v.sem_inc(m_done, 1)
            turn_mo.vector()
            prod_mla_out.run(v, after=prod_n)
            post_vector(post1, 1)
            norm2.vector()
            turn2.vector()
            V(v.memset(raw[:, :, 0:CONV_K - 1], 0.0))
            v.sem_inc(pad_ready, 1)
            for p, after in ((prod_n, prod_ng), (prod_ng, prod_z), (prod_z, prod_ab), (prod_ab, prod_dn),
                             (prod_dn, prod_gates), (prod_gates, None)):
                p.run(v, after=after)
            nsa_vector()
            prod_up.prime(v)
            dn_vector()
            merge_vector(prod_o)
            turn_mix.vector()
            add_residual(prod_o, added, prod_ffn)
            norm3.vector()
            turn3.vector()
            ffn_vector(prod_down)
            add_residual(prod_down, ffn_added)
            postf.vector()
            v.wait_ge(scaled, postf.nth)
            v.wait_ge(s_row[2], 16)
            for t in range(NT):
                V(v.scalar_tensor_tensor(out=y_tok[:, t, :], in0=X[:, t, :], scalar=stat_x[:, t:t + 1], in1=gain_row,
                                         op0=ALU.mult, op1=ALU.mult))
            v.sem_inc(out_ready, 1)

        @block.tensor
        def _(pe):
            pe.wait_ge(s_const, 16 * n_const)
            pe.wait_ge(scaled, norm0.nth)
            turn0.tensor(pe)
            turn0.wait(pe)
            prod_gla.tensor(pe)
            prod_gla_low.tensor(pe)
            gla_tensor(pe)
            pe.wait_ge(gn_out, 1)
            turn_go.tensor(pe)
            turn_go.wait(pe)
            prod_gla_out.tensor(pe)
            pe.wait_ge(scaled, norm1.nth)
            turn1.tensor(pe)
            turn1.wait(pe)
            prod_mla.tensor(pe)
            prod_mla_tail.tensor(pe)
            pe.wait_ge(scaled, norm_kv.nth)
            turn_cq.tensor(pe)
            turn_cq.wait(pe)
            turn_ckv.tensor(pe)
            turn_ckv.wait(pe)
            prod_q.tensor(pe)
            pe.wait_ge(rotated, 1)
            q_turned.tensor(pe)
            q_turned.wait(pe)
            qr_turned.tensor(pe)
            qr_turned.wait(pe)
            prod_kv.tensor(pe)
            prod_kv.wait_evicted(pe)
            k_turned.tensor(pe)
            k_turned.wait(pe)
            attend.tensor(pe)
            pe.wait_ge(m_done, 1)
            turn_mo.tensor(pe)
            turn_mo.wait(pe)
            prod_mla_out.tensor(pe)
            pe.wait_ge(scaled, norm2.nth)
            turn2.tensor(pe)
            turn2.wait(pe)
            for p in (prod_n, prod_ng, prod_z, prod_ab, prod_dn, prod_gates):
                p.tensor(pe)
            nsa_tensor(pe)
            turn_no.wait(pe)
            dn_tensor(pe)
            prod_up.tensor(pe)
            pe.wait_ge(merged, 1)
            turn_mix.tensor(pe)
            turn_mix.wait(pe)
            prod_o.tensor(pe)
            pe.wait_ge(scaled, norm3.nth)
            turn3.tensor(pe)
            turn3.wait(pe)
            prod_ffn.tensor(pe)
            pe.wait_ge(ffn_prod, prod_ffn.rounds)
            prod_down.tensor(pe)


def kernel(**inputs):
    import concourse.bacc as bacc
    from concourse.bass_utils import run_bass_kernel_spmd

    a = {k: np.asarray(v) for k, v in inputs.items()}

    def tiles(v):
        return np.ascontiguousarray(v.reshape(-1, P).T)

    def rows(v):
        return np.ascontiguousarray(np.broadcast_to(v.reshape(1, -1), (P, v.size)))

    conv = a["conv_w_2"][0, :, 0, :]
    small = {
        "l0_pre": tiles(a["l0_pre_norm"]), "l1_pre": tiles(a["l1_pre_norm"]),
        "norm1": tiles(a["norm1_w_2"][0]), "norm2": tiles(a["norm2_w_2"][0]),
        "qa": tiles(a["l1_mla_g_qa"]), "kva": tiles(a["l1_mla_g_kva"]),
        "gla_bias": rows(a["l0_gla_b_gk"]), "gla_onorm": rows(a["l0_gla_g_onorm"]),
        "dn_norm": rows(a["dn_norm_w_2"][0]), "alog": rows(a["a_log_2"][0]), "dt_bias": rows(a["dt_bias_2"][0]),
        "conv": np.ascontiguousarray(conv.reshape(CONV_K, -1, P).transpose(2, 1, 0).reshape(P, -1)),
        "cmp_pe": np.ascontiguousarray(np.concatenate([a["cmp_pe_k_2"][0].T, a["cmp_pe_v_2"][0].T], 1)),
    }
    consts = np.concatenate(list(constant_columns().values()), 1)
    arrays = {
        "x": a["x"][0], "positions": np.ascontiguousarray(a["positions"][0].reshape(NT, P).T),
        "const": consts, "gk2": a["l0_gla_w_gk2"], "w2k": a["cmp_w2_k_2"][0], "w2v": a["cmp_w2_v_2"][0],
        "l0_post": a["l0_post_norm"].reshape(1, D), "l1_post": a["l1_post_norm"].reshape(1, D),
        "norm_f": a["norm_f_w_2"].reshape(1, D),
        "w_gla_in": a["l0_gla_w_in"], "w_gla_out": a["l0_gla_w_out"], "w_mla_in": a["l1_mla_w_in"],
        "w_qb": a["l1_mla_w_qb"], "w_kvb": a["l1_mla_w_kvb"], "w_mla_out": a["l1_mla_w_out"],
        "w_in2": a["w_in_2"][0], "cmp_w1_k": a["cmp_w1_k_2"][0], "cmp_w1_v": a["cmp_w1_v_2"][0],
        "w_up_nsa": a["w_up_nsa_2"][0], "w_up_dn": a["w_up_dn_2"][0], "w_o": a["w_o_2"][0],
        "w_gate": a["w_ffn_gate_2"][0], "w_ffn_up": a["w_ffn_up_2"][0], "w_down": a["w_ffn_down_2"][0],
    }
    arrays.update({"small_" + k: v for k, v in small.items()})
    nc = bacc.Bacc("TRN2", target_bir_lowering=False, num_devices=1)
    feed, A = {}, {"small": {}}
    for name, v in arrays.items():
        v = np.ascontiguousarray(v)
        feed["in_" + name] = v
        ap = nc.dram_tensor("in_" + name, v.shape, mybir.dt.from_np(v.dtype), kind="ExternalInput").ap()
        if name.startswith("small_"):
            A["small"][name[6:]] = ap
        else:
            A[name] = ap
    A["cmp_w1"] = [A["cmp_w1_k"], A["cmp_w1_v"]]
    A["w_up"] = [A["w_up_nsa"], A["w_up_dn"]]
    A["out"] = nc.dram_tensor("out_y", (S, D), F32, kind="ExternalOutput").ap()
    program(nc, A)
    r = run_bass_kernel_spmd(nc, [feed], core_ids=[0])
    return r.results[0]["out_y"].reshape(1, S, D)
```

```python
from contextlib import ExitStack

import numpy as np
import concourse.bass as bass
from concourse import mybir
from concourse.alu_op_type import AluOpType as ALU

F32 = mybir.dt.float32
F32R = mybir.dt.float32r
I32 = mybir.dt.int32
ACT = mybir.ActivationFunctionType
AX = mybir.AxisListType.X
ds = bass.ds

P = 128
S = 256
NT = S // P
D = 2048
KD = D // P
EPS = 1e-6
CHUNK = 64
NCH = S // CHUNK
SLOTS = 4
SLOT_K = 2
PARTS = 4
W = 512
HIDDEN = -1e30

GLA_H, GLA_DK, GLA_DV, GLA_RANK, GLA_TAU = 4, 256, 512, 16, 16.0
GLA_QK, GLA_V = GLA_H * GLA_DK, GLA_H * GLA_DV

MLA_H, MLA_RANK, NOPE, ROPE = 16, 512, 128, 64
MLA_SCALE = float(NOPE + ROPE) ** -0.5
LATENT = 2 * MLA_RANK + ROPE

HD = 128
NSA_H, NSA_KV, NSA_G = 8, 2, 4
NSA_SCALE = float(HD) ** -0.5
CMP_BLOCK, CMP_STRIDE = 32, 16
NCMP = (S - CMP_BLOCK) // CMP_STRIDE + 1
CPAD = NCMP + 1
DN_H = 8
CONV_K = 4
D_FF = 5632
GELU_C, GELU_A = float(np.sqrt(2 / np.pi)), 0.044715


def constant_columns():
    i = np.arange(P)
    same = (i[:, None] // CHUNK) == (i[None, :] // CHUNK)
    upto = same & (i[:, None] <= i[None, :])
    after = same & (i[:, None] > i[None, :])
    out = {"ident": np.eye(P), "upto": upto, "after": after, "ones": np.ones((P, P)),
           "half": (i[:, None] // CHUNK) == np.arange(2)[None, :]}
    levels = []
    for n in range(6):
        b = 1 << n
        levels.append(((i[:, None] // (2 * b)) == (i[None, :] // (2 * b)))
                      & ((i[:, None] // b) % 2 == 0) & ((i[None, :] // b) % 2 == 1))
    out["levels"] = np.concatenate(levels, 1)
    causal = np.where(i[None, :] <= i[:, None], 0.0, HIDDEN)
    out["causal"] = np.concatenate([causal, np.zeros((P, P)), causal], 1)
    tok = (np.arange(NT)[None, :, None] * P + i[:, None, None])
    ends = np.arange(CPAD) * CMP_STRIDE + CMP_BLOCK - 1
    seen = (ends[None, None, :] <= tok) & (np.arange(CPAD) < NCMP)[None, None, :]
    out["cmp_mask"] = np.where(seen, 0.0, HIDDEN).reshape(P, NT * CPAD)
    out["cmp_any"] = seen.any(-1)
    out["cmp_head"] = (i[:, None] // CPAD) == np.arange(NSA_H)[None, :]
    inv = (1.0 / (np.float32(10000.0) ** (np.arange(0, HD, 2, dtype=np.float32) / np.float32(HD)))).astype(np.float32)
    ang = tok.astype(np.float32) * inv[None, None, :]
    out["cos2"] = np.cos(ang).reshape(P, -1)
    out["sin2"] = np.sin(ang).reshape(P, -1)
    inv1 = (np.float32(10000.0) ** (-np.arange(0, ROPE, 2, dtype=np.float32) / np.float32(ROPE))).astype(np.float32)
    out["inv_freq"] = np.broadcast_to(inv1[None, :], (P, ROPE // 2))
    return {k: np.ascontiguousarray(v, dtype=np.float32) for k, v in out.items()}


def program(nc, A):
    with ExitStack() as ctx:
        def sb(name, shape, dt=F32):
            return ctx.enter_context(nc.sbuf_tensor(name, shape, dt))

        def sem(name):
            return ctx.enter_context(nc.semaphore(name))

        X = sb("residual", [P, NT, D])
        with nc.sbuf_tensor("hidden_T_high", [P, KD, S], F32R) as high, \
                nc.sbuf_tensor("hidden_T_low", [P, KD, S], F32R) as low:
            HT = (high, low)
        spare = sb("spare", [P, 2 * KD * S])
        ring = sb("weight_ring", [P, SLOTS, SLOT_K, W])
        w_high = sb("weights_high", [P, PARTS, W], F32R)
        w_low = sb("weights_low", [P, PARTS, W], F32R)
        NF = D_FF // P
        with nc.sbuf_tensor("ffn_high", [P, NF, S], F32R) as act_high, \
                nc.sbuf_tensor("ffn_low", [P, NF, S], F32R) as act_low:
            pass
        proj = sb("projections", [P, 13600])
        scr = sb("scratch", [P, 9216])
        gate_stage = sb("gate_stage", [P, 2, NT, W])
        extra = sb("extra", [P, 4096])
        gates_dram = nc.dram_tensor("merge_gates", (P, 2 * D // W, NT * W), F32, kind="Internal").ap()
        ps = ctx.enter_context(nc.psum_tensor("banks", [P, 8, 512], F32))
        cols, offset = {}, 0
        for name, a in constant_columns().items():
            cols[name] = (offset, a.shape[1])
            offset += a.shape[1]
        const = sb("constants", [P, offset])

        def C(name):
            o, n = cols[name]
            return const[:, o:o + n]

        small = {}
        for name in A["small"]:
            if name == "gla_bias":
                small[name] = extra[:, 2048:2048 + GLA_QK]
            elif name == "gla_onorm":
                small[name] = extra[:, 3072:3072 + GLA_DV]
            else:
                small[name] = sb("c_" + name, list(A["small"][name].shape))
        pos_i = sb("positions_i", [P, NT], I32)
        gk2 = proj[0:GLA_RANK, 12416:12416 + GLA_QK]
        w2k = sb("cmp_w2_k", [P, HD])
        w2v = sb("cmp_w2_v", [P, HD])
        stat = sb("statistics", [P, 64])
        tab = sb("mla_rope_tables", [P, 2, NT, ROPE // 2])
        ident, upto, after, ones = C("ident"), C("upto"), C("after"), C("ones")

        v_step, a_step = sem("vector_step"), sem("scalar_step")
        steps = {"v": 0, "a": 0}

        def V(ins):
            steps["v"] += 1
            ins.then_inc(v_step, 1)
            nc.vector.wait_ge(v_step, steps["v"])

        def Sc(ins):
            steps["a"] += 1
            ins.then_inc(a_step, 1)
            nc.scalar.wait_ge(a_step, steps["a"])

        def every(n, pieces):
            for _ in pieces:
                for _ in range(n):
                    yield

        def nothing():
            pass

        landed = [sem(f"weights_landed_{n}") for n in range(SLOTS)]
        high_ready, low_ready, split_used = sem("weights_high_ready"), sem("weights_low_ready"), sem("split_weights_used")
        native_used = sem("native_weights_used")
        chunk_evicted = [sem("chunk_evicted_even"), sem("chunk_evicted_odd")]
        planned = {"use": 0, "chunk": 0, "tile": 0, "native": 0, "native_chunk": 0,
                   "turned": 0, "copied_v": 0, "copied_s": 0, "halved": 0, "norm": 0}
        freed = []

        class Product:

            def __init__(self, chunks, rounds=1, native=False):
                self.chunks, self.rounds, self.native = chunks, rounds, native
                self.use0, self.chunk0, self.tile0 = planned["use"], planned["chunk"], planned["tile"]
                self.uses = sum(c[1] // SLOT_K for c in chunks)
                self.tiles = 0 if native else self.uses * SLOT_K
                self.native0, self.nchunk0 = planned["native"], planned["native_chunk"]
                planned["use"] += self.uses * rounds
                planned["chunk"] += len(chunks) * rounds
                planned["tile"] += self.tiles * rounds
                if native:
                    planned["native"] += self.uses
                    planned["native_chunk"] += len(chunks)
                for n in range(self.uses * rounds):
                    freed.append((native_used, self.native0 + n + 1) if native
                                 else (low_ready, self.tile0 + (n + 1) * SLOT_K))
                assert rounds == 1 or (self.uses % SLOTS == 0 and len(chunks) % 2 == 0 and not native)

            def over(self, eng, body, peel_last=False):
                body(0)
                end = self.rounds - (1 if peel_last else 0)
                if end > 2:
                    with eng.Fori(1, end) as i:
                        body(i)
                elif end == 2:
                    body(1)
                if peel_last and self.rounds > 1:
                    body(self.rounds - 1)

            def load(self, sp):
                def body(i):
                    u = self.use0
                    for w, kt, col0, step, width, _, _ in self.chunks:
                        for k in range(0, kt, SLOT_K):
                            if not isinstance(i, int):
                                sp.wait_ge(low_ready, i * self.tiles + self.tile0 + (u - self.use0 - SLOTS + 1) * SLOT_K)
                            elif u + i * self.uses >= SLOTS:
                                sp.wait_ge(*freed[u + i * self.uses - SLOTS])
                            if isinstance(i, int):
                                at = slice(col0 + i * step, col0 + i * step + width)
                            else:
                                at = ds(i * step + col0, width)
                            if callable(w):
                                dst, src = w(ring[:, u % SLOTS, :, :], k)
                            else:
                                dst = ring[:, u % SLOTS, :, 0:width]
                                src = w[k * P:(k + SLOT_K) * P, at].rearrange("(k p) n -> p k n", p=P)
                            sp.dma_start(dst, src).then_inc(landed[u % SLOTS], 16)
                            u += 1
                self.over(sp, body)

            def place_of(self, n, k):
                before = sum(c[1] for c in self.chunks[:n]) + k
                return self.use0 + before // SLOT_K, self.tile0 + before

            def split(self, eng, i, n, k):
                u, q = self.place_of(n, k)
                width = self.chunks[n][4]
                raw = ring[:, u % SLOTS, k % SLOT_K, 0:width]
                hi, lo = w_high[:, q % PARTS, 0:width], w_low[:, q % PARTS, 0:width]
                if eng is nc.scalar:
                    if k % SLOT_K == 0:
                        eng.wait_ge(landed[u % SLOTS], i * (16 * self.uses // SLOTS) + 16 * (u // SLOTS + 1))
                    if not (isinstance(i, int) and q + i * self.tiles < PARTS):
                        eng.wait_ge(split_used, i * self.tiles + (q - PARTS + 1))
                    nc.scalar.copy(hi, raw).then_inc(high_ready, 1)
                else:
                    eng.wait_ge(high_ready, i * self.tiles + q + 1)
                    nc.vector.tensor_tensor(lo, raw, hi.bitcast(F32), ALU.subtract).then_inc(low_ready, 1)

            def prime(self, eng):
                for k in range(PARTS):
                    self.split(eng, 0, 0, k)

            def multiply(self, pe, i, n, k, b):
                _, kt, _, _, width, acts, turned = self.chunks[n]
                _, q = self.place_of(n, k)
                pe.wait_ge(low_ready, i * self.tiles + q + 1)
                hi, lo = w_high[:, q % PARTS, 0:width], w_low[:, q % PARTS, 0:width]
                ahi, alo = acts(k)
                if turned:
                    for f in range(W // P):
                        out = ps[:, b + f // 2, (f % 2) * S:(f % 2) * S + S]
                        fs = slice(f * P, (f + 1) * P)
                        pe.matmul(out, hi[:, fs], ahi, start=(k == 0 and f % 2 == 0), stop=False, skip_group_check=True)
                        pe.matmul(out, hi[:, fs], alo, start=False, stop=False, skip_group_check=True)
                        last = pe.matmul(out, lo[:, fs], ahi, start=False, stop=(k == kt - 1), skip_group_check=True)
                else:
                    for t in range(NT):
                        ts_ = slice(t * P, (t + 1) * P)
                        out = ps[:, b + t, 0:width]
                        pe.matmul(out, ahi[:, ts_], hi, start=(k == 0), stop=False)
                        pe.matmul(out, ahi[:, ts_], lo, start=False, stop=False)
                        last = pe.matmul(out, alo[:, ts_], hi, start=False, stop=(k == kt - 1))
                last.then_inc(split_used, 1)

            def tensor_fill(self, pe):
                steps = [(n, k) for n, c in enumerate(self.chunks) for k in range(0, c[1], PARTS)]
                assert self.rounds == 1
                at = iter(steps)

                def fill():
                    n, k0 = next(at)
                    c = self.chunk0 + n
                    if k0 == 0:
                        pe.wait_ge(chunk_evicted[c % 2], c // 2)
                    for k in range(k0, k0 + PARTS):
                        self.multiply(pe, 0, n, k, 2 * (c % 2))
                return fill

            def split_fill(self, eng, body_of=None):
                steps = [(n, k) for n, c in enumerate(self.chunks) for k in range(0, c[1], PARTS)]
                at = iter(range(len(steps)))

                def fill():
                    j = next(at)
                    if j + 1 < len(steps):
                        n, k0 = steps[j + 1]
                        for k in range(k0, k0 + PARTS):
                            self.split(eng, 0, n, k)
                    if body_of is not None and (j + 1 == len(steps) or steps[j + 1][0] != steps[j][0]):
                        n = steps[j][0]
                        self.wait_done(eng, 0, n)
                        c = self.chunk0 + n
                        body_of(0, n, 2 * (c % 2)).then_inc(chunk_evicted[c % 2], 1)
                return fill

            def tensor(self, pe, before=None):
                def body(i):
                    c = self.chunk0
                    for n, (w, kt, _, _, width, acts, turned) in enumerate(self.chunks):
                        if not (isinstance(i, int) and c + i * len(self.chunks) < 2):
                            pe.wait_ge(chunk_evicted[c % 2], i * (len(self.chunks) // 2) + c // 2)
                        b = 2 * (c % 2)
                        if self.native:
                            for k0 in range(0, kt, SLOT_K):
                                u, _ = self.place_of(n, k0)
                                pe.wait_ge(landed[u % SLOTS], 16 * (u // SLOTS + 1))
                                acts(ring[:, u % SLOTS, :, :], k0, b).then_inc(native_used, 1)
                            c += 1
                            continue
                        for k in range(kt):
                            if before is not None and isinstance(i, int) and i == 0:
                                before(n, k)
                            self.multiply(pe, i, n, k, b)
                        c += 1
                self.over(pe, body)

            def wait_done(self, eng, i, n):
                if self.native:
                    eng.wait_ge(native_used, self.native0 + sum(c[1] for c in self.chunks[:n + 1]) // SLOT_K)
                else:
                    _, q = self.place_of(n, self.chunks[n][1])
                    eng.wait_ge(split_used, i * self.tiles + q)

            def wait_evicted(self, eng):
                end = self.chunk0 + len(self.chunks) * self.rounds
                eng.wait_ge(chunk_evicted[0], (end + 1) // 2)
                if end > 1:
                    eng.wait_ge(chunk_evicted[1], end // 2)

            def run(self, eng, which=(), body_of=None, after=None, side=iter(())):
                def body(i):
                    final = isinstance(i, int) and i == self.rounds - 1
                    for n, chunk in enumerate(self.chunks):
                        if not self.native:
                            for k in range(PARTS, chunk[1]):
                                self.split(eng, i, n, k)
                                next(side, None)
                            if n + 1 < len(self.chunks):
                                for k in range(PARTS):
                                    self.split(eng, i, n + 1, k)
                                    next(side, None)
                            elif not final:
                                for k in range(PARTS):
                                    self.split(eng, i + 1, 0, k)
                                    next(side, None)
                            elif after is not None:
                                after.prime(eng)
                        if n in which:
                            self.wait_done(eng, i, n)
                            c = self.chunk0 + n
                            last = body_of(i, n, 2 * (c % 2))
                            if last is not None:
                                last.then_inc(chunk_evicted[c % 2], 1)
                    if self.rounds > 2:
                        for _ in side:
                            pass
                self.over(eng, body, peel_last=True)

        def piece(i, step, off, n):
            return slice(off + i * step, off + i * step + n) if isinstance(i, int) else ds(i * step + off, n)

        def hidden(k):
            return HT[0][:, k, :], HT[1][:, k, :]

        def wide(weights, kt, n, col0, acts):
            per = 4 if kt == 4 else 2
            return Product([(weights, kt, col0 + m * W, per * W, W, acts, False) for m in range(per)], n // per)

        def evict_wide(prod, dst, off, after=None, side=iter(())):
            per = len(prod.chunks)

            def body(i, n, b):
                for t in range(NT):
                    last = nc.scalar.copy(dst[:, t, piece(i, per * W, off + n * W, W)], ps[:, b + t, :])
                return last
            prod.run(nc.scalar, range(per), body, after, side)

        def evict_tail(prod, dst, off, n, after=None, side=iter(())):
            def body(i, m, b):
                for t in range(NT):
                    last = nc.scalar.copy(dst[:, t, off:off + n], ps[:, b + t, 0:n])
                return last
            prod.run(nc.scalar, [0], body, after, side)

        turned = sem("group_turned")
        copied_out = [sem("turned_copied_by_vector"), sem("turned_copied_by_scalar")]
        squares, inverse, rooted = sem("norm_squares"), sem("norm_inverse"), sem("norm_rooted")
        scaled = [sem("norm_scaled_by_scalar"), sem("norm_scaled_by_vector")]
        chunk_squared = sem("chunk_squared")

        class Turn:

            def __init__(self, name, groups):
                self.groups = groups

            def place(self):
                self.turned0, self.out0 = planned["turned"], [planned["copied_v"], planned["copied_s"]]
                n = len(self.groups)
                planned["turned"] += n
                planned["copied_v"] += (n + 1) // 2
                planned["copied_s"] += n // 2

            def tensor(self, pe):
                for g, (tiles, _) in enumerate(self.groups):
                    if g >= 4:
                        pe.wait_ge(copied_out[g % 2], self.out0[g % 2] + (g - 4) // 2 + 1)
                    for src, col in tiles:
                        rows, width = src.shape[0], src.shape[1]
                        last = pe.transpose(ps[0:width, 4 + g % 4, col:col + rows], src, ident[0:rows, 0:rows])
                    last.then_inc(turned, 1)

            def copies(self, eng, which):
                for g, (_, copies) in enumerate(self.groups):
                    if g % 2 != which:
                        continue
                    eng.wait_ge(turned, self.turned0 + g + 1)
                    for dst, src, scale in copies:
                        if which == 0:
                            last = nc.vector.tensor_copy(dst, src(4 + g % 4)) if scale is None else \
                                nc.vector.tensor_scalar(dst, src(4 + g % 4), scale, None, ALU.mult)
                        else:
                            last = nc.scalar.copy(dst, src(4 + g % 4)) if scale is None else \
                                nc.scalar.activation(dst, src(4 + g % 4), ACT.Copy, scale=scale)
                    last.then_inc(copied_out[which], 1)

            def vector(self):
                self.copies(nc.vector, 0)

            def scalar(self):
                self.copies(nc.scalar, 1)

            def wait(self, eng):
                eng.wait_ge(copied_out[0], self.out0[0] + (len(self.groups) + 1) // 2)
                if len(self.groups) > 1:
                    eng.wait_ge(copied_out[1], self.out0[1] + len(self.groups) // 2)

        def whole(rows, a, n):
            return lambda b: ps[0:rows, b, a:a + n]

        def turn_tokens(name, src, n_tiles, dst, gain=None):
            groups = []
            for k in range(0, n_tiles, 2):
                tiles = [(src(t, k + kk), kk * S + t * P) for kk in range(2) for t in range(NT)]
                copies = [(dst(k + kk), whole(P, kk * S, S), None if gain is None else gain(k + kk))
                          for kk in range(2)]
                groups.append((tiles, copies))
            return Turn(name, groups)

        high_out, low_out = sem("activations_high_ready"), sem("activations_low_ready")

        class Halve:

            def __init__(self, src, n_tiles, dst, gain=None):
                self.src, self.n, self.dst, self.gain = src, n_tiles // 2, dst, gain

            def place(self):
                self.turned0, self.first = planned["turned"], planned["halved"]
                planned["turned"] += self.n
                planned["halved"] += self.n

            def turn_group(self, pe, g):
                if g >= 4:
                    pe.wait_ge(low_out, self.first + g - 3)
                for kk in range(2):
                    for t in range(NT):
                        o = kk * S + t * P
                        last = pe.transpose(ps[:, 4 + g % 4, o:o + P], self.src(t, 2 * g + kk), ident)
                last.then_inc(turned, 1)

            def tensor(self, pe):
                for g in range(self.n):
                    self.turn_group(pe, g)

            def tensor_into(self, pe, prod):
                assert self.n <= 4 + PARTS

                def before(n, k):
                    if n == 0:
                        if k == 0:
                            for g in range(min(4, self.n)):
                                self.turn_group(pe, g)
                        elif 3 + k < self.n:
                            self.turn_group(pe, 3 + k)
                        pe.wait_ge(low_out, self.first + k // 2 + 1)
                prod.tensor(pe, before)

            def scalar(self):
                for g in range(self.n):
                    nc.scalar.wait_ge(turned, self.turned0 + g + 1)
                    for kk in range(2):
                        k = 2 * g + kk
                        x = ps[:, 4 + g % 4, kk * S:(kk + 1) * S]
                        last = nc.scalar.copy(self.dst(k)[0], x) if self.gain is None else \
                            nc.scalar.activation(self.dst(k)[0], x, ACT.Copy, scale=self.gain(k))
                    last.then_inc(high_out, 1)

            def vector(self):
                for g in range(self.n):
                    nc.vector.wait_ge(high_out, self.first + g + 1)
                    for kk in range(2):
                        k = 2 * g + kk
                        x = ps[:, 4 + g % 4, kk * S:(kk + 1) * S]
                        hi, lo = self.dst(k)
                        last = nc.vector.tensor_tensor(lo, x, hi.bitcast(F32), ALU.subtract) if self.gain is None else \
                            nc.vector.scalar_tensor_tensor(out=lo, in0=x, scalar=self.gain(k), in1=hi.bitcast(F32),
                                                           op0=ALU.mult, op1=ALU.subtract)
                    last.then_inc(low_out, 1)

            def wait(self, eng):
                eng.wait_ge(low_out, self.first + self.n)

        class Norm:

            def __init__(self, name, src, n, rstd, junk, dst=None, sums=None):
                self.src, self.n, self.rstd, self.junk, self.dst, self.sums = src, n, rstd, junk, dst, sums

            def place(self):
                planned["norm"] += 1
                self.nth = planned["norm"]

            def scalar(self, ready=None):
                if self.sums is None:
                    for t in range(NT):
                        if ready is not None:
                            nc.scalar.wait_ge(*ready(t))
                        Sc(nc.scalar.activation(self.junk, self.src(t), ACT.Square, accum_out=self.rstd[:, t:t + 1]))
                nc.scalar.sem_inc(squares, 1)
                nc.scalar.wait_ge(inverse, self.nth)
                Sc(nc.scalar.activation(self.rstd, self.rstd, ACT.Sqrt))
                nc.scalar.sem_inc(rooted, 1)
                if self.dst is not None:
                    Sc(nc.scalar.activation(self.dst(0), self.src(0), ACT.Copy, scale=self.rstd[:, 0:1]))
                nc.scalar.sem_inc(scaled[0], 1)

            def vector(self):
                nc.vector.wait_ge(squares, self.nth)
                if self.sums is not None:
                    V(nc.vector.tensor_reduce(self.rstd, self.sums, AX, ALU.add))
                V(nc.vector.tensor_scalar(self.rstd, self.rstd, 1.0 / self.n, EPS, ALU.mult, ALU.add))
                V(nc.vector.reciprocal(self.rstd, self.rstd))
                nc.vector.sem_inc(inverse, 1)
                nc.vector.wait_ge(rooted, self.nth)
                if self.dst is not None:
                    V(nc.vector.tensor_scalar(self.dst(1), self.src(1), self.rstd[:, 1:2], None, ALU.mult))
                nc.vector.sem_inc(scaled[1], 1)

            def wait(self, eng):
                for n in range(NT):
                    eng.wait_ge(scaled[n], self.nth)

        def view(buf, off, *dims):
            n = int(np.prod(dims))
            v = buf[:, off:off + n]
            if len(dims) == 2:
                return v.rearrange("p (a b) -> p a b", a=dims[0])
            if len(dims) == 3:
                return v.rearrange("p (a b c) -> p a b c", a=dims[0], b=dims[1])
            if len(dims) == 4:
                return v.rearrange("p (a b c d) -> p a b c d", a=dims[0], b=dims[1], c=dims[2])
            return v

        def junk_q():
            return extra[:, 2304:2304 + MLA_RANK]

        class Attention:

            def __init__(self, name, heads, parts, value, scale, buf, finish):
                self.h, self.parts, self.value, self.scale, self.finish = heads, parts, value, scale, finish
                self.s = view(buf, 0, 2, 3 * P)
                self.p = view(buf, 6 * P, 2, 3 * P)
                self.pt = view(buf, 12 * P, 2, 3 * P)
                self.st = view(buf, 18 * P, 2, 2, 2)
                self.sum = view(buf, 18 * P + 8, 2, 2)
                names = ("_scores", "_masked", "_probs", "_turned", "_turned_copied", "_mixed", "_finished")
                (self.scored, self.masked, self.probs, self.turned, self.copied, self.mixed,
                 self.finished) = (sem(name + n) for n in names)
                self.span = [(0, P), (P, 3 * P)]

            def tensor(self, pe, fill=nothing):
                def score(h):
                    if h >= 2:
                        pe.wait_ge(self.masked, h - 1)
                    for t in range(NT):
                        a, b = self.span[t]
                        parts = self.parts(h, t)
                        for n, (q, k) in enumerate(parts):
                            last = pe.matmul(ps[:, 4 + h % 2, a:b], q, k, start=(n == 0), stop=(n == len(parts) - 1))
                    last.then_inc(self.scored, 1)
                score(0)
                for h in range(self.h):
                    if h + 1 < self.h:
                        score(h + 1)
                    fill()
                    pe.wait_ge(self.probs, h + 1)
                    if h >= 1:
                        pe.wait_ge(self.copied, h)
                    for n in range(3):
                        last = pe.transpose(ps[:, 6, n * P:(n + 1) * P], self.p[:, h % 2, n * P:(n + 1) * P], ident)
                    last.then_inc(self.turned, 1)
                    fill()
                    pe.wait_ge(self.copied, h + 1)
                    if h >= 1:
                        pe.wait_ge(self.finished, h)
                    pt = self.pt[:, h % 2, :]
                    pe.matmul(ps[:, 7, 0:P], pt[:, 0:P], self.value(h, 0), start=True, stop=True)
                    pe.matmul(ps[:, 7, P:2 * P], pt[:, P:2 * P], self.value(h, 0), start=True, stop=False)
                    pe.matmul(ps[:, 7, P:2 * P], pt[:, 2 * P:3 * P], self.value(h, 1), start=False, stop=True)\
                        .then_inc(self.mixed, 1)

            def vector(self, fill=nothing):
                def mask(h):
                    nc.vector.wait_ge(self.scored, h + 1)
                    if h >= 2:
                        nc.vector.wait_ge(self.probs, h - 1)
                    V(nc.vector.scalar_tensor_tensor(out=self.s[:, h % 2, :], in0=ps[:, 4 + h % 2, 0:3 * P],
                                                     scalar=self.scale, in1=C("causal"), op0=ALU.mult, op1=ALU.add))
                    for t in range(NT):
                        a, b = self.span[t]
                        ins = nc.vector.tensor_reduce(self.st[:, h % 2, 0, t:t + 1], self.s[:, h % 2, a:b], AX, ALU.max)
                        V(ins)
                    V(nc.vector.tensor_scalar(self.st[:, h % 2, 1, :], self.st[:, h % 2, 0, :], -1.0, None, ALU.mult))
                    nc.vector.sem_inc(self.masked, 1)
                mask(0)
                for h in range(self.h):
                    if h + 1 < self.h:
                        mask(h + 1)
                    fill()
                    fill()
                    nc.vector.wait_ge(self.mixed, h + 1)
                    V(nc.vector.reciprocal(self.sum[:, h % 2, :], self.sum[:, h % 2, :]))
                    self.finish(h, 7, self.sum[:, h % 2, :])
                    nc.vector.sem_inc(self.finished, 1)

            def scalar(self, fill=nothing):
                for h in range(self.h):
                    nc.scalar.wait_ge(self.masked, h + 1)
                    if h >= 2:
                        nc.scalar.wait_ge(self.turned, h - 1)
                        nc.scalar.wait_ge(self.finished, h - 1)
                    for t in range(NT):
                        a, b = self.span[t]
                        Sc(nc.scalar.activation(self.p[:, h % 2, a:b], self.s[:, h % 2, a:b], ACT.Exp,
                                                bias=self.st[:, h % 2, 1, t:t + 1],
                                                accum_out=self.sum[:, h % 2, t:t + 1]))
                    nc.scalar.sem_inc(self.probs, 1)
                    fill()
                    nc.scalar.wait_ge(self.turned, h + 1)
                    if h >= 2:
                        nc.scalar.wait_ge(self.mixed, h - 1)
                    nc.scalar.copy(self.pt[:, h % 2, :], ps[:, 6, 0:3 * P]).then_inc(self.copied, 1)
                    fill()

        s_x = [sem("x_landed_0"), sem("x_landed_1")]
        s_first = sem("first_constants_landed")
        s_const, s_pos = sem("constants_landed"), sem("positions_landed")
        s_row = [sem("gain_row_landed_0"), sem("gain_row_landed_1"), sem("gain_row_landed_2")]
        out_landed = sem("output_landed")
        out_ready = sem("output_ready")
        n_const = 2 + len(small)

        g_proj = view(proj, 0, NT, 6160)
        G_K, G_V, G_G, G_LOW = GLA_QK, 2 * GLA_QK, 2 * GLA_QK + GLA_V, 2 * GLA_QK + 2 * GLA_V
        y_tok = view(scr, 0, NT, D)
        gain_row = scr[:, 2 * D:3 * D]
        gain_f = gate_stage.rearrange("p a t n -> p (a t n)")
        normed = view(proj, 0, NT, D)
        junk = proj[:, 2 * D:3 * D]

        stat_x = stat[:, 0:2]
        stat_q, stat_kv = stat[:, 2:4], stat[:, 4:6]

        sums = view(stat, 24, NT, D // W)

        def square_chunk(t, j, src):
            Sc(nc.scalar.activation(ps[:, 4, :], src, ACT.Square, accum_out=sums[:, t, j:j + 1]))

        def x_norm(name, gain, sums=None):
            n = Norm(name, lambda t: X[:, t, :], D, stat_x, junk, lambda t: normed[:, t, :], sums)
            tr = Halve(lambda t, k: normed[:, t, k * P:(k + 1) * P], KD, hidden, lambda k: small[gain][:, k:k + 1])
            return n, tr

        norm0, turn0 = x_norm("norm0", "l0_pre")
        norm1, turn1 = x_norm("norm1", "l1_pre")
        norm2, turn2 = x_norm("norm2", "norm1")
        norm3, turn3 = x_norm("norm3", "norm2", sums)
        post0 = Norm("post0", None, D, stat_x, None, None, sums)
        post1 = Norm("post1", None, D, stat_x, None, None, sums)
        postf = Norm("postf", None, D, stat_x, None, None, sums)

        la = view(scr, 0, NT, GLA_QK)
        tmp_a = view(scr, 2048, NT, GLA_QK)
        kl = view(scr, 2048, NT, GLA_QK)
        qeT = view(scr, 4096, 8, NT, 2, P)
        keT = view(extra, 0, 8, S)
        gst = view(spare, 0, GLA_H, 2, GLA_DV)
        gst2 = view(spare, 4096, GLA_H, 2, GLA_DV)

        def gst_in(ch):
            return gst if ch % 2 else gst2

        g_o = view(proj, 0, NT, 6160)[:, :, 0:D]
        lowT = scr[:, 8192:8192 + S]
        dlT = view(scr, 8448, 8, NCH)
        gAT = view(scr, 8512, 2, P)
        gst_r = stat[:, 8:16]

        prod_gla_low = Product([(A["w_gla_in"], KD, G_LOW, 0, GLA_RANK, hidden, False)])
        prod_gla = wide(A["w_gla_in"], KD, 12, 0, hidden)
        turn_low = Turn("gla_low", [([(g_proj[:, t, G_LOW:G_LOW + GLA_RANK], t * P) for t in range(NT)],
                                     [(lowT[0:GLA_RANK, :], whole(GLA_RANK, 0, S), None)])])
        gk_done, gk_used = sem("gla_gate_done"), sem("gla_gate_used")
        gk_exp, gk_dec = sem("gla_gate_exp"), sem("gla_decay_ready")
        gk_abs = sem("gla_gate_abs")
        cum_done, cum_exp, cum_free = sem("gla_cumulated"), sem("gla_cumulated_exp"), sem("gla_cumulated_used")
        groups = []
        for k in range(8):
            tiles = [(g_proj[:, t, k * P:(k + 1) * P], t * P) for t in range(NT)]
            copies = [(qeT[:, k, t, par, par * CHUNK:(par + 1) * CHUNK],
                       whole(P, t * P + par * CHUNK, CHUNK), None) for t in range(NT) for par in range(2)]
            groups.append((tiles, copies))
        for k in range(8):
            tiles = [(g_proj[:, t, G_K + k * P:G_K + (k + 1) * P], t * P) for t in range(NT)]
            groups.append((tiles, [(keT[:, k, :], whole(P, 0, S), None)]))
        turn_qk = Turn("gla_qk", groups)
        qk_ready = sem("gla_scaled_ready")
        zeroed = sem("gla_zeroed")
        dl_done, dl_ready = sem("gla_chunk_decay_done"), sem("gla_chunk_decay_ready")
        ga_done, ga_masked = sem("gla_scores"), sem("gla_scores_masked")
        go_done, go_out = sem("gla_output_done"), sem("gla_output_evicted")
        gs_done, gs_out = sem("gla_update_done"), sem("gla_state_ready")
        gate_act = sem("gla_gate_activated")
        gn_sq, gn_inv, gn_rs, gn_out = sem("gla_norm_squares"), sem("gla_norm_inverse"), sem("gla_norm_ready"), sem("gla_gated")
        turn_go = Halve(lambda t, k: g_o[:, t, k * P:(k + 1) * P], KD, hidden)
        prod_gla_out = wide(A["w_gla_out"], KD, 4, 0, hidden)

        def gla_gates_tensor(pe, chunk, tile):
            if (chunk, tile) == (0, 8):
                prod_gla_low.wait_evicted(pe)
                turn_low.tensor(pe)
            if (chunk, tile) != (1, 0):
                return
            turn_low.wait(pe)
            pe.wait_ge(s_const, 16 * n_const)
            for t in range(NT):
                for n in range(2):
                    last = pe.matmul(ps[:, 4 + 2 * t + n, :], lowT[0:GLA_RANK, t * P:(t + 1) * P],
                                     gk2[:, n * W:(n + 1) * W], start=True, stop=True)
            last.then_inc(gk_done, 1)

        def gla_tensor(pe):
            prod_gla.wait_evicted(pe)
            for t in range(NT):
                pe.wait_ge(gk_dec, t + 1)
                for n in range(2):
                    pe.matmul(ps[:, 2 * t + n, :], upto, la[:, t, n * W:(n + 1) * W], start=True, stop=True)
                    last = pe.matmul(ps[:, 4 + 2 * t + n, :], after, la[:, t, n * W:(n + 1) * W], start=True, stop=True)
            last.then_inc(cum_done, 1)
            pe.wait_ge(cum_free, 2)
            for k in range(8):
                for t in range(NT):
                    last = pe.matmul(ps[:, 0, k * NCH + 2 * t:k * NCH + 2 * t + 2], la[:, t, k * P:(k + 1) * P],
                                     C("half"), start=True, stop=True)
            last.then_inc(dl_done, 1)
            pe.wait_ge(qk_ready, 1)
            pe.wait_ge(zeroed, 1)
            turn_qk.tensor(pe)
            turn_qk.wait(pe)
            pe.wait_ge(dl_ready, 1)
            n = 0
            m = 0
            for t in range(NT):
                for par in range(2):
                    ch = 2 * t + par
                    rows = slice(par * CHUNK, (par + 1) * CHUNK)
                    if ch < NCH - 1:
                        for h in range(GLA_H):
                            for j in range(2):
                                k = 2 * h + j
                                if m >= 2:
                                    pe.wait_ge(gs_out, m - 1)
                                pe.matmul(ps[:, 6 + m % 2, :], kl[rows, t, k * P:(k + 1) * P],
                                          g_proj[rows, t, G_V + h * GLA_DV:G_V + (h + 1) * GLA_DV],
                                          start=True, stop=True).then_inc(gs_done, 1)
                                m += 1
                    if par == 0:
                        for h in range(GLA_H):
                            a = t * GLA_H + h
                            if a >= 2:
                                pe.wait_ge(ga_masked, a - 1)
                            for j in range(2):
                                k = 2 * h + j
                                for half in range(2):
                                    hs = slice(half * CHUNK, (half + 1) * CHUNK)
                                    last = pe.matmul(ps[:, 4 + a % 2, hs], keT[:, k, t * P:(t + 1) * P],
                                                     qeT[:, k, t, half, hs], start=(j == 0 and half == 0),
                                                     stop=(j == 1), skip_group_check=True)
                            last.then_inc(ga_done, 1)
                            pe.wait_ge(ga_masked, a + 1)
                            if t == 1:
                                pe.wait_ge(go_out, h + 1)
                            pe.matmul(ps[:, h, :], gAT[:, a % 2, :],
                                      g_proj[:, t, G_V + h * GLA_DV:G_V + (h + 1) * GLA_DV], start=True, stop=False)
                    for h in range(GLA_H):
                        for j in range(2):
                            k = 2 * h + j
                            if ch > 0:
                                pe.wait_ge(gs_out, 8 * (ch - 1) + k + 1)
                                last = pe.matmul(ps[:, h, :], qeT[:, k, t, par, :], gst_in(ch)[:, h, j, :],
                                                 start=False, stop=(par == 1 and j == 1))
                        if par == 1:
                            last.then_inc(go_done, 1)


        def gla_gates_scalar():
            act = nc.scalar
            for _ in range(21):
                yield
            for t in range(NT):
                act.wait_ge(gk_abs, t + 1)
                Sc(act.activation(tmp_a[:, t, :], tmp_a[:, t, :], ACT.Exp, scale=-1.0))
                yield
                yield
            for t in range(NT):
                Sc(act.activation(tmp_a[:, t, :], tmp_a[:, t, :], ACT.Ln, bias=1.0))
                act.sem_inc(gk_exp, 1)
                yield

        def gla_gates_vector():
            v = nc.vector
            for _ in range(9):
                yield
            turn_low.vector()
            for _ in range(8):
                yield
            v.wait_ge(s_const, 16 * n_const)
            v.wait_ge(gk_done, 1)
            for t in range(NT):
                for n in range(2):
                    V(v.tensor_tensor(la[:, t, n * W:(n + 1) * W], ps[:, 4 + 2 * t + n, :],
                                      small["gla_bias"][:, n * W:(n + 1) * W], ALU.add))
                yield
                V(v.scalar_tensor_tensor(out=tmp_a[:, t, :], in0=la[:, t, :], scalar=-1.0, in1=la[:, t, :],
                                         op0=ALU.mult, op1=ALU.max))
                v.sem_inc(gk_abs, 1)
                yield
                yield
            V(v.tensor_scalar(la, la, 0.0, 1.0 / GLA_TAU, ALU.min, ALU.mult))
            for _ in range(4):
                yield
            for t in range(NT):
                v.wait_ge(gk_exp, t + 1)
                V(v.scalar_tensor_tensor(out=la[:, t, :], in0=tmp_a[:, t, :], scalar=-1.0 / GLA_TAU, in1=la[:, t, :],
                                         op0=ALU.mult, op1=ALU.add))
                v.sem_inc(gk_dec, 1)
                yield

        def gla_scalar():
            act = nc.scalar
            act.wait_ge(cum_done, 1)
            act.wait_ge(gk_used, 1)
            for t in range(NT):
                for n in range(2):
                    e = tmp_a[:, t, n * W:(n + 1) * W]
                    Sc(act.activation(e, ps[:, 2 * t + n, :], ACT.Exp, scale=-1.0))
                    Sc(act.activation(ps[:, 2 * t + n, :], ps[:, 2 * t + n, :], ACT.Exp))
                    Sc(act.activation(ps[:, 4 + 2 * t + n, :], ps[:, 4 + 2 * t + n, :], ACT.Exp))
                    act.sem_inc(cum_exp, 1)
            act.wait_ge(dl_done, 1)
            Sc(act.activation(dlT, ps[:, 0, 0:8 * NCH].rearrange("p (k c) -> p k c", k=8), ACT.Exp))
            act.sem_inc(dl_ready, 1)
            turn_qk.scalar()
            for t in range(NT):
                Sc(act.activation(g_proj[:, t, G_G:G_G + GLA_V], g_proj[:, t, G_G:G_G + GLA_V], ACT.Silu))
            act.sem_inc(gate_act, 1)
            for t in range(NT):
                for h in range(GLA_H):
                    act.wait_ge(go_done, t * GLA_H + h + 1)
                    Sc(act.copy(g_o[:, t, h * GLA_DV:(h + 1) * GLA_DV], ps[:, h, :]))
                    act.sem_inc(go_out, 1)
                    Sc(act.activation(g_junk, g_o[:, t, h * GLA_DV:(h + 1) * GLA_DV], ACT.Square,
                                      accum_out=gst_r[:, t * GLA_H + h:t * GLA_H + h + 1]))
                act.sem_inc(gn_sq, 1)
                act.wait_ge(gn_inv, t + 1)
                r = gst_r[:, t * GLA_H:(t + 1) * GLA_H]
                Sc(act.activation(r, r, ACT.Sqrt))
                act.sem_inc(gn_rs, 1)
            turn_go.scalar()

        def gla_vector():
            v = nc.vector
            prod_gla.wait_evicted(v)
            V(v.memset(qeT, 0.0))
            v.sem_inc(zeroed, 1)
            v.sem_inc(gk_used, 1)
            for t in range(NT):
                for n in range(2):
                    v.wait_ge(cum_exp, 2 * t + n + 1)
                    c = slice(n * W, (n + 1) * W)
                    q = g_proj[:, t, n * W:(n + 1) * W]
                    k = g_proj[:, t, G_K + n * W:G_K + (n + 1) * W]
                    V(v.scalar_tensor_tensor(out=q, in0=q, scalar=float(GLA_DK) ** -0.5, in1=ps[:, 2 * t + n, :],
                                             op0=ALU.mult, op1=ALU.mult))
                    V(v.tensor_tensor(keT_tmp[:, 0:W], k, ps[:, 4 + 2 * t + n, :], ALU.mult))
                    V(v.tensor_tensor(k, k, tmp_a[:, t, c], ALU.mult))
                    V(v.tensor_copy(kl[:, t, c], keT_tmp[:, 0:W]))
                    if n == 1:
                        v.sem_inc(cum_free, 1)
            v.sem_inc(qk_ready, 1)
            turn_qk.vector()
            v.wait_ge(dl_ready, 1)
            m = 0
            for t in range(NT):
                for par in range(2):
                    ch = 2 * t + par
                    if ch < NCH - 1:
                        for h in range(GLA_H):
                            for j in range(2):
                                k = 2 * h + j
                                v.wait_ge(gs_done, m + 1)
                                if ch == 0:
                                    V(v.tensor_copy(gst_in(1)[:, h, j, :], ps[:, 6 + m % 2, :]))
                                else:
                                    V(v.scalar_tensor_tensor(out=gst_in(ch + 1)[:, h, j, :], in0=gst_in(ch)[:, h, j, :],
                                                             scalar=dlT[:, k, ch:ch + 1], in1=ps[:, 6 + m % 2, :],
                                                             op0=ALU.mult, op1=ALU.add))
                                v.sem_inc(gs_out, 1)
                                m += 1
                    if par == 0:
                        for h in range(GLA_H):
                            a = t * GLA_H + h
                            v.wait_ge(ga_done, a + 1)
                            V(v.tensor_tensor(gAT[:, a % 2, :], ps[:, 4 + a % 2, 0:P], upto, ALU.mult))
                            v.sem_inc(ga_masked, 1)
                        v.wait_ge(gate_act, 1)
                        gate = g_proj[:, t, G_G:G_G + GLA_V].rearrange("p (h d) -> p h d", h=GLA_H)
                        V(v.tensor_tensor(gate, gate, over(small["gla_onorm"].unsqueeze(1), [P, GLA_H, GLA_DV]), ALU.mult))
            for t in range(NT):
                v.wait_ge(gn_sq, t + 1)
                r = gst_r[:, t * GLA_H:(t + 1) * GLA_H]
                V(v.tensor_scalar(r, r, 1.0 / GLA_DV, EPS, ALU.mult, ALU.add))
                V(v.reciprocal(r, r))
                v.sem_inc(gn_inv, 1)
                v.wait_ge(gn_rs, t + 1)
                for h in range(GLA_H):
                    c = slice(h * GLA_DV, (h + 1) * GLA_DV)
                    gate = g_proj[:, t, G_G + h * GLA_DV:G_G + (h + 1) * GLA_DV]
                    V(v.scalar_tensor_tensor(out=g_o[:, t, c], in0=g_o[:, t, c], scalar=gst_r[:, t * GLA_H + h:t * GLA_H + h + 1],
                                             in1=gate, op0=ALU.mult, op1=ALU.mult))
            v.sem_inc(gn_out, 1)
            turn_go.vector()

        keT_tmp = extra[:, 0:W]
        g_junk = scr[:, 0:GLA_DV]

        def over(ap, shape):
            return ap.to_broadcast(shape)

        m_proj = view(proj, 0, NT, 3136)
        M_G = LATENT
        m_q = view(proj, 6272, NT, 3072)
        m_kv = view(scr, 0, NT, 2 * D)
        m_norm = view(scr, 6144, NT, 2, MLA_RANK)
        m_qr = gate_stage.rearrange("p a t n -> p (a t n)").rearrange("p (t n) -> p t n", t=NT)
        m_tmp = view(extra, 0, 2, NT, MLA_H * ROPE // 2)
        m_kr = view(extra, 3072, NT, 2 * ROPE)
        m_angle = view(scr, 4352, 4, NT, ROPE // 2)
        m_qT = lambda h: view(spare, 2048 + 4096 * (h // 8), 8, S)[:, h % 8, :]
        m_qrT = view(extra, 0, MLA_H // 2, S)
        m_krT = extra[:, 2048:2048 + S]
        m_kT = view(proj, 6272, MLA_H, S)
        m_buf = proj[:, 10368:13600]

        prod_mla = wide(A["w_mla_in"], KD, 6, 0, hidden)
        prod_mla_tail = Product([(A["w_mla_in"], KD, 3072, 0, 64, hidden, False)])
        norm_q = Norm("norm_q", lambda t: m_proj[:, t, 0:MLA_RANK], MLA_RANK, stat_q, junk_q(),
                      lambda t: m_norm[:, t, 0, :])
        norm_kv = Norm("norm_kv", lambda t: m_proj[:, t, MLA_RANK:2 * MLA_RANK], MLA_RANK, stat_kv, junk_q(),
                       lambda t: m_norm[:, t, 1, :])
        turn_cq = Halve(lambda t, k: m_norm[:, t, 0, k * P:(k + 1) * P], 4, hidden,
                              lambda k: small["qa"][:, k:k + 1])
        turn_ckv = Halve(lambda t, k: m_norm[:, t, 1, k * P:(k + 1) * P], 4, lambda k: hidden(4 + k),
                               lambda k: small["kva"][:, k:k + 1])
        prod_q = Product([(A["w_qb"], 4, n * W, 0, W, hidden, False) for n in range(6)])
        prod_kv = wide(A["w_kvb"], 4, 8, 0, lambda k: hidden(4 + k))
        q_turned = turn_tokens("mla_q", lambda t, k: m_q[:, t, k * 192:k * 192 + NOPE], MLA_H, m_qT)
        qr_groups = turn_tokens("mla_unused", lambda t, k: m_qr[:, t, k * P:(k + 1) * P], 8, lambda k: m_qrT[:, k, :]).groups
        qr_groups = qr_groups + [([(m_kr[:, t, :], t * P) for t in range(NT)], [(m_krT, whole(P, 0, S), None)])]
        qr_turned = Turn("mla_rope", qr_groups)
        k_turned = turn_tokens("mla_k", lambda t, k: m_kv[:, t, k * 256:k * 256 + NOPE], MLA_H, lambda k: m_kT[:, k, :])
        angles, tables, rotated, m_gate = (sem("mla_" + n) for n in ("angles", "tables", "rotated", "gate_activated"))
        m_done = sem("mla_gated")

        def mla_parts(h, t):
            q = slice(t * P, (t + 1) * P)
            half = slice(ROPE * (h % 2), ROPE * (h % 2) + ROPE)
            return [(m_qT(h)[:, q], m_kT[:, h, 0:(t + 1) * P]),
                    (m_qrT[half, h // 2, q], m_krT[half, 0:(t + 1) * P])]

        def mla_finish(h, bank, inv):
            for t in range(NT):
                g = m_proj[:, t, M_G + h * P:M_G + (h + 1) * P]
                V(nc.vector.scalar_tensor_tensor(out=g, in0=ps[:, bank, t * P:(t + 1) * P], scalar=inv[:, t:t + 1],
                                                 in1=g, op0=ALU.mult, op1=ALU.mult))

        attend = Attention("mla", MLA_H, mla_parts, lambda h, t: m_kv[:, t, h * 256 + NOPE:h * 256 + 256],
                           MLA_SCALE, m_buf, mla_finish)
        turn_mo = Halve(lambda t, k: m_proj[:, t, M_G + k * P:M_G + (k + 1) * P], KD, hidden)
        prod_mla_out = wide(A["w_mla_out"], KD, 4, 0, hidden)

        def rotate(x1, x2, c, s, t1, t2, out1, out2):
            v = nc.vector
            V(v.tensor_tensor(t1, x1, s, ALU.mult))
            V(v.tensor_tensor(t2, x2, s, ALU.mult))
            V(v.tensor_tensor(out1, x1, c, ALU.mult))
            V(v.tensor_tensor(out1, out1, t2, ALU.subtract))
            V(v.tensor_tensor(out2, x2, c, ALU.mult))
            V(v.tensor_tensor(out2, out2, t1, ALU.add))

        def mla_tables_vector():
            v = nc.vector
            n_ang, ang, cosang, ge = (m_angle[:, j] for j in range(4))
            v.wait_ge(s_pos, 16)
            V(v.tensor_copy(stat[:, 6:8], pos_i[:, :]))
            for t in range(NT):
                V(v.tensor_scalar(ang[:, t, :], C("inv_freq"), stat[:, 6 + t:7 + t], None, ALU.mult))
            rounder = 1.5 * 2.0 ** 23
            V(v.tensor_scalar(n_ang, ang, 1.0 / (2 * np.pi), rounder, ALU.mult, ALU.add))
            V(v.tensor_scalar(n_ang, n_ang, -rounder, None, ALU.add))
            p1 = 6.28125
            p2 = float(np.float32(np.round((2 * np.pi - p1) * 2 ** 21) / 2 ** 21))
            p3 = float(np.float32(2 * np.pi - p1 - p2))
            for part in (p1, p2, p3):
                V(v.scalar_tensor_tensor(out=ang, in0=n_ang, scalar=-part, in1=ang, op0=ALU.mult, op1=ALU.add))
            V(v.tensor_scalar(cosang, ang, float(np.pi / 2), None, ALU.add))
            V(v.tensor_scalar(ge, cosang, float(np.pi), -2 * float(np.pi), ALU.is_gt, ALU.mult))
            V(v.tensor_tensor(cosang, cosang, ge, ALU.add))
            for a in (ang, cosang):
                V(v.tensor_scalar(a, a, 3.14159, -3.14159, ALU.min, ALU.max))
            v.sem_inc(angles, 1)

        def mla_tables_scalar():
            nc.scalar.wait_ge(angles, 1)
            Sc(nc.scalar.activation(tab[:, 0, :, :], m_angle[:, 2], ACT.Sin))
            Sc(nc.scalar.activation(tab[:, 1, :, :], m_angle[:, 1], ACT.Sin))
            nc.scalar.sem_inc(tables, 1)

        def mla_rotate():
            v = nc.vector
            v.wait_ge(tables, 1)
            prod_q.wait_evicted(v)
            H2 = ROPE // 2
            for t in range(NT):
                q = m_q[:, t, :].rearrange("p (h d) -> p h d", h=MLA_H)
                out = m_qr[:, t, :].rearrange("p (h d) -> p h d", h=MLA_H)
                t1, t2 = (m_tmp[:, j, t, :].rearrange("p (h d) -> p h d", h=MLA_H) for j in range(2))
                c, s = (over(tab[:, j, t:t + 1, :], [P, MLA_H, H2]) for j in range(2))
                rotate(q[:, :, NOPE:NOPE + H2], q[:, :, NOPE + H2:], c, s, t1, t2, out[:, :, 0:H2], out[:, :, H2:])
                yield
                k = m_proj[:, t, 2 * MLA_RANK:2 * MLA_RANK + ROPE]
                kr = m_kr[:, t, :]
                rotate(k[:, 0:H2], k[:, H2:], tab[:, 0, t, :], tab[:, 1, t, :], m_tmp[:, 0, t, 0:H2], m_tmp[:, 1, t, 0:H2],
                       kr[:, 0:H2], kr[:, H2:ROPE])
                V(v.tensor_copy(kr[:, ROPE:], kr[:, 0:ROPE]))
                yield
            v.sem_inc(rotated, 1)

        NQ, NKVW = NSA_H * HD, 6 * NSA_KV * HD
        O_G = NQ + NKVW
        O_DN = O_G + 3 * NSA_H
        O_Z = O_DN + 3 * DN_H * HD
        O_AB = O_Z + DN_H * HD
        O_M = O_AB + 2 * DN_H
        z_tok = view(proj, 0, NT, DN_H * HD)
        n_g = view(proj, 2048, NT, 3 * NSA_H)
        d_ab = view(proj, 2096, NT, 2 * DN_H)
        n_qkv = view(proj, 2128, NT, NQ + NKVW)
        RAWW = S + CONV_K - 1
        raw = view(proj, 2128 + 5120, 3 * DN_H, RAWW)
        convd = raw[:, :, 0:S]
        conv_tmp = view(extra, 3072, 4, S)
        n_qT = view(scr, 0, NSA_H, S)
        n_kT = view(scr, 2048, 4, NSA_KV, S)
        n_blk = view(scr, 4096, 2, CMP_BLOCK, NSA_KV * NCMP)
        n_buf = scr[:, 6144:8464]
        n_tmp = view(extra, 0, 2, NSA_H * HD // 2)
        c_s = view(extra, 1024, NT, NSA_H, CPAD)
        c_p = view(extra, 1280, NT, NSA_H, CPAD)
        c_pT = view(extra, 1536, NT, P)
        c_v = view(extra, 0, NSA_H, HD)
        c_g = view(extra, 1792, 2, NSA_KV, CPAD)
        c_u = view(extra, 1856, 2, NSA_KV * NCMP)
        c_h = view(extra, 1916, 2, NSA_KV * NCMP)
        c_k = view(extra, 1976, NSA_KV, CPAD)
        c_gx = view(extra, 2008, NSA_H, CPAD)
        c_max = view(extra, 2136, NT, NSA_H)
        c_sum = view(extra, 2152, NT, NSA_H)
        c_fac = extra[:, 2168:2170]

        prod_dn = Product([(A["w_in2"], KD, O_DN + n * W, 2 * W, W, hidden, True) for n in range(2)], 3)
        prod_n = Product([(A["w_in2"], KD, n * W, 0, W, hidden, False) for n in range(5)])
        prod_ng = Product([(A["w_in2"], KD, O_G, 0, 3 * NSA_H, hidden, False)])
        prod_z = wide(A["w_in2"], KD, 2, O_Z, hidden)
        prod_ab = Product([(A["w_in2"], KD, O_AB, 0, 2 * DN_H, hidden, False)])

        def cmp_weights(w):
            def pair(slot, k0):
                r = k0 * (W // HD)
                return (slot.rearrange("p a b -> p (a b)").rearrange("p (r f) -> p r f", f=HD),
                        w[r * P:(r + 8) * P, :].rearrange("(r p) f -> p r f", p=P))
            return pair

        def cmp_multiply(j):
            def mm(slot, k0, b):
                flat = slot.rearrange("p a b -> p (a b)")
                for r in range(8):
                    rr = k0 * (W // HD) + r
                    last = nc.tensor.matmul(ps[:, b, 0:NSA_KV * NCMP], flat[:, r * HD:(r + 1) * HD], n_blk[:, j, rr, :],
                                            start=(rr == 0), stop=(rr == CMP_BLOCK - 1))
                return last
            return mm

        prod_cmp = Product([(cmp_weights(A["cmp_w1"][j]), 8, 0, 0, W, cmp_multiply(j), False) for j in range(2)], native=True)

        prod_gates = Product([(A["w_in2"], KD, O_M + n * W, 0, W, hidden, False) for n in range(8)])
        n_rot, n_gates, blk_ready = sem("nsa_rotated"), sem("nsa_gates_ready"), sem("nsa_blocks_ready")
        groups = turn_tokens("nsa_unused", lambda t, k: n_qkv[:, t, k * P:(k + 1) * P], NSA_H, lambda k: n_qT[:, k, :]).groups
        for j, idx in enumerate((0, 1, 2, 4)):
            tiles = [(n_qkv[:, t, NQ + (2 * idx + hk) * HD:NQ + (2 * idx + hk + 1) * HD], hk * S + t * P)
                     for hk in range(NSA_KV) for t in range(NT)]
            groups.append((tiles, [(n_kT[:, j, hk, :], whole(P, hk * S, S), None) for hk in range(NSA_KV)]))
        turn_n = Turn("nsa_qk", groups)
        c_lin, c_tanh, c_act, c_proj, c_keys = (sem("cmp_" + n) for n in ("cubic", "tanh", "activated", "projected", "keys_ready"))
        c_scored, c_centred, c_exped, c_probs = (sem("cmp_" + n) for n in ("scored", "centred", "exped", "probs"))
        turn_cp = Turn("cmp_probs", [([(c_p[:, t, :, :].rearrange("p h c -> p (h c)"), t * P) for t in range(NT)],
                                      [(c_pT.rearrange("p t n -> p (t n)"), whole(P, 0, S), None)])])
        c_mixed, c_out = sem("cmp_mixed"), sem("cmp_out")

        def nsa_parts(h, t):
            which, hh = h // NSA_H, h % NSA_H
            return [(n_qT[:, hh, t * P:(t + 1) * P], n_kT[:, 2 + which, hh // NSA_G, 0:(t + 1) * P])]

        def nsa_value(h, t):
            which, hh = h // NSA_H, h % NSA_H
            o = NQ + (2 * (3 + 2 * which) + hh // NSA_G) * HD
            return n_qkv[:, t, o:o + HD]

        def nsa_finish(h, bank, inv):
            which, hh = h // NSA_H, h % NSA_H
            for t in range(NT):
                g = n_g[:, t, 3 * hh + 1 + which:3 * hh + 2 + which]
                V(nc.vector.tensor_tensor(c_fac[:, t:t + 1], inv[:, t:t + 1], g, ALU.mult))
                o = n_qkv[:, t, hh * HD:(hh + 1) * HD]
                V(nc.vector.scalar_tensor_tensor(out=o, in0=ps[:, bank, t * P:(t + 1) * P], scalar=c_fac[:, t:t + 1],
                                                 in1=o, op0=ALU.mult, op1=ALU.add))

        attend2 = Attention("nsa", 2 * NSA_H, nsa_parts, nsa_value, NSA_SCALE, n_buf, nsa_finish)
        turn_no = Halve(lambda t, k: n_qkv[:, t, k * P:(k + 1) * P], NSA_H, hidden)

        def nsa_tensor(pe):
            pe.wait_ge(n_rot, 1)
            turn_n.tensor(pe)
            prepare_sums(pe)
            pe.wait_ge(blk_ready, 1)
            prod_cmp.tensor(pe)
            prepare_cumulated(pe)
            pe.wait_ge(c_act, 1)
            pe.matmul(ps[:, 4, 0:NSA_KV * CPAD], w2k[:, :], c_g[:, 0, :, :].rearrange("p a b -> p (a b)"), start=True, stop=True)
            pe.matmul(ps[:, 5, 0:HD], c_gx.rearrange("p h c -> p (h c)"), w2v[:, :], start=True, stop=True).then_inc(c_proj, 1)
            pe.wait_ge(c_keys, 1)
            for t in range(NT):
                for h in range(NSA_H):
                    o = (t * NSA_H + h) * CPAD
                    last = pe.matmul(ps[:, 6, o:o + CPAD], n_qT[:, h, t * P:(t + 1) * P], c_k[:, h // NSA_G, :],
                                     start=True, stop=True)
            last.then_inc(c_scored, 1)
            pe.wait_ge(c_probs, 1)
            turn_cp.tensor(pe)
            turn_cp.wait(pe)
            pe.wait_ge(ab_cexp, 1)
            for t in range(NT):
                for n in range(2):
                    last = pe.matmul(ps[:, 4 + 2 * t + n, :], c_pT[:, t, :],
                                     c_v[:, 4 * n:4 * n + 4, :].rearrange("p h d -> p (h d)"), start=True, stop=True)
            last.then_inc(c_mixed, 1)
            pe.wait_ge(c_out, 1)
            attend2.tensor(pe, prod_gates.tensor_fill(pe))
            pe.wait_ge(attend2.finished, 2 * NSA_H)
            turn_no.tensor(pe)

        def nsa_scalar():
            act = nc.scalar
            Sc(act.activation(n_g, n_g, ACT.Sigmoid))
            act.sem_inc(n_gates, 1)
            turn_n.scalar()
            prepare_squares()
            prepare_roots()
            act.wait_ge(c_lin, 1)
            Sc(act.activation(c_u, c_u, ACT.Tanh, scale=GELU_C))
            act.sem_inc(c_tanh, 1)
            prepare_exps()
            prod_gates.prime(act)
            act.wait_ge(c_centred, 1)
            Sc(act.activation(c_p, c_s, ACT.Exp))
            act.sem_inc(c_exped, 1)
            attend2.scalar(prod_gates.split_fill(act, stage_gates))
            turn_no.scalar()

        def nsa_rotate():
            v = nc.vector
            cos, sin = (C(n).rearrange("p (t f) -> p t f", t=NT) for n in ("cos2", "sin2"))
            prod_n.wait_evicted(v)
            H2 = HD // 2
            for t in range(NT):
                q = n_qkv[:, t, 0:NQ].rearrange("p (h d) -> p h d", h=NSA_H)
                sets = [(q, NSA_H)]
                for idx in (0, 2, 4):
                    o = NQ + 2 * idx * HD
                    sets.append((n_qkv[:, t, o:o + 2 * HD].rearrange("p (h d) -> p h d", h=2), 2))
                for x, n in sets:
                    t1, t2 = (n_tmp[:, j, 0:n * H2].rearrange("p (h d) -> p h d", h=n) for j in range(2))
                    c, s = (over(a[:, t:t + 1, :], [P, n, H2]) for a in (cos, sin))
                    rotate(x[:, :, 0:H2], x[:, :, H2:], c, s, t1, t2, x[:, :, 0:H2], x[:, :, H2:])
                    yield
            v.sem_inc(n_rot, 1)

        def nsa_vector():
            v = nc.vector
            prod_ab.wait_evicted(v)
            prepare_logits()
            turn_n.vector()
            turn_n.wait(v)
            for j in range(2):
                pe_t = small["cmp_pe"][:, j * CMP_BLOCK:(j + 1) * CMP_BLOCK].unsqueeze(2)
                for hk in range(NSA_KV):
                    base = n_kT[:, j, hk, 0:NCMP * CMP_STRIDE].rearrange("p (c r) -> p r c", r=CMP_STRIDE)
                    next_ = n_kT[:, j, hk, CMP_STRIDE:(NCMP + 1) * CMP_STRIDE].rearrange("p (c r) -> p r c", r=CMP_STRIDE)
                    for half, src in enumerate((base, next_)):
                        r = slice(half * CMP_STRIDE, (half + 1) * CMP_STRIDE)
                        V(v.tensor_tensor(n_blk[:, j, r, hk * NCMP:(hk + 1) * NCMP], src,
                                          over(pe_t[:, r, :], [P, CMP_STRIDE, NCMP]), ALU.add))
            v.sem_inc(blk_ready, 1)
            V(v.memset(c_g, 0.0))
            prepare_heads()

            def copy_hidden(i, n, b):
                return v.tensor_copy(c_h[:, n, :], ps[:, b, 0:NSA_KV * NCMP])
            prod_cmp.run(v, range(2), copy_hidden)
            prod_cmp.wait_evicted(v)
            V(v.tensor_tensor(c_u, c_h, c_h, ALU.mult))
            V(v.tensor_scalar(c_u, c_u, GELU_A, 1.0, ALU.mult, ALU.add))
            V(v.tensor_tensor(c_u, c_u, c_h, ALU.mult))
            v.sem_inc(c_lin, 1)
            prod_gates.prime(v)
            v.wait_ge(c_tanh, 1)
            V(v.scalar_tensor_tensor(out=c_u, in0=c_u, scalar=1.0, in1=c_h, op0=ALU.add, op1=ALU.mult))
            for j in range(2):
                V(v.tensor_scalar(c_g[:, j, :, 0:NCMP], c_u[:, j, :].rearrange("p (a b) -> p a b", a=NSA_KV), 0.5, None, ALU.mult))
            for hk in range(NSA_KV):
                V(v.tensor_copy(c_gx[:, hk * NSA_G:(hk + 1) * NSA_G, :], over(c_g[:, 1, hk:hk + 1, :], [P, NSA_G, CPAD])))
            v.sem_inc(c_act, 1)
            v.wait_ge(c_proj, 1)
            V(v.tensor_copy(c_k, ps[:, 4, 0:NSA_KV * CPAD].rearrange("p (a b) -> p a b", a=NSA_KV)))
            for h in range(NSA_H):
                V(v.tensor_scalar(c_v[:, h, :], ps[:, 5, 0:HD], C("cmp_head")[:, h:h + 1], None, ALU.mult))
            v.sem_inc(c_keys, 1)
            v.wait_ge(c_scored, 1)
            mask = C("cmp_mask").rearrange("p (t c) -> p t c", t=NT)
            for t in range(NT):
                V(v.scalar_tensor_tensor(out=c_s[:, t, :, :],
                                         in0=ps[:, 6, t * P:(t + 1) * P].rearrange("p (h c) -> p h c", h=NSA_H),
                                         scalar=NSA_SCALE, in1=over(mask[:, t:t + 1, :], [P, NSA_H, CPAD]),
                                         op0=ALU.mult, op1=ALU.add))
                V(v.tensor_reduce(c_max[:, t, :], c_s[:, t, :, :], AX, ALU.max))
                V(v.tensor_tensor(c_s[:, t, :, :], c_s[:, t, :, :], over(c_max[:, t, :].unsqueeze(2), [P, NSA_H, CPAD]),
                                  ALU.subtract))
            v.sem_inc(c_centred, 1)
            v.wait_ge(c_exped, 1)
            for t in range(NT):
                V(v.tensor_reduce(c_sum[:, t, :], c_p[:, t, :, :], AX, ALU.add))
            V(v.reciprocal(c_sum, c_sum))
            v.wait_ge(n_gates, 1)
            for t in range(NT):
                V(v.scalar_tensor_tensor(out=c_sum[:, t, :], in0=c_sum[:, t, :], scalar=C("cmp_any")[:, t:t + 1],
                                         in1=n_g[:, t, :].rearrange("p (h j) -> p h j", j=3)[:, :, 0],
                                         op0=ALU.mult, op1=ALU.mult))
                V(v.tensor_tensor(c_p[:, t, :, :], c_p[:, t, :, :], over(c_sum[:, t, :].unsqueeze(2), [P, NSA_H, CPAD]), ALU.mult))
            v.sem_inc(c_probs, 1)
            turn_cp.vector()
            v.wait_ge(c_mixed, 1)
            for t in range(NT):
                for n in range(2):
                    V(v.tensor_copy(n_qkv[:, t, n * W:(n + 1) * W], ps[:, 4 + 2 * t + n, :]))
            v.sem_inc(c_out, 1)
            attend2.vector(prod_gates.split_fill(v))
            turn_no.vector()

        HB = 4
        small_eps = sb("dn_eps", [P, 1])
        NM = HB * NT
        base = 2128

        def mats(n):
            return view(scr, n * NM * P, NM, P) if n < 8 else view(proj, base + (n - 8) * NM * P, NM, P)

        (d_u0, d_ct, d_er, d_dt, d_at, d_lt, d_x, d_xt, d_kg, d_kd, d_vb) = (mats(n) for n in range(11))
        d_vn, d_os = d_u0, d_ct
        d_s = view(proj, 5200, HB, HD)
        d_uu, d_w = d_dt, d_lt
        d_st = view(scr, 8464, 8, NT, DN_H)
        d_beta, d_dec, d_gc, d_egc, d_eleft, d_t0, d_t1, d_bg = (d_st[:, n] for n in range(8))
        d_eps = small_eps[:, :]
        d_nst = stat[:, 16:16 + NM]
        pad_ready = sem("dn_pad_ready")
        conv_done, conv_act = sem("dn_convolved"), sem("dn_conv_activated")
        l2_sq, l2_sum, l2_log, l2_inv = (sem("l2_" + n) for n in ("squares", "sums", "logarithms", "inverted"))
        ab_abs, ab_exp, ab_dec, ab_cum, ab_cexp = (sem("dn_" + n) for n in ("abs", "softplus", "decays", "cumulated", "decay_exps"))
        l2_done = sem("dn_normalised")
        (b_rows, b_rowed, b_erow, b_clamped, b_dexp, b_kk, b_lt, b_tok) = (sem("dn_" + n) for n in (
            "row_inputs", "rows", "row_exps", "clamped", "decay_ready", "products", "systems_ready", "tokens"))
        (b_ct, b_t1, b_t1c, b_x, b_xd) = (sem("dn_inv_" + n) for n in ("corner", "corner_times", "corner_times_copied", "update", "updated"))
        (b_uw, b_uwc, b_sc, b_vn, b_sn, b_si, b_in, b_ind) = (sem("dn_" + n) for n in (
            "uw", "uw_copied", "state_read", "values_new", "state_update", "state_ready", "within", "outputs"))
        b_inc, b_nsq, b_ninv, b_nrs, b_fin = (sem("dn_" + n) for n in ("scan_outputs_copied", "norm_squares", "norm_inverse", "norm_ready", "normed"))
        turn_do = []
        for bt in range(DN_H // HB):
            turn_do.append(Halve(lambda t, k: d_os[:, k * NT + t, :], HB,
                                 lambda k, bt=bt: hidden(NSA_H + bt * HB + k)))
        BANK = lambda a: ps[:, a:a + 2, :].rearrange("p a (m n) -> p (a m) n", n=P)
        HALVES = range(2)
        LEVELS = 6
        SCAN = (4, 1)

        def ms(hf):
            return range(hf * NM // 2, (hf + 1) * NM // 2)

        def part_of(a, hf):
            return a[:, hf * NM // 2:(hf + 1) * NM // 2, :]

        def by_head(a, hf):
            return part_of(a, hf).rearrange("p (h t) n -> p h t n", t=NT)

        def scanned(hf, n):
            return ps[:, SCAN[hf] + n, 0:HB // 2 * P].rearrange("p (h n) -> p h n", n=P)

        def dn_tensor(pe):
            for bt in range(DN_H // HB):
                def kq(which, m):
                    return convd[:, which * DN_H + bt * HB + m // NT, (m % NT) * P:(m % NT + 1) * P]
                for hf in HALVES:
                    pe.wait_ge(b_rows, 2 * bt + hf + 1)
                    for m in ms(hf):
                        pe.matmul(BANK(0)[:, m, :], ones, d_u0[:, m, :], start=True, stop=True)
                        last = pe.matmul(BANK(2)[:, m, :], ones, d_ct[:, m, :], start=True, stop=True)
                    last.then_inc(b_rowed, 1)
                if bt == 0:
                    pe.wait_ge(l2_done, 1)
                for hf in HALVES:
                    for m in ms(hf):
                        pe.matmul(BANK(4)[:, m, :], kq(1, m), kq(1, m), start=True, stop=True)
                        last = pe.matmul(BANK(6)[:, m, :], kq(1, m), kq(0, m), start=True, stop=True)
                    last.then_inc(b_kk, 1)
                for hf in HALVES:
                    pe.wait_ge(b_lt, 2 * bt + hf + 1)
                    for m in ms(hf):
                        pe.transpose(BANK(4)[:, m, :], kq(1, m), ident)
                        last = pe.transpose(BANK(6)[:, m, :], kq(2, m), ident)
                    last.then_inc(b_tok, 1)
                for hf in HALVES:
                    pe.wait_ge(b_ct, 2 * bt + hf + 1)
                    for m in ms(hf):
                        last = pe.transpose(BANK(0)[:, m, :], d_ct[:, m, :], ident)
                    last.then_inc(b_t1, 1)
                for lv in range(1, LEVELS):
                    for hf in HALVES:
                        pe.wait_ge(b_xd, 2 * (LEVELS * bt + lv - 1) + hf + 1)
                        for m in ms(hf):
                            last = pe.matmul(BANK(0)[:, m, :], d_ct[:, m, :], d_x[:, m, :], start=True, stop=True)
                        last.then_inc(b_t1, 1)
                    for hf in HALVES:
                        pe.wait_ge(b_t1c, 2 * ((LEVELS - 1) * bt + lv - 1) + hf + 1)
                        for m in ms(hf):
                            if lv < LEVELS - 1:
                                pe.matmul(BANK(4)[:, m, :], d_xt[:, m, :], d_u0[:, m, :], start=True, stop=True)
                            last = pe.matmul(BANK(6)[:, m, :], d_u0[:, m, :], d_xt[:, m, :], start=True, stop=True)
                        last.then_inc(b_x, 1)
                for hf in HALVES:
                    pe.wait_ge(b_xd, 2 * (LEVELS * (bt + 1) - 1) + hf + 1)
                    for m in ms(hf):
                        pe.matmul(BANK(0)[:, m, :], d_xt[:, m, :], d_vb[:, m, :], start=True, stop=True)
                        last = pe.matmul(BANK(2)[:, m, :], d_kg[:, m, :], d_xt[:, m, :], start=True, stop=True)
                    last.then_inc(b_uw, 1)
                pe.wait_ge(b_uwc, 2 * (bt + 1))
                for ch in range(NCH):
                    t, par = ch // 2, ch % 2
                    rows = slice(par * CHUNK, (par + 1) * CHUNK)
                    if ch > 0:
                        for hf in HALVES:
                            pe.wait_ge(b_si, 2 * ((NCH - 1) * bt + ch - 1) + hf + 1)
                            if ch > 1:
                                pe.wait_ge(b_inc, 2 * ((NCH - 1) * bt + ch - 2) + hf + 1)
                            for j in range(HB // 2):
                                hl = hf * HB // 2 + j
                                m = hl * NT + t
                                pe.matmul(ps[:, SCAN[hf], j * P:(j + 1) * P], d_w[:, m, :], d_s[:, hl, :], start=True, stop=True)
                                last = pe.matmul(ps[:, SCAN[hf] + 1, j * P:(j + 1) * P], kq(0, m), d_s[:, hl, :],
                                                 start=True, stop=True)
                            last.then_inc(b_sc, 1)
                    if ch < NCH - 1:
                        for hf in HALVES:
                            pe.wait_ge(b_vn, 2 * (NCH * bt + ch) + hf + 1)
                            for j in range(HB // 2):
                                m = (hf * HB // 2 + j) * NT + t
                                last = pe.matmul(ps[:, SCAN[hf] + 2, j * P:(j + 1) * P], d_kd[rows, m, :], d_vn[rows, m, :],
                                                 start=True, stop=True)
                            last.then_inc(b_sn, 1)
                pe.wait_ge(b_vn, 2 * NCH * (bt + 1))
                for hf in HALVES:
                    for m in ms(hf):
                        last = pe.matmul(BANK(0)[:, m, :], d_at[:, m, :], d_vn[:, m, :], start=True, stop=True)
                    last.then_inc(b_in, 1)
                pe.wait_ge(b_fin, bt + 1)
                turn_do[bt].tensor(pe)
                if bt + 1 < DN_H // HB:
                    turn_do[bt].wait(pe)

        L2_BANK = (4, 5, 6, 7, 1, 3, 4, 5)

        def prepare_sums(pe):
            turn_n.wait(pe)
            for g in range(DN_H):
                pe.wait_ge(l2_sq, g + 1)
                if g >= 6:
                    pe.wait_ge(l2_log, g - 5)
                pe.matmul(ps[:, L2_BANK[g], :], ones, d_rt(g).rearrange("p a n -> p (a n)"), start=True, stop=True).then_inc(l2_sum, 1)

        def prepare_cumulated(pe):
            pe.wait_ge(ab_dec, 1)
            for t in range(NT):
                pe.matmul(ps[:, 7, t * 8:t * 8 + 8], upto, d_dec[:, t, :], start=True, stop=True)
                last = pe.matmul(ps[:, 7, 16 + t * 8:24 + t * 8], after, d_dec[:, t, :], start=True, stop=True)
            last.then_inc(ab_cum, 1)

        def prepare_squares():
            act = nc.scalar
            for g in range(DN_H):
                Sc(act.activation(d_rt(g), convd[:, 2 * g:2 * g + 2, :], ACT.Square))
                act.sem_inc(l2_sq, 1)

        def prepare_roots():
            act = nc.scalar
            act.wait_ge(ab_abs, 1)
            for g in range(DN_H):
                act.wait_ge(l2_sum, g + 1)
                Sc(act.activation(d_rt(g).rearrange("p a n -> p (a n)"), ps[:, L2_BANK[g], :], ACT.Ln, bias=d_eps))
                act.sem_inc(l2_log, 1)
            Sc(act.activation(d_t0, d_t0, ACT.Exp, scale=-1.0))
            Sc(act.activation(small_alog[:, :], small["alog"][:, :], ACT.Exp))
            for g in range(DN_H):
                Sc(act.activation(d_rt(g), d_rt(g), ACT.Exp, scale=-0.5))
                act.sem_inc(l2_inv, 1)
            Sc(act.activation(d_t0, d_t0, ACT.Ln, bias=1.0))
            act.sem_inc(ab_exp, 1)

        def prepare_exps():
            act = nc.scalar
            act.wait_ge(ab_cum, 1)
            Sc(act.copy(d_gc, ps[:, 7, 0:16].rearrange("p (t h) -> p t h", t=NT)))
            Sc(act.activation(d_egc, ps[:, 7, 0:16].rearrange("p (t h) -> p t h", t=NT), ACT.Exp))
            Sc(act.activation(d_eleft, ps[:, 7, 16:32].rearrange("p (t h) -> p t h", t=NT), ACT.Exp))
            act.sem_inc(ab_cexp, 1)

        def prepare_logits():
            v = nc.vector
            V(v.memset(d_eps, EPS))
            for t in range(NT):
                V(v.tensor_tensor(d_t1[:, t, :], d_ab[:, t, 0:DN_H], small["dt_bias"][:, :], ALU.add))
            V(v.scalar_tensor_tensor(out=d_t0, in0=d_t1, scalar=-1.0, in1=d_t1, op0=ALU.mult, op1=ALU.max))
            v.sem_inc(ab_abs, 1)

        def prepare_heads():
            v = nc.vector
            for g in range(DN_H):
                v.wait_ge(l2_inv, g + 1)
                x = convd[:, 2 * g:2 * g + 2, :]
                V(v.scalar_tensor_tensor(out=x, in0=x, scalar=float(HD) ** -0.5 if g < 4 else 1.0, in1=d_rt(g),
                                         op0=ALU.mult, op1=ALU.mult))
            v.sem_inc(l2_done, 1)
            v.wait_ge(ab_exp, 1)
            V(v.scalar_tensor_tensor(out=d_t0, in0=d_t1, scalar=0.0, in1=d_t0, op0=ALU.max, op1=ALU.add))
            for t in range(NT):
                V(v.scalar_tensor_tensor(out=d_dec[:, t, :], in0=d_t0[:, t, :], scalar=-1.0, in1=small_alog[:, :],
                                         op0=ALU.mult, op1=ALU.mult))
            v.sem_inc(ab_dec, 1)

        def dn_scalar():
            act = nc.scalar
            act.wait_ge(pad_ready, 2)
            Sc(act.activation(d_beta, d_ab[:, :, DN_H:], ACT.Sigmoid))
            act.sem_inc(dn_begun, 1)
            Sc(act.activation(z_tok, z_tok, ACT.Silu))
            for bt in range(DN_H // HB):
                for hf in HALVES:
                    act.wait_ge(b_rowed, 2 * bt + hf + 1)
                    Sc(act.activation(part_of(d_er, hf), part_of(BANK(0), hf), ACT.Exp))
                    act.sem_inc(b_erow, 1)
                for hf in HALVES:
                    act.wait_ge(b_clamped, 2 * bt + hf + 1)
                    Sc(act.activation(part_of(d_dt, hf), part_of(d_dt, hf), ACT.Exp))
                    act.sem_inc(b_dexp, 1)
                for lv in range(1, LEVELS):
                    for hf in HALVES:
                        act.wait_ge(b_t1, 2 * (LEVELS * bt + lv) + hf + 1)
                        Sc(act.copy(part_of(d_u0, hf), part_of(BANK(0), hf)))
                        act.sem_inc(b_t1c, 1)
                for hf in HALVES:
                    act.wait_ge(b_uw, 2 * bt + hf + 1)
                    Sc(act.copy(part_of(d_uu, hf), part_of(BANK(0), hf)))
                    Sc(act.copy(part_of(d_w, hf), part_of(BANK(2), hf)))
                    act.sem_inc(b_uwc, 1)
                for ch in range(1, NCH):
                    t, par = ch // 2, ch % 2
                    rows = slice(par * CHUNK, (par + 1) * CHUNK)
                    for hf in HALVES:
                        act.wait_ge(b_sc, 2 * ((NCH - 1) * bt + ch - 1) + hf + 1)
                        Sc(act.copy(by_head(d_os, hf)[rows, :, t, :], scanned(hf, 1)[rows]))
                        act.sem_inc(b_inc, 1)
                for hf in HALVES:
                    act.wait_ge(b_ind, 2 * bt + hf + 1)
                    for m in ms(hf):
                        Sc(act.activation(d_x[:, 0, :], d_os[:, m, :], ACT.Square, accum_out=d_nst[:, m:m + 1]))
                act.sem_inc(b_nsq, 1)
                act.wait_ge(b_ninv, bt + 1)
                Sc(act.activation(d_nst, d_nst, ACT.Sqrt))
                act.sem_inc(b_nrs, 1)
                turn_do[bt].scalar()

        small_alog = sb("dn_decay_rate", [P, DN_H])

        def d_rt(g):
            return view(gate_stage.rearrange("p a t n -> p (a t n)"), g * 512, 2, S) if g < 4 else view(n_buf, (g - 4) * 512, 2, S)

        dn_begun = sem("dn_begun")

        def conv_vector():
            v = nc.vector
            prod_dn.wait_evicted(v)
            cw = small["conv"]
            for f in range(3 * DN_H):
                if f >= 4:
                    v.wait_ge(conv_act, f - 3)
                t = conv_tmp[:, f % 4, :]
                V(v.tensor_scalar(t, raw[:, f, 0:S], cw[:, CONV_K * f:CONV_K * f + 1], None, ALU.mult))
                for j in range(1, CONV_K):
                    V(v.scalar_tensor_tensor(out=t, in0=raw[:, f, j:j + S], scalar=cw[:, CONV_K * f + j:CONV_K * f + j + 1],
                                             in1=t, op0=ALU.mult, op1=ALU.add))
                v.sem_inc(conv_done, 1)
                yield

        def conv_scalar():
            for _ in range(2):
                yield
            for f in range(3 * DN_H):
                nc.scalar.wait_ge(conv_done, f + 1)
                nc.scalar.activation(convd[:, f, :], conv_tmp[:, f % 4, :], ACT.Silu).then_inc(conv_act, 1)
                yield

        def dn_vector():
            v = nc.vector
            v.sem_inc(pad_ready, 1)
            v.wait_ge(dn_begun, 1)
            V(v.tensor_tensor(d_bg, d_beta, d_egc, ALU.mult))
            H2 = HB // 2
            wide4 = [P, H2, NT, P]
            for bt in range(DN_H // HB):
                def col(a, hf):
                    h = bt * HB + hf * H2
                    return over(a[:, :, h:h + H2].rearrange("p t h -> p h t").unsqueeze(3), wide4)
                for hf in HALVES:
                    V(v.tensor_tensor(by_head(d_u0, hf), over(upto.unsqueeze(1).unsqueeze(1), wide4), col(d_dec, hf), ALU.mult))
                    V(v.tensor_tensor(by_head(d_ct, hf), over(ident.unsqueeze(1).unsqueeze(1), wide4), col(d_beta, hf), ALU.mult))
                    v.sem_inc(b_rows, 1)
                for hf in HALVES:
                    v.wait_ge(b_rowed, 2 * bt + hf + 1)
                    v.wait_ge(b_erow, 2 * bt + hf + 1)
                    V(v.tensor_tensor(by_head(d_dt, hf), by_head(BANK(0), hf), col(d_gc, hf), ALU.subtract))
                    V(v.tensor_scalar(part_of(d_dt, hf), part_of(d_dt, hf), 0.0, None, ALU.min))
                    v.sem_inc(b_clamped, 1)
                for hf in HALVES:
                    v.wait_ge(b_dexp, 2 * bt + hf + 1)
                    at, lt, dt = (part_of(a, hf) for a in (d_at, d_lt, d_dt))
                    V(v.tensor_tensor(dt, dt, over(upto.unsqueeze(1), [P, NM // 2, P]), ALU.mult))
                    v.wait_ge(b_kk, 2 * bt + hf + 1)
                    V(v.tensor_tensor(at, part_of(BANK(6), hf), dt, ALU.mult))
                    V(v.tensor_tensor(lt, part_of(BANK(4), hf), dt, ALU.mult))
                    V(v.tensor_tensor(lt, lt, part_of(BANK(2), hf), ALU.mult))
                    v.sem_inc(b_lt, 1)
                def corner(lv, hf):
                    V(v.tensor_tensor(part_of(d_ct, hf), part_of(d_lt, hf),
                                      over(C("levels")[:, lv * P:(lv + 1) * P].unsqueeze(1), [P, NM // 2, P]), ALU.mult))
                for hf in HALVES:
                    v.wait_ge(b_tok, 2 * bt + hf + 1)
                    V(v.tensor_tensor(by_head(d_kg, hf), by_head(BANK(4), hf), col(d_bg, hf), ALU.mult))
                    V(v.tensor_tensor(by_head(d_kd, hf), by_head(BANK(4), hf), col(d_eleft, hf), ALU.mult))
                    V(v.tensor_tensor(by_head(d_vb, hf), by_head(BANK(6), hf), col(d_beta, hf), ALU.mult))
                    corner(0, hf)
                    v.sem_inc(b_ct, 1)
                for hf in HALVES:
                    for j in range(H2):
                        hl = hf * H2 + j
                        q = convd[:, bt * HB + hl, :].rearrange("p (t n) -> p t n", t=NT)
                        V(v.tensor_tensor(q, q, d_er[:, hl * NT:(hl + 1) * NT, :], ALU.mult))
                for hf in HALVES:
                    v.wait_ge(b_t1, 2 * LEVELS * bt + hf + 1)
                    eye = over(ident.unsqueeze(1), [P, NM // 2, P])
                    V(v.tensor_tensor(part_of(d_x, hf), eye, part_of(BANK(0), hf), ALU.subtract))
                    V(v.tensor_tensor(part_of(d_xt, hf), eye, part_of(d_ct, hf), ALU.subtract))
                    corner(1, hf)
                    v.sem_inc(b_xd, 1)
                for lv in range(1, LEVELS):
                    if lv + 1 < LEVELS:
                        for hf in HALVES:
                            v.wait_ge(b_t1, 2 * (LEVELS * bt + lv) + hf + 1)
                            corner(lv + 1, hf)
                    for hf in HALVES:
                        v.wait_ge(b_x, 2 * ((LEVELS - 1) * bt + lv - 1) + hf + 1)
                        if lv < LEVELS - 1:
                            V(v.tensor_tensor(part_of(d_x, hf), part_of(d_x, hf), part_of(BANK(4), hf), ALU.subtract))
                        V(v.tensor_tensor(part_of(d_xt, hf), part_of(d_xt, hf), part_of(BANK(6), hf), ALU.subtract))
                        v.sem_inc(b_xd, 1)
                v.wait_ge(b_uwc, 2 * (bt + 1))
                for ch in range(NCH):
                    t, par = ch // 2, ch % 2
                    rows = slice(par * CHUNK, (par + 1) * CHUNK)
                    for hf in HALVES:
                        vn, uu, os_, er = (by_head(a, hf) for a in (d_vn, d_uu, d_os, d_er))
                        st = d_s[:, hf * H2:(hf + 1) * H2, :]
                        if ch == 0:
                            V(v.tensor_copy(vn[rows, :, t, :], uu[rows, :, t, :]))
                            V(v.memset(os_[rows, :, t, :], 0.0))
                        else:
                            v.wait_ge(b_sc, 2 * ((NCH - 1) * bt + ch - 1) + hf + 1)
                            V(v.tensor_tensor(vn[rows, :, t, :], uu[rows, :, t, :], scanned(hf, 0)[rows], ALU.subtract))
                        v.sem_inc(b_vn, 1)
                        if 0 < ch < NCH - 1:
                            last = par * CHUNK + CHUNK - 1
                            V(v.tensor_tensor(st, st, over(er[:, :, t, last:last + 1], [P, H2, HD]), ALU.mult))
                    if ch < NCH - 1:
                        for hf in HALVES:
                            st = d_s[:, hf * H2:(hf + 1) * H2, :]
                            v.wait_ge(b_sn, 2 * ((NCH - 1) * bt + ch) + hf + 1)
                            if ch == 0:
                                V(v.tensor_copy(st, scanned(hf, 2)))
                            else:
                                V(v.tensor_tensor(st, st, scanned(hf, 2), ALU.add))
                            v.sem_inc(b_si, 1)
                v.wait_ge(b_inc, 2 * (NCH - 1) * (bt + 1))
                for hf in HALVES:
                    v.wait_ge(b_in, 2 * bt + hf + 1)
                    V(v.tensor_tensor(part_of(d_os, hf), part_of(d_os, hf), part_of(BANK(0), hf), ALU.add))
                    v.sem_inc(b_ind, 1)
                v.wait_ge(b_nsq, bt + 1)
                V(v.tensor_scalar(d_nst, d_nst, 1.0 / HD, EPS, ALU.mult, ALU.add))
                V(v.reciprocal(d_nst, d_nst))
                v.sem_inc(b_ninv, 1)
                v.wait_ge(b_nrs, bt + 1)
                z4 = z_tok[:, :, bt * HB * HD:(bt + 1) * HB * HD].rearrange("p t (h d) -> p h t d", h=HB)
                V(v.tensor_tensor(d_os, d_os, over(d_nst.unsqueeze(2), [P, NM, HD]), ALU.mult))
                V(v.tensor_tensor(d_os, d_os, over(small["dn_norm"][:, :].unsqueeze(1), [P, NM, HD]), ALU.mult))
                V(v.tensor_tensor(d_os.rearrange("p (h t) d -> p h t d", t=NT), d_os.rearrange("p (h t) d -> p h t d", t=NT),
                                  z4, ALU.mult))
                v.sem_inc(b_fin, 1)
                turn_do[bt].vector()
                turn_do[bt].wait(v)

        mixed = view(proj, 0, NT, D)
        part = view(proj, 4096, 2, NT, W)
        prod_up = Product([(A["w_up"][0], 8, 0, W, W, hidden, False),
                           (A["w_up"][1], 8, 0, W, W, lambda k: hidden(NSA_H + k), False)], D // W)
        sig_landed = [sem("gates_landed_even"), sem("gates_landed_odd")]
        stored = [sem("gates_stored_even"), sem("gates_stored_odd")]
        gates_bounded, sum_done = sem("merge_gates_bounded"), sem("merge_sums")
        merged = sem("merged")
        turn_mix = Halve(lambda t, k: mixed[:, t, k * P:(k + 1) * P], KD, hidden)
        prod_o = wide(A["w_o"], KD, 4, 0, hidden)

        def stage_gates(i, n, b):
            if n >= 2:
                nc.scalar.wait_ge(stored[n % 2], 16 * (n // 2))
            for t in range(NT):
                last = nc.scalar.copy(gate_stage[:, n % 2, t, :], ps[:, b + t, :])
            return last

        def gates_of(r):
            return [view(extra, 2048 * (r % 2) + 1024 * j, NT, W) for j in range(2)]

        def merge_scalar(after):
            act = nc.scalar
            pr = prod_up
            for i in range(pr.rounds):
                for n in range(2):
                    for k in range(PARTS, 8):
                        pr.split(act, i, n, k)
                    if n == 0:
                        act.wait_ge(sig_landed[i % 2], 32 * (i // 2 + 1))
                    act.activation(gates_of(i)[n], gates_of(i)[n], ACT.Sigmoid).then_inc(gates_bounded, 1)
                    if n == 0:
                        for k in range(PARTS):
                            pr.split(act, i, 1, k)
                    elif i + 1 < pr.rounds:
                        for k in range(PARTS):
                            pr.split(act, i + 1, 0, k)
                    else:
                        after.prime(act)

        def merge_vector(after):
            v = nc.vector

            def body(i, n, b):
                for t in range(NT):
                    last = v.tensor_tensor(part[:, n, t, :], ps[:, b + t, :], gates_of(i)[n][:, t, :], ALU.mult)
                return last
            pr = prod_up
            for i in range(pr.rounds):
                for n in range(2):
                    for k in range(PARTS, 8):
                        pr.split(v, i, n, k)
                    if n == 0:
                        for k in range(PARTS):
                            pr.split(v, i, 1, k)
                    elif i + 1 < pr.rounds:
                        for k in range(PARTS):
                            pr.split(v, i + 1, 0, k)
                    else:
                        after.prime(v)
                    pr.wait_done(v, i, n)
                    v.wait_ge(gates_bounded, 2 * i + n + 1)
                    c = pr.chunk0 + n
                    body(i, n, 2 * (c % 2)).then_inc(chunk_evicted[c % 2], 1)
                end = pr.chunk0 + 2 * (i + 1)
                v.wait_ge(chunk_evicted[0], (end + 1) // 2)
                v.wait_ge(chunk_evicted[1], end // 2)
                for t in range(NT):
                    last = v.tensor_tensor(mixed[:, t, i * W:(i + 1) * W], part[:, 0, t, :], part[:, 1, t, :], ALU.add)
                last.then_inc(sum_done, 1)
            v.wait_ge(sum_done, pr.rounds)
            v.sem_inc(merged, 1)

        gateT = view(extra, 0, 4, S)
        ffn_act = view(extra, 1024, 4, S)
        prod_ffn = Product([(A["w_gate"], KD, 0, W, W, hidden, True),
                            (A["w_ffn_up"], KD, 0, W, W, hidden, True)], D_FF // W)
        ffn_high, ffn_prod = sem("ffn_high_ready"), sem("ffn_low_ready")
        prod_down = Product([(A["w_down"], NF, n * W, 0, W, lambda k: (act_high[:, k, :], act_low[:, k, :]), False)
                             for n in range(4)])

        def two(b, t):
            return ps[:, b + t, :].rearrange("p (f n) -> p f n", n=S)

        def ffn_scalar(after):
            def body(i, n, b):
                if not (isinstance(i, int) and i == 0):
                    nc.scalar.wait_ge(ffn_prod, i)
                for t in range(2):
                    last = nc.scalar.activation(gateT[:, 2 * t:2 * t + 2, :], two(b, t), ACT.Silu)
                return last
            prod_ffn.run(nc.scalar, [0], body, after)

        def ffn_vector(after):
            v = nc.vector
            c0 = prod_ffn.chunk0

            def body(i, n, b):
                v.wait_ge(chunk_evicted[c0 % 2], i + c0 // 2 + 1)
                for t in range(2):
                    last = v.tensor_tensor(ffn_act[:, 2 * t:2 * t + 2, :], two(b, t), gateT[:, 2 * t:2 * t + 2, :], ALU.mult)
                last.then_inc(chunk_evicted[(c0 + 1) % 2], 1)
                v.wait_ge(chunk_evicted[(c0 + 1) % 2], i + (c0 + 1) // 2 + 1)
                v.tensor_copy(act_high[:, piece(i, 4, 0, 4), :], ffn_act).then_inc(ffn_high, 1)
                v.wait_ge(ffn_high, i + 1)
                v.tensor_tensor(act_low[:, piece(i, 4, 0, 4), :], ffn_act, act_high[:, piece(i, 4, 0, 4), :].bitcast(F32),
                                ALU.subtract).then_inc(ffn_prod, 1)
                return None
            prod_ffn.run(v, [1], body, after)

        def add_residual(prod, after=None):
            per = len(prod.chunks)

            def body(i, n, b):
                for t in range(NT):
                    x = X[:, t, piece(i, per * W, n * W, W)]
                    last = nc.vector.tensor_tensor(x, ps[:, b + t, :], x, ALU.add)
                return last
            prod.run(nc.vector, range(per), body, after)
            prod.wait_evicted(nc.vector)

        res_ready = [sem("residual_ready_0"), sem("residual_ready_1")]

        def square_product(prod, n, after):
            per = len(prod.chunks)

            def body(i, m, b):
                for t in range(NT):
                    square_chunk(t, i * per + m, ps[:, b + t, :])
                    nc.scalar.sem_inc(chunk_squared, 1)
            prod.run(nc.scalar, range(per), body, after)

        def post_vector(prod, post, n, after):
            v = nc.vector
            per = len(prod.chunks)

            def body(i, m, b):
                if i == 0 and m == 0:
                    v.wait_ge(s_row[n], 16)
                for t in range(NT):
                    v.wait_ge(chunk_squared, NT * (n * per * prod.rounds + i * per + m) + t + 1)
                    c = slice((i * per + m) * W, (i * per + m + 1) * W)
                    last = v.tensor_tensor(y_tok[:, t, c], ps[:, b + t, :], gain_row[:, c], ALU.mult)
                return last
            prod.run(v, range(per), body, after)
            prod.wait_evicted(v)
            post.vector()
            for t in range(NT):
                V(v.scalar_tensor_tensor(out=X[:, t, :], in0=y_tok[:, t, :], scalar=stat_x[:, t:t + 1], in1=X[:, t, :],
                                         op0=ALU.mult, op1=ALU.add))
                v.sem_inc(res_ready[n], 1)

        def square_residual(prod, after=None):
            per = len(prod.chunks)

            def body(i, m, b):
                j = i * per + m
                c = prod.chunk0 + j
                nc.scalar.wait_ge(chunk_evicted[c % 2], c // 2 + 1)
                for t in range(NT):
                    square_chunk(t, j, X[:, t, j * W:(j + 1) * W])
            prod.run(nc.scalar, range(per), body, after)

        for stage in (norm0, turn0, turn_low, turn_qk, turn_go, post0, norm1, turn1, norm_q, norm_kv, turn_cq, turn_ckv,
                      q_turned, qr_turned, k_turned, turn_mo, post1, norm2, turn2, turn_n, turn_cp, turn_no,
                      turn_do[0], turn_do[1], turn_mix, norm3, turn3, postf):
            stage.place()

        block = ctx.enter_context(nc.Block())

        @block.sync
        def _(sp):
            sp.dma_start(X[:, 0, :], A["x"][0:P, :]).then_inc(s_x[0], 16)
            for t in range(NT):
                sp.wait_ge(s_x[t], 16)
            for p in (prod_gla_low, prod_gla, prod_gla_out, prod_mla, prod_mla_tail, prod_q, prod_kv, prod_mla_out,
                      prod_dn, prod_n, prod_ng, prod_z, prod_ab, prod_cmp, prod_gates, prod_up, prod_o, prod_ffn,
                      prod_down):
                p.load(sp)
            for t in range(NT):
                sp.wait_ge(out_ready, t + 1)
                sp.dma_start(A["out"][t * P:(t + 1) * P, :], y_tok[:, t, :]).then_inc(out_landed, 16)
            sp.wait_ge(out_landed, 16 * NT)

        @block.gpsimd
        def _(pool):
            pool.dma_start(const[:, :], A["const"]).then_inc(s_first, 16)
            pool.dma_start(small["l0_pre"][:, :], A["small"]["l0_pre"]).then_inc(s_first, 16)
            pool.dma_start(pos_i[:, :], A["positions"]).then_inc(s_pos, 16)
            pool.dma_start(gk2, A["gk2"]).then_inc(s_const, 16)
            pool.dma_start(w2k[:, :], A["w2k"]).then_inc(s_const, 16)
            pool.dma_start(w2v[:, :], A["w2v"]).then_inc(s_const, 16)
            for name, buf in small.items():
                if name == "l0_pre":
                    continue
                src = A["small"][name]
                pool.dma_start(buf[:, :], src).then_inc(s_const, 16)
            for m in range(2 * D // W):
                c = prod_gates.chunk0 + m
                pool.wait_ge(chunk_evicted[c % 2], c // 2 + 1)
                pool.dma_start(gates_dram[:, m, :], gate_stage[:, m % 2, :, :].rearrange("p t n -> p (t n)"))\
                    .then_inc(stored[m % 2], 16)
            for n in range(2):
                pool.wait_ge(stored[n], 16 * (D // W))
            pool.wait_ge(attend2.finished, 2 * NSA_H)
            for r in range(D // W):
                if r >= 2:
                    pool.wait_ge(sum_done, r - 1)
                for j in range(2):
                    pool.dma_start(gates_of(r)[j].rearrange("p t n -> p (t n)"), gates_dram[:, r + j * (D // W), :])\
                        .then_inc(sig_landed[r % 2], 16)

        @block.scalar
        def _(act):
            act.dma_start(X[:, 1, :], A["x"][P:, :]).then_inc(s_x[1], 16)
            norm0.scalar(lambda t: (s_x[t], 16))
            prod_gla_low.prime(act)
            act.wait_ge(s_first, 32)
            turn0.scalar()
            evict_tail(prod_gla_low, g_proj, G_LOW, GLA_RANK, prod_gla)
            evict_wide(prod_gla, g_proj, 0, prod_gla_out, gla_gates_scalar())
            act.wait_ge(s_const, 16 * n_const)
            gla_scalar()
            act.dma_start(gain_row, A["l0_post"].to_broadcast([P, D])).then_inc(s_row[0], 16)
            square_product(prod_gla_out, 0, prod_mla)
            post0.scalar()
            norm1.scalar(lambda t: (res_ready[0], t + 1))
            turn1.scalar()
            mla_tables_scalar()
            evict_wide(prod_mla, m_proj, 0, prod_mla_tail)
            evict_tail(prod_mla_tail, m_proj, 3072, 64, prod_q)
            prod_mla_tail.wait_evicted(act)
            norm_q.scalar()
            norm_kv.scalar()
            turn_cq.scalar()
            turn_ckv.scalar()
            evict_wide(prod_q, m_q, 0, prod_kv)
            q_turned.scalar()
            for t in range(NT):
                Sc(act.activation(m_proj[:, t, M_G:M_G + D], m_proj[:, t, M_G:M_G + D], ACT.Silu))
            act.sem_inc(m_gate, 1)
            evict_wide(prod_kv, m_kv, 0, prod_mla_out)
            qr_turned.scalar()
            k_turned.scalar()
            attend.scalar()
            turn_mo.scalar()
            act.dma_start(gain_row, A["l1_post"].to_broadcast([P, D])).then_inc(s_row[1], 16)
            square_product(prod_mla_out, 1, prod_dn)
            post1.scalar()
            norm2.scalar(lambda t: (res_ready[1], t + 1))
            turn2.scalar()
            act.wait_ge(pad_ready, 1)

            def to_raw(i, n, b):
                for t in range(2):
                    last = act.copy(raw[:, piece(i, 8, 4 * n + 2 * t, 2), CONV_K - 1:], two(b, t))
                return last
            prod_dn.run(act, range(2), to_raw, prod_n)
            conv = every(3, conv_scalar())
            evict_wide(prod_n, n_qkv, 0, prod_ng, conv)
            evict_tail(prod_ng, n_g, 0, 3 * NSA_H, prod_z, conv)
            evict_wide(prod_z, z_tok, 0, prod_ab, conv)
            evict_tail(prod_ab, d_ab, 0, 2 * DN_H, None, conv)
            for _ in conv:
                pass
            prod_ab.wait_evicted(act)
            nsa_scalar()
            prod_up.prime(act)
            dn_scalar()
            merge_scalar(prod_o)
            turn_mix.scalar()
            square_residual(prod_o, prod_ffn)
            norm3.scalar()
            turn3.scalar()
            ffn_scalar(prod_down)
            act.dma_start(gain_f, A["norm_f"].to_broadcast([P, D])).then_inc(s_row[2], 16)
            square_residual(prod_down)
            postf.scalar()

        @block.vector
        def _(v):
            v.wait_ge(s_x[1], 16)
            norm0.vector()
            prod_gla_low.prime(v)
            v.wait_ge(s_first, 32)
            turn0.vector()
            prod_gla_low.run(v, after=prod_gla)
            prod_gla.run(v, after=prod_gla_out, side=gla_gates_vector())
            v.wait_ge(s_const, 16 * n_const)
            gla_vector()
            post_vector(prod_gla_out, post0, 0, prod_mla)
            norm1.vector()
            turn1.vector()
            mla_tables_vector()
            prod_mla.run(v, after=prod_mla_tail)
            prod_mla_tail.run(v, after=prod_q)
            norm_q.vector()
            norm_kv.vector()
            turn_cq.vector()
            turn_ckv.vector()
            prod_q.run(v, after=prod_kv)
            q_turned.vector()
            rotary = every(5, mla_rotate())
            prod_kv.run(v, after=prod_mla_out, side=rotary)
            for _ in rotary:
                pass
            qr_turned.vector()
            k_turned.vector()
            v.wait_ge(m_gate, 1)
            attend.vector()
            v.sem_inc(m_done, 1)
            turn_mo.vector()
            post_vector(prod_mla_out, post1, 1, prod_dn)
            norm2.vector()
            turn2.vector()
            V(v.memset(raw[:, :, 0:CONV_K - 1], 0.0))
            v.sem_inc(pad_ready, 1)
            prod_dn.run(v, after=prod_n)
            conv, rotary = every(3, conv_vector()), every(7, nsa_rotate())
            prod_n.run(v, after=prod_ng, side=conv)
            for _ in conv:
                pass
            prod_ng.run(v, after=prod_z, side=rotary)
            prod_z.run(v, after=prod_ab, side=rotary)
            prod_ab.run(v, side=rotary)
            for _ in rotary:
                pass
            nsa_vector()
            prod_up.prime(v)
            dn_vector()
            merge_vector(prod_o)
            turn_mix.vector()
            add_residual(prod_o, prod_ffn)
            norm3.vector()
            turn3.vector()
            ffn_vector(prod_down)
            add_residual(prod_down)
            postf.vector()
            v.wait_ge(s_row[2], 16)
            for t in range(NT):
                V(v.scalar_tensor_tensor(out=y_tok[:, t, :], in0=X[:, t, :], scalar=stat_x[:, t:t + 1], in1=gain_f,
                                         op0=ALU.mult, op1=ALU.mult))
                v.sem_inc(out_ready, 1)

        @block.tensor
        def _(pe):
            pe.wait_ge(s_first, 32)
            norm0.wait(pe)
            turn0.tensor_into(pe, prod_gla_low)
            prod_gla.tensor(pe, lambda n, k: gla_gates_tensor(pe, n, k))
            gla_tensor(pe)
            pe.wait_ge(gn_out, 1)
            turn_go.tensor_into(pe, prod_gla_out)
            norm1.wait(pe)
            turn1.tensor_into(pe, prod_mla)
            prod_mla_tail.tensor(pe)
            norm_kv.wait(pe)
            turn_cq.tensor(pe)
            turn_cq.wait(pe)
            turn_ckv.tensor(pe)
            prod_q.tensor(pe)
            prod_q.wait_evicted(pe)
            turn_ckv.wait(pe)
            q_turned.tensor(pe)
            q_turned.wait(pe)
            prod_kv.tensor(pe)
            pe.wait_ge(rotated, 1)
            qr_turned.tensor(pe)
            qr_turned.wait(pe)
            prod_kv.wait_evicted(pe)
            k_turned.tensor(pe)
            k_turned.wait(pe)
            attend.tensor(pe)
            pe.wait_ge(m_done, 1)
            turn_mo.tensor_into(pe, prod_mla_out)
            norm2.wait(pe)
            turn2.tensor_into(pe, prod_dn)
            for p in (prod_n, prod_ng, prod_z, prod_ab):
                p.tensor(pe)
            nsa_tensor(pe)
            turn_no.wait(pe)
            dn_tensor(pe)
            prod_up.tensor(pe, lambda n, k: turn_do[-1].wait(pe) if n == 1 and k == 0 else None)
            pe.wait_ge(merged, 1)
            turn_mix.tensor_into(pe, prod_o)
            norm3.wait(pe)
            turn3.tensor_into(pe, prod_ffn)
            prod_down.tensor(pe, lambda n, k: pe.wait_ge(ffn_prod, k // 4 + 1) if n == 0 else None)


def kernel(**inputs):
    import concourse.bacc as bacc
    from concourse.bass_utils import run_bass_kernel_spmd

    a = {k: np.asarray(v) for k, v in inputs.items()}

    def tiles(v):
        return np.ascontiguousarray(v.reshape(-1, P).T)

    def rows(v):
        return np.ascontiguousarray(np.broadcast_to(v.reshape(1, -1), (P, v.size)))

    conv = a["conv_w_2"][0, :, 0, :]
    small = {
        "l0_pre": tiles(a["l0_pre_norm"]), "l1_pre": tiles(a["l1_pre_norm"]),
        "norm1": tiles(a["norm1_w_2"][0]), "norm2": tiles(a["norm2_w_2"][0]),
        "qa": tiles(a["l1_mla_g_qa"]), "kva": tiles(a["l1_mla_g_kva"]),
        "gla_bias": rows(a["l0_gla_b_gk"]), "gla_onorm": rows(a["l0_gla_g_onorm"]),
        "dn_norm": rows(a["dn_norm_w_2"][0]), "alog": rows(a["a_log_2"][0]), "dt_bias": rows(a["dt_bias_2"][0]),
        "conv": np.ascontiguousarray(conv.reshape(CONV_K, -1, P).transpose(2, 1, 0).reshape(P, -1)),
        "cmp_pe": np.ascontiguousarray(np.concatenate([a["cmp_pe_k_2"][0].T, a["cmp_pe_v_2"][0].T], 1)),
    }
    consts = np.concatenate(list(constant_columns().values()), 1)
    arrays = {
        "x": a["x"][0], "positions": np.ascontiguousarray(a["positions"][0].reshape(NT, P).T),
        "const": consts, "gk2": a["l0_gla_w_gk2"], "w2k": a["cmp_w2_k_2"][0], "w2v": a["cmp_w2_v_2"][0],
        "l0_post": a["l0_post_norm"].reshape(1, D), "l1_post": a["l1_post_norm"].reshape(1, D),
        "norm_f": a["norm_f_w_2"].reshape(1, D),
        "w_gla_in": a["l0_gla_w_in"], "w_gla_out": a["l0_gla_w_out"], "w_mla_in": a["l1_mla_w_in"],
        "w_qb": a["l1_mla_w_qb"], "w_kvb": a["l1_mla_w_kvb"], "w_mla_out": a["l1_mla_w_out"],
        "w_in2": a["w_in_2"][0], "cmp_w1_k": a["cmp_w1_k_2"][0], "cmp_w1_v": a["cmp_w1_v_2"][0],
        "w_up_nsa": a["w_up_nsa_2"][0], "w_up_dn": a["w_up_dn_2"][0], "w_o": a["w_o_2"][0],
        "w_gate": a["w_ffn_gate_2"][0], "w_ffn_up": a["w_ffn_up_2"][0], "w_down": a["w_ffn_down_2"][0],
    }
    arrays.update({"small_" + k: v for k, v in small.items()})
    nc = bacc.Bacc("TRN2", target_bir_lowering=False, num_devices=1)
    feed, A = {}, {"small": {}}
    for name, v in arrays.items():
        v = np.ascontiguousarray(v)
        feed["in_" + name] = v
        ap = nc.dram_tensor("in_" + name, v.shape, mybir.dt.from_np(v.dtype), kind="ExternalInput").ap()
        if name.startswith("small_"):
            A["small"][name[6:]] = ap
        else:
            A[name] = ap
    A["cmp_w1"] = [A["cmp_w1_k"], A["cmp_w1_v"]]
    A["w_up"] = [A["w_up_nsa"], A["w_up_dn"]]
    A["out"] = nc.dram_tensor("out_y", (S, D), F32, kind="ExternalOutput").ap()
    program(nc, A)
    r = run_bass_kernel_spmd(nc, [feed], core_ids=[0])
    return r.results[0]["out_y"].reshape(1, S, D)
```
